# Optimizing a Trainium2 kernel written in Bass

```python
import math
import jax
import jax.numpy as jnp
from jax import lax
import numpy as np

D_MODEL = 1024
BATCH = 1
SEQ = 512
DEPTH = 2

D_FF = 2816
MLA_HEADS = 4
MLA_NOPE_DIM = 64
MLA_ROPE_DIM = 32
MLA_V_DIM = 64
MLA_Q_LORA = 256
MLA_KV_LORA = 128
DIFF_HEADS = 4
DIFF_QK_DIM = 32
DIFF_V_DIM = 64
NSA_HEADS = 8
NSA_GROUPS = 2
NSA_DK = 64
NSA_DV = 64
CMP_BLOCK = 32
CMP_STRIDE = 16
CMP_HIDDEN = 256
SEL_BLOCK = 64
SEL_TOPK = 16
WINDOW = 512
NSA_Q_BLOCK = 64
ATTN_Q_BLOCK = 128
ROPE_THETA = 10000.0
EPS = 1e-6
NEG = -1e30
FORCE = 1e4

D_MIX = MLA_HEADS * MLA_V_DIM + DIFF_HEADS * DIFF_V_DIM + NSA_HEADS * NSA_DV
IN_SPLITS = (
    MLA_Q_LORA,
    MLA_KV_LORA,
    MLA_ROPE_DIM,
    DIFF_HEADS * 2 * DIFF_QK_DIM,
    DIFF_HEADS * 2 * DIFF_QK_DIM,
    DIFF_HEADS * DIFF_V_DIM,
    NSA_HEADS * NSA_DK,
    3 * 2 * NSA_GROUPS * NSA_DK,
    NSA_HEADS * 3,
)
N_IN = sum(IN_SPLITS)


def rms_norm(x, g):
    xf = x.astype(jnp.float32)
    y = xf * lax.rsqrt(jnp.mean(xf * xf, axis=-1, keepdims=True) + EPS)
    return (y * g.astype(jnp.float32)).astype(x.dtype)

def rope_tables(seq, dim):
    inv = ROPE_THETA ** (-jnp.arange(0, dim, 2, dtype=jnp.float32) / dim)
    ang = jnp.arange(seq, dtype=jnp.float32)[:, None] * inv[None, :]
    return jnp.cos(ang), jnp.sin(ang)

def apply_rope(x, cos, sin):
    half = x.shape[-1] // 2
    x1, x2 = x[..., :half], x[..., half:]
    c = cos[None, :, None, :].astype(x.dtype)
    s = sin[None, :, None, :].astype(x.dtype)
    return jnp.concatenate([x1 * c - x2 * s, x2 * c + x1 * s], axis=-1)

def swiglu(h, wg, wu, wd):
    return (jax.nn.silu(h @ wg) * (h @ wu)) @ wd

def to_blocks(a, nb, qb):
    return a.reshape((a.shape[0], nb, qb) + a.shape[2:]).swapaxes(0, 1)

def from_blocks(a):
    nb, b, qb = a.shape[:3]
    return a.swapaxes(0, 1).reshape((b, nb * qb) + a.shape[3:])

def mla_attention(q_nope, q_rope, k_nope, k_rope, v):
    t = q_nope.shape[1]
    nb = t // ATTN_Q_BLOCK
    kpos = jnp.arange(t)
    scale = (MLA_NOPE_DIM + MLA_ROPE_DIM) ** -0.5

    def block(args):
        qn, qr, bi = args
        qpos = bi * ATTN_Q_BLOCK + jnp.arange(ATTN_Q_BLOCK)
        s = (jnp.einsum('bqhd,bkhd->bhqk', qn, k_nope)
             + jnp.einsum('bqhr,bkr->bhqk', qr, k_rope)).astype(jnp.float32) * scale
        s = jnp.where(kpos[None, :] <= qpos[:, None], s, NEG)
        p = jax.nn.softmax(s, axis=-1).astype(v.dtype)
        return jnp.einsum('bhqk,bkhd->bqhd', p, v)

    out = lax.map(block, (to_blocks(q_nope, nb, ATTN_Q_BLOCK),
                          to_blocks(q_rope, nb, ATTN_Q_BLOCK), jnp.arange(nb)))
    return from_blocks(out)

def diff_attention(q, k, v, lam):
    t = q.shape[1]
    nb = t // ATTN_Q_BLOCK
    kpos = jnp.arange(t)
    scale = DIFF_QK_DIM ** -0.5

    def block(args):
        qb, bi = args
        qpos = bi * ATTN_Q_BLOCK + jnp.arange(ATTN_Q_BLOCK)
        s = jnp.einsum('bqhmd,bkhmd->bhmqk', qb, k).astype(jnp.float32) * scale
        s = jnp.where(kpos[None, :] <= qpos[:, None], s, NEG)
        p = jax.nn.softmax(s, axis=-1)
        a = p[:, :, 0] - lam * p[:, :, 1]
        return jnp.einsum('bhqk,bkhd->bqhd', a.astype(v.dtype), v)

    out = lax.map(block, (to_blocks(q, nb, ATTN_Q_BLOCK), jnp.arange(nb)))
    return from_blocks(out)

def compress_tokens(tok, pos_emb, w1, b1, w2):
    b, t, g, d = tok.shape
    nc = (t - CMP_BLOCK) // CMP_STRIDE + 1
    idx = np.arange(nc)[:, None] * CMP_STRIDE + np.arange(CMP_BLOCK)[None, :]
    blk = tok[:, idx] + pos_emb[None, None, :, None, :]
    flat = blk.transpose(0, 1, 3, 2, 4).reshape(b, nc, g, CMP_BLOCK * d)
    return jax.nn.silu(flat @ w1 + b1) @ w2

def nsa_attention(q, k_cmp, v_cmp, k_slc, v_slc, k_win, v_win, gates):
    b, t, h, dk = q.shape
    g = NSA_GROUPS
    hg = h // g
    dv = v_slc.shape[-1]
    nc = k_cmp.shape[1]
    nb_sel = t // SEL_BLOCK
    n_sel = min(SEL_TOPK, nb_sel)
    qn = NSA_Q_BLOCK
    nq = t // qn
    scale = dk ** -0.5
    cmp_end = jnp.arange(nc) * CMP_STRIDE + CMP_BLOCK - 1
    r_sel = SEL_BLOCK // CMP_STRIDE
    r_cmp = CMP_BLOCK // CMP_STRIDE
    map_idx = (np.arange(nb_sel)[:, None, None] * r_sel
               - np.arange(r_sel)[None, :, None]
               - np.arange(r_cmp)[None, None, :]).reshape(nb_sel, -1)
    map_valid = (map_idx >= 0) & (map_idx < nc)
    map_idx = np.clip(map_idx, 0, nc - 1)
    k_blk = k_slc.reshape(b, nb_sel, SEL_BLOCK, g, dk).transpose(0, 3, 1, 2, 4)
    v_blk = v_slc.reshape(b, nb_sel, SEL_BLOCK, g, dv).transpose(0, 3, 1, 2, 4)
    k_wp = jnp.pad(k_win, ((0, 0), (WINDOW, 0), (0, 0), (0, 0)))
    v_wp = jnp.pad(v_win, ((0, 0), (WINDOW, 0), (0, 0), (0, 0)))
    bi = jnp.arange(b)[:, None, None, None]
    gi = jnp.arange(g)[None, :, None, None]
    blk_ids = jnp.arange(nb_sel)
    tok_in_blk = jnp.arange(SEL_BLOCK)
    win_off = jnp.arange(qn + WINDOW)

    def chunk(args):
        qc, gc, ci = args
        qg = qc.reshape(b, qn, g, hg, dk)
        tpos = ci * qn + jnp.arange(qn)
        s = jnp.einsum('bqghd,bngd->bghqn', qg, k_cmp).astype(jnp.float32) * scale
        valid = cmp_end[None, :] <= tpos[:, None]
        p_c = jax.nn.softmax(jnp.where(valid, s, NEG), axis=-1) * valid
        o_cmp = jnp.einsum('bghqn,bngd->bqghd', p_c.astype(v_cmp.dtype), v_cmp)
        pg = p_c.sum(axis=2)
        p_slc = jnp.where(map_valid, pg[..., map_idx], 0.0).sum(-1)
        cblk = (tpos // SEL_BLOCK)[:, None]
        forced = (blk_ids == 0) | (blk_ids == cblk) | (blk_ids == cblk - 1)
        score = jnp.where(blk_ids > cblk, -1.0, p_slc + jnp.where(forced, FORCE, 0.0))
        _, sel = lax.top_k(score, n_sel)
        k_sel = k_blk[bi, gi, sel]
        v_sel = v_blk[bi, gi, sel]
        kpos = sel[..., None] * SEL_BLOCK + tok_in_blk
        m_s = (kpos <= tpos[None, None, :, None, None])[:, :, None]
        s = jnp.einsum('bqghd,bgqnkd->bghqnk', qg, k_sel).astype(jnp.float32) * scale
        p_s = jax.nn.softmax(jnp.where(m_s, s, NEG), axis=(-2, -1))
        o_slc = jnp.einsum('bghqnk,bgqnkd->bqghd', p_s.astype(v_sel.dtype), v_sel)
        k_w = lax.dynamic_slice_in_dim(k_wp, ci * qn, qn + WINDOW, axis=1)
        v_w = lax.dynamic_slice_in_dim(v_wp, ci * qn, qn + WINDOW, axis=1)
        kpos_w = ci * qn - WINDOW + win_off
        delta = tpos[:, None] - kpos_w[None, :]
        m_w = (delta >= 0) & (delta < WINDOW) & (kpos_w >= 0)[None, :]
        s = jnp.einsum('bqghd,bkgd->bghqk', qg, k_w).astype(jnp.float32) * scale
        p_w = jax.nn.softmax(jnp.where(m_w, s, NEG), axis=-1)
        o_win = jnp.einsum('bghqk,bkgd->bqghd', p_w.astype(v_w.dtype), v_w)
        gt = gc.reshape(b, qn, g, hg, 3)
        o = gt[..., 0:1] * o_cmp + gt[..., 1:2] * o_slc + gt[..., 2:3] * o_win
        return o.reshape(b, qn, h, dv)

    out = lax.map(chunk, (to_blocks(q, nq, qn), to_blocks(gates, nq, qn), jnp.arange(nq)))
    return from_blocks(out)

def token_mixer(h, w_in, mla_q_norm_g, mla_w_uq, mla_kv_norm_g, mla_w_ukv,
                diff_lambda, diff_norm_g, lam_init,
                cmp_pos, cmp_w1, cmp_b1, cmp_w2, gate_b, w_out,
                cs_mla, cs_diff, cs_nsa):
    b, t, _ = h.shape
    splits = np.cumsum(IN_SPLITS)[:-1].tolist()
    cq, ckv, kr, dq, dkk, dvv, nq, nkv, ng = jnp.split(h @ w_in, splits, axis=-1)

    qm = (rms_norm(cq, mla_q_norm_g) @ mla_w_uq).reshape(b, t, MLA_HEADS, MLA_NOPE_DIM + MLA_ROPE_DIM)
    q_nope = qm[..., :MLA_NOPE_DIM]
    q_rope = apply_rope(qm[..., MLA_NOPE_DIM:], *cs_mla)
    kvm = (rms_norm(ckv, mla_kv_norm_g) @ mla_w_ukv).reshape(b, t, MLA_HEADS, MLA_NOPE_DIM + MLA_V_DIM)
    k_nope = kvm[..., :MLA_NOPE_DIM]
    v_mla = kvm[..., MLA_NOPE_DIM:]
    k_rope = apply_rope(kr[:, :, None, :], *cs_mla)[:, :, 0, :]
    o_mla = mla_attention(q_nope, q_rope, k_nope, k_rope, v_mla)

    qd = apply_rope(dq.reshape(b, t, DIFF_HEADS * 2, DIFF_QK_DIM), *cs_diff).reshape(b, t, DIFF_HEADS, 2, DIFF_QK_DIM)
    kd = apply_rope(dkk.reshape(b, t, DIFF_HEADS * 2, DIFF_QK_DIM), *cs_diff).reshape(b, t, DIFF_HEADS, 2, DIFF_QK_DIM)
    vd = dvv.reshape(b, t, DIFF_HEADS, DIFF_V_DIM)
    lf = diff_lambda.astype(jnp.float32)
    lam = jnp.exp(jnp.sum(lf[0] * lf[1])) - jnp.exp(jnp.sum(lf[2] * lf[3])) + lam_init
    o_diff = rms_norm(diff_attention(qd, kd, vd, lam), diff_norm_g) * (1.0 - lam_init)

    qn_ = apply_rope(nq.reshape(b, t, NSA_HEADS, NSA_DK), *cs_nsa)
    kv = nkv.reshape(b, t, 3, 2, NSA_GROUPS, NSA_DK)
    k_all = apply_rope(kv[:, :, :, 0].reshape(b, t, 3 * NSA_GROUPS, NSA_DK), *cs_nsa).reshape(b, t, 3, NSA_GROUPS, NSA_DK)
    v_all = kv[:, :, :, 1]
    k_cmp = compress_tokens(k_all[:, :, 0], cmp_pos[0], cmp_w1[0], cmp_b1[0], cmp_w2[0])
    v_cmp = compress_tokens(v_all[:, :, 0], cmp_pos[1], cmp_w1[1], cmp_b1[1], cmp_w2[1])
    gates = jax.nn.sigmoid(ng + gate_b).reshape(b, t, NSA_HEADS, 3)
    o_nsa = nsa_attention(qn_, k_cmp, v_cmp, k_all[:, :, 1], v_all[:, :, 1],
                          k_all[:, :, 2], v_all[:, :, 2], gates)

    o = jnp.concatenate([o_mla.reshape(b, t, -1), o_diff.reshape(b, t, -1),
                         o_nsa.reshape(b, t, -1)], axis=-1)
    return o @ w_out

def first_inputs(seed: int = 0) -> dict:
    key = jax.random.key(seed)
    ks = jax.random.split(key, 24)

    def nrm(k, shape, scale):
        return jax.random.normal(k, shape, jnp.float32) * scale

    def gain(k, shape):
        return 1.0 + 0.02 * jax.random.normal(k, shape, jnp.float32)

    return {
        'x': nrm(ks[0], (BATCH, SEQ, D_MODEL), 1.0),
        'ffn_norm_g': gain(ks[1], (DEPTH, 2, D_MODEL)),
        'ffn_w_gate': nrm(ks[2], (DEPTH, 2, D_MODEL, D_FF), D_MODEL ** -0.5),
        'ffn_w_up': nrm(ks[3], (DEPTH, 2, D_MODEL, D_FF), D_MODEL ** -0.5),
        'ffn_w_down': nrm(ks[4], (DEPTH, 2, D_FF, D_MODEL), D_FF ** -0.5),
        'mix_norm_g': gain(ks[5], (DEPTH, D_MODEL)),
        'w_in': nrm(ks[6], (DEPTH, D_MODEL, N_IN), D_MODEL ** -0.5),
        'mla_q_norm_g': gain(ks[7], (DEPTH, MLA_Q_LORA)),
        'mla_w_uq': nrm(ks[8], (DEPTH, MLA_Q_LORA, MLA_HEADS * (MLA_NOPE_DIM + MLA_ROPE_DIM)), MLA_Q_LORA ** -0.5),
        'mla_kv_norm_g': gain(ks[9], (DEPTH, MLA_KV_LORA)),
        'mla_w_ukv': nrm(ks[10], (DEPTH, MLA_KV_LORA, MLA_HEADS * (MLA_NOPE_DIM + MLA_V_DIM)), MLA_KV_LORA ** -0.5),
        'diff_lambda': nrm(ks[11], (DEPTH, 4, DIFF_QK_DIM), 0.1),
        'diff_norm_g': gain(ks[12], (DEPTH, DIFF_V_DIM)),
        'nsa_cmp_pos': nrm(ks[13], (DEPTH, 2, CMP_BLOCK, NSA_DK), 0.02),
        'nsa_cmp_w1': nrm(ks[14], (DEPTH, 2, CMP_BLOCK * NSA_DK, CMP_HIDDEN), (CMP_BLOCK * NSA_DK) ** -0.5),
        'nsa_cmp_b1': nrm(ks[15], (DEPTH, 2, CMP_HIDDEN), 0.01),
        'nsa_cmp_w2': nrm(ks[16], (DEPTH, 2, CMP_HIDDEN, NSA_DK), CMP_HIDDEN ** -0.5),
        'nsa_gate_b': nrm(ks[17], (DEPTH, NSA_HEADS * 3), 0.01),
        'w_out': nrm(ks[18], (DEPTH, D_MIX, D_MODEL), D_MIX ** -0.5),
        'final_norm_g': gain(ks[19], (D_MODEL,)),
    }

def first_block(x, ffn_norm_g, ffn_w_gate, ffn_w_up, ffn_w_down, mix_norm_g, w_in,
              mla_q_norm_g, mla_w_uq, mla_kv_norm_g, mla_w_ukv, diff_lambda, diff_norm_g,
              nsa_cmp_pos, nsa_cmp_w1, nsa_cmp_b1, nsa_cmp_w2, nsa_gate_b, w_out,
              final_norm_g):
    t = x.shape[1]
    cs_mla = rope_tables(t, MLA_ROPE_DIM)
    cs_diff = rope_tables(t, DIFF_QK_DIM)
    cs_nsa = rope_tables(t, NSA_DK)
    for l in range(DEPTH):
        lam_init = 0.8 - 0.6 * math.exp(-0.3 * l)
        x = x + 0.5 * swiglu(rms_norm(x, ffn_norm_g[l, 0]), ffn_w_gate[l, 0],
                             ffn_w_up[l, 0], ffn_w_down[l, 0])
        x = x + token_mixer(rms_norm(x, mix_norm_g[l]), w_in[l],
                            mla_q_norm_g[l], mla_w_uq[l], mla_kv_norm_g[l], mla_w_ukv[l],
                            diff_lambda[l], diff_norm_g[l], lam_init,
                            nsa_cmp_pos[l], nsa_cmp_w1[l], nsa_cmp_b1[l], nsa_cmp_w2[l],
                            nsa_gate_b[l], w_out[l], cs_mla, cs_diff, cs_nsa)
        x = x + 0.5 * swiglu(rms_norm(x, ffn_norm_g[l, 1]), ffn_w_gate[l, 1],
                             ffn_w_up[l, 1], ffn_w_down[l, 1])
    return rms_norm(x, final_norm_g)


DEPTH_2 = 1

GRID_W = 64
CTX_LEN = 256
RET_HEADS = 4
RET_DK = 128
RET_DV = 128
RET_CHUNK = 128
GLA_HEADS = 4
GLA_DK = 64
GLA_DV = 128
GLA_RANK = 16
GLA_TAU = 16.0
GLA_CHUNK = 64
RET_WIDTH = RET_HEADS * RET_DV
GLA_WIDTH = GLA_HEADS * GLA_DV
D_MIX_2 = RET_WIDTH + GLA_WIDTH
N_MOD = 9
ROPE_BASE = 10000.0
IN_WIDTHS = (RET_HEADS * RET_DK, RET_HEADS * RET_DK, RET_WIDTH, RET_WIDTH,
             GLA_HEADS * GLA_DK, GLA_HEADS * GLA_DK, GLA_WIDTH, GLA_WIDTH, GLA_RANK, GLA_RANK)
IN_COLS = sum(IN_WIDTHS)
IN_SPLITS_2 = tuple(int(v) for v in np.cumsum(IN_WIDTHS)[:-1])


def rms_norm_2(x, w):
    xf = x.astype(jnp.float32)
    y = xf * lax.rsqrt(jnp.mean(xf * xf, axis=-1, keepdims=True) + EPS)
    return (y * w.astype(jnp.float32)).astype(x.dtype)

def modulate(h, shift, scale):
    return h * (1.0 + scale[:, None, :]) + shift[:, None, :]

def swiglu_2(h, w1, w3, w2):
    return (jax.nn.silu(h @ w1) * (h @ w3)) @ w2

def split_heads(t, n_heads):
    b, n, _ = t.shape
    return t.reshape(b, n, n_heads, -1).transpose(0, 2, 1, 3).astype(jnp.float32)

def merge_heads(t):
    b, h, n, d = t.shape
    return t.transpose(0, 2, 1, 3).reshape(b, n, h * d)

def rotate(x, ang):
    x1, x2 = jnp.split(x, 2, axis=-1)
    cos, sin = jnp.cos(ang), jnp.sin(ang)
    return jnp.concatenate([x1 * cos - x2 * sin, x1 * sin + x2 * cos], axis=-1)

def grid_rope(x, n_tok):
    rows = n_tok // GRID_W
    row = jnp.repeat(jnp.arange(rows, dtype=jnp.float32), GRID_W)
    col = jnp.tile(jnp.arange(GRID_W, dtype=jnp.float32), rows)
    n_freq = x.shape[-1] // 4
    freqs = ROPE_BASE ** (-jnp.arange(n_freq, dtype=jnp.float32) / n_freq)
    xr, xc = jnp.split(x, 2, axis=-1)
    return jnp.concatenate([rotate(xr, row[:, None] * freqs), rotate(xc, col[:, None] * freqs)], axis=-1)

def to_chunks(t, c):
    b, h, n, d = t.shape
    return t.reshape(b, h, n // c, c, d).transpose(2, 0, 1, 3, 4)

def from_chunks(t):
    nc, b, h, c, d = t.shape
    return t.transpose(1, 2, 0, 3, 4).reshape(b, h, nc * c, d)

def retention_chunked(q, k, v, s0, log_gamma):
    c = RET_CHUNK
    pos = jnp.arange(c, dtype=jnp.float32)
    diff = pos[:, None] - pos[None, :]
    lg = log_gamma[:, None, None]
    decay = jnp.exp(jnp.where(diff >= 0, diff * lg, -jnp.inf))
    q_dec = jnp.exp((pos + 1.0) * log_gamma[:, None])[..., None]
    k_dec = jnp.exp((c - 1.0 - pos) * log_gamma[:, None])[..., None]
    chunk_dec = jnp.exp(c * log_gamma)[:, None, None]

    def step(s, xs):
        qc, kc, vc = xs
        scores = jnp.einsum('bhid,bhjd->bhij', qc, kc) * decay
        o = jnp.einsum('bhij,bhje->bhie', scores, vc) + jnp.einsum('bhid,bhde->bhie', qc * q_dec, s)
        s = chunk_dec * s + jnp.einsum('bhjd,bhje->bhde', kc * k_dec, vc)
        return s, o

    s_fin, o = lax.scan(step, s0, (to_chunks(q, c), to_chunks(k, c), to_chunks(v, c)))
    return from_chunks(o), s_fin

def gla_chunked(q, k, v, g, s0):
    c = GLA_CHUNK
    tri = jnp.tril(jnp.ones((c, c), dtype=bool))

    def step(s, xs):
        qc, kc, vc, gc = xs
        b = jnp.cumsum(gc, axis=-2)
        rel = b[:, :, :, None, :] - b[:, :, None, :, :]
        rel = jnp.exp(jnp.where(tri[:, :, None], rel, -jnp.inf))
        scores = jnp.einsum('bhid,bhjd,bhijd->bhij', qc, kc, rel)
        o = jnp.einsum('bhij,bhje->bhie', scores, vc) + jnp.einsum('bhid,bhde->bhie', qc * jnp.exp(b), s)
        b_last = b[:, :, -1:, :]
        s = jnp.exp(b_last[:, :, 0, :])[..., None] * s + jnp.einsum('bhjd,bhje->bhde', kc * jnp.exp(b_last - b), vc)
        return s, o

    s_fin, o = lax.scan(step, s0, (to_chunks(q, c), to_chunks(k, c), to_chunks(v, c), to_chunks(g, c)))
    return from_chunks(o), s_fin

def bidir_prefix(scan_f, scan_b, lat_f, lat_b, ctx_f, ctx_b):
    flip = lambda ts: tuple(t[:, :, ::-1] for t in ts)
    q0, v0 = ctx_f[0], ctx_f[2]
    s0 = jnp.zeros(q0.shape[:2] + (q0.shape[-1], v0.shape[-1]), jnp.float32)
    o_cf, s_f = scan_f(*ctx_f, s0)
    o_cb, s_b = scan_b(*flip(ctx_b), s0)
    o_lf, _ = scan_f(*lat_f, s_f)
    o_lb, _ = scan_b(*flip(lat_b), s_b)
    return o_lf + o_lb[:, :, ::-1], o_cf + o_cb[:, :, ::-1]

def retention_inputs(p, n_tok):
    q = split_heads(p[0], RET_HEADS) * (RET_DK ** -0.5)
    k = split_heads(p[1], RET_HEADS)
    if n_tok is not None:
        q, k = grid_rope(q, n_tok), grid_rope(k, n_tok)
    return (q, k, split_heads(p[2], RET_HEADS))

def gla_inputs(p, w_f, b_f, w_b, b_b):
    q = split_heads(p[4], GLA_HEADS) * (GLA_DK ** -0.5)
    k = split_heads(p[5], GLA_HEADS)
    v = split_heads(p[6], GLA_HEADS)
    g_f = split_heads(jax.nn.log_sigmoid((p[8] @ w_f + b_f).astype(jnp.float32)), GLA_HEADS) / GLA_TAU
    g_b = split_heads(jax.nn.log_sigmoid((p[9] @ w_b + b_b).astype(jnp.float32)), GLA_HEADS) / GLA_TAU
    return (q, k, v, g_f), (q, k, v, g_b)

def merge_outputs(o_ret, o_gla, p, ret_norm_w, gla_norm_w, w_out, dtype):
    mu = jnp.mean(o_ret, axis=-1, keepdims=True)
    var = jnp.mean(jnp.square(o_ret - mu), axis=-1, keepdims=True)
    r = merge_heads((o_ret - mu) * lax.rsqrt(var + EPS)) * ret_norm_w * jax.nn.silu(p[3].astype(jnp.float32))
    gl = merge_heads(o_gla * lax.rsqrt(jnp.mean(o_gla * o_gla, axis=-1, keepdims=True) + EPS))
    gl = gl * gla_norm_w * jax.nn.silu(p[7].astype(jnp.float32))
    return jnp.concatenate([r, gl], axis=-1).astype(dtype) @ w_out

def token_mixing(h_lat, h_ctx, w_in, ret_decay_f, ret_decay_b, ret_norm_w,
                 gla_gate_w_f, gla_gate_b_f, gla_gate_w_b, gla_gate_b_b, gla_norm_w, w_out, with_ctx):
    n_lat = h_lat.shape[1]
    p_lat = jnp.split(h_lat @ w_in, IN_SPLITS_2, axis=-1)
    p_ctx = jnp.split(h_ctx @ w_in, IN_SPLITS_2, axis=-1)
    lg_f = jax.nn.log_sigmoid(ret_decay_f.astype(jnp.float32))
    lg_b = jax.nn.log_sigmoid(ret_decay_b.astype(jnp.float32))
    ret_lat = retention_inputs(p_lat, n_lat)
    ret_ctx = retention_inputs(p_ctx, None)
    o_ret_l, o_ret_c = bidir_prefix(lambda q, k, v, s: retention_chunked(q, k, v, s, lg_f),
                                    lambda q, k, v, s: retention_chunked(q, k, v, s, lg_b),
                                    ret_lat, ret_lat, ret_ctx, ret_ctx)
    gla_lat_f, gla_lat_b = gla_inputs(p_lat, gla_gate_w_f, gla_gate_b_f, gla_gate_w_b, gla_gate_b_b)
    gla_ctx_f, gla_ctx_b = gla_inputs(p_ctx, gla_gate_w_f, gla_gate_b_f, gla_gate_w_b, gla_gate_b_b)
    o_gla_l, o_gla_c = bidir_prefix(gla_chunked, gla_chunked, gla_lat_f, gla_lat_b, gla_ctx_f, gla_ctx_b)
    y_lat = merge_outputs(o_ret_l, o_gla_l, p_lat, ret_norm_w, gla_norm_w, w_out, h_lat.dtype)
    y_ctx = None
    if with_ctx:
        y_ctx = merge_outputs(o_ret_c, o_gla_c, p_ctx, ret_norm_w, gla_norm_w, w_out, h_ctx.dtype)
    return y_lat, y_ctx

def second_inputs(seed: int = 0) -> dict:
    key = jax.random.key(seed)
    ks = jax.random.split(key, 32)
    f32 = jnp.float32

    def nrm(k, shape, scale):
        return jax.random.normal(k, shape, f32) * scale

    def gain(k, shape):
        return 1.0 + 0.05 * jax.random.normal(k, shape, f32)

    decay_logit = jnp.log(2.0 ** (5.0 + jnp.arange(RET_HEADS, dtype=f32)) - 1.0)
    return {
        "x": nrm(ks[0], (BATCH, SEQ, D_MODEL), 1.0),
        "c": nrm(ks[1], (BATCH, D_MODEL), 1.0),
        "ctx": nrm(ks[2], (BATCH, CTX_LEN, D_MODEL), 1.0),
        "c_ctx": nrm(ks[3], (D_MODEL,), 1.0),
        "ada_w": nrm(ks[4], (DEPTH_2, D_MODEL, N_MOD * D_MODEL), 0.5 * D_MODEL ** -0.5),
        "ada_b": nrm(ks[5], (DEPTH_2, N_MOD * D_MODEL), 0.02),
        "norm1_w": gain(ks[6], (DEPTH_2, D_MODEL)),
        "ffn1_w1": nrm(ks[7], (DEPTH_2, D_MODEL, D_FF), D_MODEL ** -0.5),
        "ffn1_w3": nrm(ks[8], (DEPTH_2, D_MODEL, D_FF), D_MODEL ** -0.5),
        "ffn1_w2": nrm(ks[9], (DEPTH_2, D_FF, D_MODEL), D_FF ** -0.5),
        "norm2_w": gain(ks[10], (DEPTH_2, D_MODEL)),
        "w_in": nrm(ks[11], (DEPTH_2, D_MODEL, IN_COLS), D_MODEL ** -0.5),
        "ret_decay_f": decay_logit + 0.1 * jax.random.normal(ks[12], (DEPTH_2, RET_HEADS), f32),
        "ret_decay_b": decay_logit + 0.1 * jax.random.normal(ks[13], (DEPTH_2, RET_HEADS), f32),
        "ret_norm_w": gain(ks[14], (DEPTH_2, RET_WIDTH)),
        "gla_gate_w_f": nrm(ks[15], (DEPTH_2, GLA_RANK, GLA_HEADS * GLA_DK), GLA_RANK ** -0.5),
        "gla_gate_b_f": 1.0 + 0.5 * jax.random.normal(ks[16], (DEPTH_2, GLA_HEADS * GLA_DK), f32),
        "gla_gate_w_b": nrm(ks[17], (DEPTH_2, GLA_RANK, GLA_HEADS * GLA_DK), GLA_RANK ** -0.5),
        "gla_gate_b_b": 1.0 + 0.5 * jax.random.normal(ks[18], (DEPTH_2, GLA_HEADS * GLA_DK), f32),
        "gla_norm_w": gain(ks[19], (DEPTH_2, GLA_WIDTH)),
        "w_out": nrm(ks[20], (DEPTH_2, D_MIX_2, D_MODEL), D_MIX_2 ** -0.5),
        "norm3_w": gain(ks[21], (DEPTH_2, D_MODEL)),
        "ffn2_w1": nrm(ks[22], (DEPTH_2, D_MODEL, D_FF), D_MODEL ** -0.5),
        "ffn2_w3": nrm(ks[23], (DEPTH_2, D_MODEL, D_FF), D_MODEL ** -0.5),
        "ffn2_w2": nrm(ks[24], (DEPTH_2, D_FF, D_MODEL), D_FF ** -0.5),
        "final_norm_w": gain(ks[25], (D_MODEL,)),
    }

def second_block(x, c, ctx, c_ctx, ada_w, ada_b, norm1_w, ffn1_w1, ffn1_w3, ffn1_w2, norm2_w, w_in,
              ret_decay_f, ret_decay_b, ret_norm_w, gla_gate_w_f, gla_gate_b_f, gla_gate_w_b, gla_gate_b_b,
              gla_norm_w, w_out, norm3_w, ffn2_w1, ffn2_w3, ffn2_w2, final_norm_w):
    cond_lat = jax.nn.silu(c)
    cond_ctx = jax.nn.silu(c_ctx)[None, :]
    for i in range(DEPTH_2):
        update_ctx = i < DEPTH_2 - 1
        m_l = jnp.split(cond_lat @ ada_w[i] + ada_b[i], N_MOD, axis=-1)
        m_c = jnp.split(cond_ctx @ ada_w[i] + ada_b[i], N_MOD, axis=-1)
        x = x + 0.5 * m_l[2][:, None, :] * swiglu_2(modulate(rms_norm_2(x, norm1_w[i]), m_l[0], m_l[1]),
                                                    ffn1_w1[i], ffn1_w3[i], ffn1_w2[i])
        ctx = ctx + 0.5 * m_c[2][:, None, :] * swiglu_2(modulate(rms_norm_2(ctx, norm1_w[i]), m_c[0], m_c[1]),
                                                        ffn1_w1[i], ffn1_w3[i], ffn1_w2[i])
        y_l, y_c = token_mixing(modulate(rms_norm_2(x, norm2_w[i]), m_l[3], m_l[4]),
                                modulate(rms_norm_2(ctx, norm2_w[i]), m_c[3], m_c[4]),
                                w_in[i], ret_decay_f[i], ret_decay_b[i], ret_norm_w[i],
                                gla_gate_w_f[i], gla_gate_b_f[i], gla_gate_w_b[i], gla_gate_b_b[i],
                                gla_norm_w[i], w_out[i], update_ctx)
        x = x + m_l[5][:, None, :] * y_l
        x = x + 0.5 * m_l[8][:, None, :] * swiglu_2(modulate(rms_norm_2(x, norm3_w[i]), m_l[6], m_l[7]),
                                                    ffn2_w1[i], ffn2_w3[i], ffn2_w2[i])
        if update_ctx:
            ctx = ctx + m_c[5][:, None, :] * y_c
            ctx = ctx + 0.5 * m_c[8][:, None, :] * swiglu_2(modulate(rms_norm_2(ctx, norm3_w[i]), m_c[6], m_c[7]),
                                                            ffn2_w1[i], ffn2_w3[i], ffn2_w2[i])
    return rms_norm_2(x, final_norm_w)


def setup_inputs(seed=0):
    out = dict(first_inputs(seed))
    for name, value in second_inputs(seed + 1).items():
        if name != "x":
            out[name + "_2"] = value
    return out


def reference(
    x, ffn_norm_g, ffn_w_gate, ffn_w_up, ffn_w_down, mix_norm_g, w_in, mla_q_norm_g, mla_w_uq,
    mla_kv_norm_g, mla_w_ukv, diff_lambda, diff_norm_g, nsa_cmp_pos, nsa_cmp_w1, nsa_cmp_b1,
    nsa_cmp_w2, nsa_gate_b, w_out, final_norm_g, c_2, ctx_2, c_ctx_2, ada_w_2, ada_b_2,
    norm1_w_2, ffn1_w1_2, ffn1_w3_2, ffn1_w2_2, norm2_w_2, w_in_2, ret_decay_f_2, ret_decay_b_2,
    ret_norm_w_2, gla_gate_w_f_2, gla_gate_b_f_2, gla_gate_w_b_2, gla_gate_b_b_2, gla_norm_w_2,
    w_out_2, norm3_w_2, ffn2_w1_2, ffn2_w3_2, ffn2_w2_2, final_norm_w_2,
):
    x = first_block(
        x, ffn_norm_g, ffn_w_gate, ffn_w_up, ffn_w_down, mix_norm_g, w_in, mla_q_norm_g,
        mla_w_uq, mla_kv_norm_g, mla_w_ukv, diff_lambda, diff_norm_g, nsa_cmp_pos, nsa_cmp_w1,
        nsa_cmp_b1, nsa_cmp_w2, nsa_gate_b, w_out, final_norm_g,
    )
    return second_block(
        x, c_2, ctx_2, c_ctx_2, ada_w_2, ada_b_2, norm1_w_2, ffn1_w1_2, ffn1_w3_2, ffn1_w2_2,
        norm2_w_2, w_in_2, ret_decay_f_2, ret_decay_b_2, ret_norm_w_2, gla_gate_w_f_2,
        gla_gate_b_f_2, gla_gate_w_b_2, gla_gate_b_b_2, gla_norm_w_2, w_out_2, norm3_w_2,
        ffn2_w1_2, ffn2_w3_2, ffn2_w2_2, final_norm_w_2,
    )


_drawn_inputs = setup_inputs


def setup_inputs(seed=0):
    import zlib

    import numpy as np

    out = dict(_drawn_inputs(seed))
    spreads = {}
    factors = {'ffn_norm_g': 3.142,
     'mix_norm_g': 2.919,
     'mla_q_norm_g': 8.0,
     'mla_kv_norm_g': 8.0,
     'diff_norm_g': 5.53,
     'nsa_cmp_pos': 8.0,
     'nsa_cmp_b1': 8.0,
     'nsa_gate_b': 8.0,
     'norm1_w_2': 6.953,
     'norm2_w_2': 2.717,
     'ret_norm_w_2': 8.0,
     'gla_norm_w_2': 7.958,
     'norm3_w_2': 7.591}
    for name, (base, spread) in spreads.items():
        noise = np.random.default_rng([zlib.crc32(name.encode()), seed]).standard_normal(out[name].shape)
        drawn = base * np.exp(spread * noise) if base else spread * noise
        out[name] = jnp.asarray(drawn.astype(out[name].dtype))
    for name, factor in factors.items():
        out[name] = (out[name] * factor).astype(out[name].dtype)
    return out
```

```python
from contextlib import ExitStack

import numpy as np

import concourse.bass as bass
from concourse import mybir

F32 = mybir.dt.float32
F32R = mybir.dt.float32r
BF16 = mybir.dt.bfloat16
ALU = mybir.AluOpType
ACT = mybir.ActivationFunctionType
AX_X = mybir.AxisListType.X

P = 128
D = 1024
KD = D // P
T = 512
TT = T // P
C = 256
TC = T + C
DEPTH = 2
D_FF = 2816
NF = D_FF // P
EPS = 1e-6
SLOTS = 4
SLOT = KD * P
PARTS = ((0, 8), (8, 8), (16, 6))
FFN_SLOTS = 2 * NF + KD * len(PARTS)
MLA_H, MLA_NOPE, MLA_ROPE = 4, 64, 32
MLA_QK = MLA_NOPE + MLA_ROPE
MLA_QR, MLA_KVR = 256, 128
DIFF_H, DIFF_QK = 4, 32
NSA_H, NSA_G = 8, 2
DV = 64
CMP_BLOCK, CMP_STRIDE, CMP_HID = 32, 16, 256
NC = (T - CMP_BLOCK) // CMP_STRIDE + 1
NEG = -1e30
assert T // 64 <= 16 and T <= 512
IN_CQ, IN_CKV, IN_KR, IN_DQ, IN_DK, IN_DV, IN_NQ, IN_NKV, IN_NG = (
    int(v) for v in np.cumsum((0, MLA_QR, MLA_KVR, MLA_ROPE, 256, 256, 256, 512, 768)))
N_IN = IN_NG + 3 * NSA_H
GATE_AT = P - 3 * NSA_H
CMP_K, CMP_V, SLC_K, SLC_V, WIN_K, WIN_V = (IN_NKV + P * i for i in range(6))
TILES = ([("cq", IN_CQ, 0), ("cq", IN_CQ + P, 1), ("cq", IN_CKV, 2), ("kr", IN_KR, 0), ("ck", CMP_K, 0), ("cv", CMP_V, 0)]
         + [("nq", IN_NQ + DV * j, j) for j in range(4)] + [("ks", SLC_K, 0), ("kw", WIN_K, 0)]
         + [("dq", IN_DQ + P * i, i) for i in range(2)] + [("dk", IN_DK + P * i, i) for i in range(2)] + [("ng", N_IN - P, 0)])
ROWS = ((IN_DV, 0, 2 * P), (SLC_V, 2 * P, P), (WIN_V, 3 * P, P))
ROW_K = 2
N_T, N_R = len(TILES), KD // ROW_K
UQ_SLOTS = 2
ROW_S0 = N_T + UQ_SLOTS + 1
PROJ_SLOTS = ROW_S0 + N_R
LATE_ITEMS = 2 * MLA_H + 2
ITEMS = N_T + LATE_ITEMS + TT
SLOT_ENDS = (1, 3, LATE_ITEMS - 1)
N_MOD = 9
ADA_SLOTS = N_MOD * KD // DEPTH
MIX_SLOTS = PROJ_SLOTS + ADA_SLOTS + KD
LAYER_SLOTS = 2 * FFN_SLOTS + MIX_SLOTS
ROPED = ("kr", "ck", "nq", "ks", "kw", "dq", "dk")
AUX_TAPS = 2
AUX_V = CMP_BLOCK // AUX_TAPS
AUX_RING = 4
AUX_AT = {}
for _s, _n in zip(range(7, 17), (3, 3, 3, 3, 3, 1, 4, 4, 4, 4)):
    AUX_AT[_s] = range(sum(len(r) for r in AUX_AT.values()), sum(len(r) for r in AUX_AT.values()) + _n)
VALUES_AT = 13
assert AUX_AT[VALUES_AT][0] == AUX_V and AUX_AT[16][-1] == 2 * AUX_V - 1
PARAMS = 8
HEADS = ([("mla", h, 0) for h in range(MLA_H)] + [("diff", h, m) for h in range(DIFF_H) for m in range(2)]
         + [("slc", h, 0) for h in range(NSA_H)] + [("win", h, 0) for h in range(NSA_H)])
NH = len(HEADS)
ATT = NH * TT
SCALED = 2 * DIFF_H // 2 + 2 * NSA_H
ADA_AT = {6 * i + 1: i for i in range(ADA_SLOTS // 2)}
ADA_K = KD // 2
COND_M = 66
assert max(ADA_AT) + 5 < ATT
AT_TURN, AT_CMP, AT_DIFF = 2, 6, 16
MIX_Y = KD
RET_H, RET_DK = 4, 128
GLA_H, GLA_DK, GLA_RANK, GLA_TAU = 4, 64, 16, 16.0
PAIRS = GLA_H // 2
GRID_W = 64
TCT = C // P
IN_2 = dict(zip(("rq", "rk", "rv", "rg", "gq", "gk", "gv", "gg", "gates"),
                (int(v) for v in np.cumsum((0, 512, 512, 512, 512, 256, 256, 512, 512 + 2 * GLA_RANK - P)))))
IN_2.update(rk_ctx=IN_2["rk"], gk_ctx=IN_2["gk"])
GATE_ROW = P - 2 * GLA_RANK
SLOTS_2 = []
for _kind, _slots in (("rk", 4), ("rq", 4), ("rk_ctx", 4), ("rv", 4), ("gk", 2), ("gq", 2), ("gk_ctx", 2), ("gv", 4),
                      ("gates", 2), ("rg", 4), ("gg", 4)):
    for _j in range(_slots):
        _wide = {"rk_ctx": (2, 4 * P), "rv": (2, 4 * P), "gv": (2, 4 * P), "gk_ctx": (4, 2 * P), "gates": (4, P)}
        _nk, _n = _wide.get(_kind, (KD, P))
        SLOTS_2.append((_kind, _j, _j * _nk if _kind in _wide else 0, _nk, _n))
OUTS_2 = []
_tiles = 0
for _s, (_kind, _j, _k0, _nk, _n) in enumerate(SLOTS_2):
    if _k0 + _nk < KD:
        continue
    if _kind in ("rv", "gv"):
        OUTS_2 += [(_s, _kind, 0, _t, _t) for _t in range(TT)]
    if _kind in ("rv", "gv", "rk_ctx", "gk_ctx"):
        OUTS_2 += [(_s, _kind.removesuffix("_ctx") + "_ctx", 0, _t, 6 + _t) for _t in range(TCT)]
    else:
        OUTS_2.append((_s, _kind, _j, 0, _tiles % 4))
        _tiles += 1
        if _kind == "gates":
            OUTS_2.append((_s, "gates_ctx", 0, 0, 6))
N_2 = len(OUTS_2)
ROPED_2 = ("rk", "rq")
S_FFN1 = 0
S_MIX2 = S_FFN1 + FFN_SLOTS
S_FFN2 = S_MIX2 + len(SLOTS_2) + KD
SLOTS_ALL = DEPTH * LAYER_SLOTS + S_FFN2 + FFN_SLOTS
assert S_MIX2 % SLOTS == 0 and S_FFN2 % SLOTS == 0
Y_FFN1 = KD
Y_MIX2 = Y_FFN1 + len(PARTS) * KD
Y_FFN2 = Y_MIX2 + KD
Y_END = Y_FFN2 + len(PARTS) * KD
ROW_NORM, ROW_FINAL, ROW_RET, ROW_GLA, ROW_COND = (int(v) for v in np.cumsum((0, 3 * KD, KD, 4, 4)))
STRIP = 2 * T - P
MID = T - P
LEVELS = 7
UNITS = TT * PAIRS
STATES = TCT + TT - 1
NORMS = 3
FFN_V = (0, NORMS - 1)


class Signal:

    def __init__(self, sem, per_layer, start=0):
        self.sem, self.per_layer, self.start = sem, per_layer, start

    def __call__(self, layer, n):
        return self.sem, layer * self.per_layer + (self.start + n)


def build(nc, a, out):
    ctx = ExitStack()
    with ctx:
        top = [(nc.sbuf_base + 63) // 64 * 64]

        def put(name, shape, dt=F32):
            t = nc.alloc_sbuf_tensor_at(name, shape, dt, offset=top[0])
            size = int(np.prod(shape[1:])) * (2 if dt == BF16 else 4)
            top[0] += (size + 31) // 32 * 32
            assert top[0] <= nc.sbuf_usable_end, (name, top[0])
            return t

        def sem(name):
            return ctx.enter_context(nc.semaphore(name))

        def signal(name, per_layer, start=0):
            return Signal(sem(name), per_layer, start)

        x_lat = put("x_lat", [P, KD, T])
        w_raw = put("w_raw", [P, SLOTS, SLOT])
        w_hi = put("w_hi", [P, SLOTS, SLOT], F32R)
        w_lo = put("w_lo", [P, SLOTS, SLOT], F32R)
        h_at = top[0]
        h_hi = put("h_hi", [P, KD, T], F32R)
        h_lo = put("h_lo", [P, KD, T], F32R)
        squares_at = top[0]
        squares = put("squares", [P, 2, TC])
        normed_at = top[0]
        normed = put("normed", [P, 2, TC])
        rstd = put("rstd", [P, TC])
        ident = put("ident", [P, P])
        ones = put("ones", [P, P])
        gains = put("gains", [P, 70])
        layer_gains = put("layer_gains", [P, 31])
        eps = put("eps", [P, 1])
        rope_at = top[0]
        rope = put("rope", [P, 4, T])
        rotate = put("rotate", [P, 2, P])
        ident_b = put("ident_b", [P, P], BF16)
        causal_b = put("causal_b", [P, P], BF16)
        cmp_any = put("cmp_any", [P, 1])
        lam_consts = put("lam_consts", [P, 2 * DEPTH])
        lam_layer = put("lam_layer", [P, 2])
        credits = put("credits", [P, 20])
        gains_2 = put("gains_2", [P, 56])
        mod = put("mod", [P, 2, N_MOD * KD])
        cond_hi = put("cond_hi", [P, 2 * KD + COND_M], F32R)
        cond_lo = put("cond_lo", [P, 2 * KD + COND_M], F32R)
        decay = put("decay", [P, 2, RET_H])
        zone = top[0]

        a_hi = put("a_hi", [P, PARTS[0][1], TC], F32R)
        a_lo = put("a_lo", [P, PARTS[0][1], TC], F32R)
        silu_g = put("silu_g", [P, 2, TC])
        gated = put("gated", [P, 2, TC])
        x_ctx = put("x_ctx", [P, KD, C])
        h_ctx_hi = put("h_ctx_hi", [P, KD, C], F32R)
        h_ctx_lo = put("h_ctx_lo", [P, KD, C], F32R)
        top[0] = zone
        x_rows = put("x_rows", [P, TT, D])
        gain_rows = put("gain_rows", [P, P])
        gain_rows_2 = put("gain_rows_2", [P, P])
        cond = put("cond", [P, KD, 2])
        causal = put("causal", [P, P])
        top[0] = zone
        y_rows = put("y_rows", [P, 2, D])

        top[0] = zone
        aux = nc.alloc_sbuf_tensor_at("aux", [P, AUX_RING, AUX_TAPS * CMP_HID], F32, offset=zone)
        q_mla = put("q_mla", [P, MLA_H, T])
        k_mla = put("k_mla", [P, MLA_H, T])
        v_mla = put("v_mla", [P, TT, MLA_H * DV])
        q_diff = put("q_diff", [P, 2, T])
        k_diff = put("k_diff", [P, 2, T])
        v_diff = put("v_diff", [P, TT, 2 * P])
        q_nsa = put("q_nsa", [P, 4, T])
        k_slc = put("k_slc", [P, T])
        k_win = put("k_win", [P, T])
        v_slc = put("v_slc", [P, TT, P])
        v_win = put("v_win", [P, TT, P])
        taps = put("taps", [P, CMP_BLOCK, NC])
        rope_in = put("rope_in", [P, 2, T])
        v_cmp = put("v_cmp", [P, 2, 4 * DV])
        lam_rows = put("lam_rows", [P, 4 * DIFF_QK])
        lam_stats = put("lam_stats", [P, 8])
        diff_gain = put("diff_gain", [P, DV])
        gate_bias = put("gate_bias", [P, 3 * NSA_H])
        gates = put("gates", [P, TT, 3 * NSA_H])
        pos_rows = put("pos_rows", [2 * CMP_BLOCK, P])
        pos_cols = put("pos_cols", [P, 2 * CMP_BLOCK])
        cmp_w2 = put("cmp_w2", [P, 2, 2, DV])
        cmp_mask = put("cmp_mask", [P, TT, NC])
        cmp_hid = put("cmp_hid", [P, 2, 2, 2, NC])
        k_cmp = put("k_cmp", [P, NC])
        neg_max = put("neg_max", [P, ATT])
        exp_sum = put("exp_sum", [P, ATT])
        scaled_inv = put("scaled_inv", [P, ATT])
        cmp_stats = put("cmp_stats", [P, 3, NSA_H])
        diff_stats = put("diff_stats", [P, DIFF_H])
        latents_at = top[0]
        latents = put("latents", [P, 3, T])
        latents_hi = put("latents_hi", [P, 3, T], F32R)
        latents_lo = put("latents_lo", [P, 3, T], F32R)
        tok_cmp = nc.alloc_sbuf_tensor_at("tok_cmp", [P, 2, T], F32, offset=zone + 4 * 2 * MLA_H * T)
        top[0] = zone + 4 * (2 * MLA_H * T + TT * MLA_H * DV + 2 * 2 * T + TT * 2 * P + 4 * T + 2 * T + 2 * TT * P)
        cmp_p = put("cmp_p", [P, NSA_H, CMP_BLOCK])
        cmp_pt = put("cmp_pt", [P, 2, P])
        diff_sq = put("diff_sq", [P, DIFF_H, DV])
        top[0] = latents_at
        probs = put("probs", [P, 2, T])
        probs_t = put("probs_t", [P, 2, T])
        o_rows = put("o_rows", [P, 2, D])
        diff_half = put("diff_half", [P, DV])
        mod_rows = put("mod_rows", [COND_M, 2 * P])

        top[0] = rope_at
        grid = put("grid", [P, 2, T])
        mod_gain = put("mod_gain", [P, 3, KD, 2])
        res = put("res", [P, 3, KD, 2])
        log_decay = put("log_decay", [P, 2, RET_H])
        log_steps = put("log_steps", [P, 4, 2 * RET_H])
        key_decay = put("key_decay", [P, 2, TCT, RET_H])
        key_pos = put("key_pos", [P, 2, TCT])
        chunk_decay = put("chunk_decay", [P, (TT + TCT) * PAIRS * 2, 2])
        gk_ctx = put("gk_ctx", [P, TCT, 2 * P])
        assert top[0] <= rope_at + 4 * 4 * T
        top[0] = zone
        ctx_rows = nc.alloc_sbuf_tensor_at("ctx_rows", [P, TCT, D], F32, offset=zone)
        rq = put("rq", [P, RET_H, T])
        rk = put("rk", [P, RET_H, T])
        rv = put("rv", [P, TT, RET_H * P])
        rv_ctx = put("rv_ctx", [P, TCT, RET_H * P])
        rk_ctx = put("rk_ctx", [P, TCT, RET_H * P])
        gv = put("gv", [P, TT, GLA_H * P])
        gv_ctx = put("gv_ctx", [P, TCT, GLA_H * P])
        gq = put("gq", [P, PAIRS, T])
        gk = put("gk", [P, PAIRS, T])
        gg = put("gg", [P, GLA_H, T])
        rg = put("rg", [P, RET_H, T])
        log_gates = put("log_gates", [P, TT + TCT, 2 * 2 * P])
        row_pos = put("row_pos", [P, 2, T])
        assert top[0] <= nc.sbuf_usable_end

        def over(name, shape, at, dt=F32):
            return nc.alloc_sbuf_tensor_at(name, shape, dt, offset=at)

        gate_in = over("gate_in", [P, TC], normed_at)
        strip = over("strip", [P, RET_H, STRIP], h_at)
        scores_r = over("scores_r", [P, TT, T], h_at + 14336)
        ctx_keys = over("ctx_keys", [P, 2, TCT, RET_H * P], h_at + 14336)
        q_dec = over("q_dec", [P, 2, T], h_at + 22528)
        strip_mid = over("strip_mid", [P, 2, RET_H, P], h_at + 22528)
        ret_state = over("ret_state", [P, 2, RET_H, P], h_at + 26624)
        gate_w = over("gate_w", [P, 4 * P], h_at + 26624)
        gate_b = over("gate_b", [P, 4 * P], h_at + 28672)
        gate_tmp = over("gate_tmp", [P, TT + TCT, 4 * P], h_at)
        distance = over("distance", [P, STRIP + 2 * P], squares_at)
        sums_f = over("sums_f", [P, 2 * (LEVELS + 1) * P], h_at)
        sums_b = over("sums_b", [P, 2 * (LEVELS + 1) * P], h_at + 8192)
        factors = over("factors", [P, 2, 2 * (LEVELS + 1), P], h_at + 16384)
        masks = over("masks", [P, LEVELS + 1, P], rope_at, mybir.dt.uint32)
        gla_state = over("gla_state", [P, 2, PAIRS, STATES, P], zone + 16384)
        scores_g = over("scores_g", [P, 2, 2, P], zone + 28672)
        tri = over("tri", [P, 2, P], zone + 28672 + 2048)
        gk_dec = over("gk_dec", [P, 2, 2, 2 * P], squares_at)
        gk_rows = over("gk_rows", [P, TT, 2 * P], squares_at + 4096)
        q_twice = over("q_twice", [P, PAIRS, T], squares_at + 8192)
        std_2 = over("std_2", [P, 2, T], rope_at)

        psum = ctx.enter_context(nc.psum_tensor("psum", [P, 8, 512], F32))

        consts_loaded = sem("consts_loaded")
        x_rows_loaded = sem("x_rows_loaded")
        eps_set = sem("eps_set")
        x_turned = sem("x_turned")
        gains_turned = sem("gains_turned")
        gains_ready = sem("gains_ready")
        layer_gains_ready = signal("layer_gains_ready", 1)
        slot_loaded = [sem(f"slot_loaded{i}") for i in range(SLOTS)]
        hi_ready = sem("hi_ready")
        lo_ready = sem("lo_ready")
        slot_used = sem("slot_used")
        sq_ready = signal("sq_ready", NORMS * KD)
        sq_used = signal("sq_used", NORMS * KD, 2)
        std_ready = signal("std_ready", NORMS)
        rstd_ready = signal("rstd_ready", NORMS)
        normed_ready = signal("normed_ready", NORMS * KD)
        h_hi_ready = signal("h_hi_ready", NORMS * KD)
        h_lo_ready = signal("h_lo_ready", NORMS * KD, 2)
        silu_done = signal("silu_done", 2 * NF)
        gated_ready = signal("gated_ready", 2 * NF, 2)
        a_hi_ready = signal("a_hi_ready", 2 * NF)
        a_lo_ready = signal("a_lo_ready", 2 * NF, 2)
        LAYER_Y = 2 * len(PARTS) * KD + MIX_Y
        x_updated = signal("x_updated", LAYER_Y, KD)
        params_loaded = signal("params_loaded", PARAMS * 16)
        aux_loaded = [signal(f"aux_loaded{i}", 2 * AUX_V // AUX_RING * 32) for i in range(AUX_RING)]
        nq_loaded = [signal(f"nq_loaded{i}", 16) for i in range(4)]
        aux_used = signal("aux_used", 2 * AUX_V, AUX_RING)
        copied = signal("copied", ITEMS, 2)
        item_done = signal("item_done", LATE_ITEMS - len(SLOT_ENDS))
        latent_sq = signal("latent_sq", 2)
        latent_sum = signal("latent_sum", 2)
        latent_std = signal("latent_std", 2)
        latent_normed = signal("latent_normed", 3)
        latent_hi_ready = signal("latent_hi_ready", 3)
        latent_lo_ready = signal("latent_lo_ready", 3)
        rows_loaded = [signal(f"rows_loaded{i}", 32) for i in range(N_R)]
        rows_done = signal("rows_done", TT - 1)
        gates_turned_1 = signal("gates_turned_1", 1)
        GATE_EVENT = 2 + sum(k in ROPED for k, _, _ in TILES) + 1
        EVENTS = GATE_EVENT + MLA_H
        rotated = signal("rotated", EVENTS - 3)
        turn_read = signal("turn_read", EVENTS, 2)
        roped = signal("roped", EVENTS - 3)
        lam_step = signal("lam_step", 4)
        lam_exp = signal("lam_exp", 1)
        pos_turned = signal("pos_turned", 1)
        pos_ready = signal("pos_ready", 1)
        taps_ready = signal("taps_ready", 2)
        hid_ready = signal("hid_ready", 2)
        cmp_kv_done = signal("cmp_kv_done", 1)
        cmp_kv_ready = signal("cmp_kv_ready", 1)
        cmp_zeroed = signal("cmp_zeroed", 1)
        gate_exp = signal("gate_exp", 1)
        gate_step = signal("gate_step", 2)
        scores_done = signal("scores_done", ATT)
        max_ready = signal("max_ready", ATT)
        exp_ready = signal("exp_ready", ATT)
        probs_turned = signal("probs_turned", ATT)
        probs_t_act = signal("probs_t_act", ATT // 2)
        probs_t_dve = signal("probs_t_dve", ATT // 2)
        o_done = signal("o_done", ATT)
        inv_ready = signal("inv_ready", ATT)
        scaled_ready = signal("scaled_ready", SCALED * TT)
        o_ready = signal("o_ready", ATT)
        cmp_scores_done = signal("cmp_scores_done", TT)
        cmp_step = signal("cmp_step", 7 * TT + 2)
        cmp_exp = signal("cmp_exp", TT)
        cmp_turned = signal("cmp_turned", TT)
        cmp_pt_ready = signal("cmp_pt_ready", TT)
        cmp_o_done = signal("cmp_o_done", TT)
        cmp_o_ready = signal("cmp_o_ready", TT)
        diff_step = signal("diff_step", 4 * TT)
        diff_std = signal("diff_std", TT)
        diff_ready = signal("diff_ready", TT)
        o_turned = signal("o_turned", 2 * TT)
        o_hi_ready = signal("o_hi_ready", 2 * TT)
        o_lo_ready = signal("o_lo_ready", 2 * TT)
        final_ready = sem("final_ready")
        cond_step = sem("cond_step")
        log_step = sem("log_step")
        log_exp = sem("log_exp")
        key_step = sem("key_step")
        cond_ready = sem("cond_ready")
        mod_done = sem("mod_done")
        block2_loaded = sem("block2_loaded")
        ctx_loaded = sem("ctx_loaded")
        ctx_turned = sem("ctx_turned")
        ctx_ready = sem("ctx_ready")
        item_done_2 = sem("item_done_2")
        copied_2 = sem("copied_2")
        rotated_2 = sem("rotated_2")
        rot_read_2 = sem("rot_read_2")
        roped_2 = sem("roped_2")
        gate_w_zeroed = sem("gate_w_zeroed")
        gate_w_loaded = sem("gate_w_loaded")
        ret_consts_loaded = sem("ret_consts_loaded")
        gla_consts_loaded = sem("gla_consts_loaded")
        sums_loaded = sem("sums_loaded")
        gate_done = sem("gate_done")
        gate_read = sem("gate_read")
        gate_neg = sem("gate_neg")
        gate_log = sem("gate_log")
        log_gates_ready = sem("log_gates_ready")
        strip_exp = sem("strip_exp")
        strip_step = sem("strip_step")
        strip_ready = sem("strip_ready")
        ctx_keys_ready = sem("ctx_keys_ready")
        ret_state_done = sem("ret_state_done")
        ret_state_ready = sem("ret_state_ready")
        ret_scores_done = sem("ret_scores_done")
        ret_scores_ready = sem("ret_scores_ready")
        q_exp_ready = sem("q_exp_ready")
        q_dec_ready = sem("q_dec_ready")
        ret_o_done = sem("ret_o_done")
        ret_o_ready = sem("ret_o_ready")
        gk_turned = sem("gk_turned")
        gk_rows_ready = sem("gk_rows_ready")
        totals_done = sem("totals_done")
        totals_ready = sem("totals_ready")
        suffix_done = sem("suffix_done")
        suffix_exp = sem("suffix_exp")
        gk_dec_ready = sem("gk_dec_ready")
        state_done = sem("state_done")
        state_copied = sem("state_copied")
        state_step = sem("state_step")
        sums_done = sem("sums_done")
        factor_exp = sem("factor_exp")
        factors_ready = sem("factors_ready")
        gla_scores_done = sem("gla_scores_done")
        gla_scores_step = sem("gla_scores_step")
        gla_o_done = sem("gla_o_done")
        gla_o_ready = sem("gla_o_ready")
        mean_done = sem("mean_done")
        centred = sem("centred")
        merge_sq = sem("merge_sq")
        merge_sum = sem("merge_sum")
        merge_std = sem("merge_std")
        merge_inv = sem("merge_inv")
        merge_normed = sem("merge_normed")
        merged = sem("merged")
        merge_hi = sem("merge_hi")
        merge_lo = sem("merge_lo")
        out_turned = sem("out_turned")
        y_rows_ready = sem("y_rows_ready")
        stored = [sem("stored0"), sem("stored1")]

        FFN_S0 = (0, FFN_SLOTS + MIX_SLOTS)
        FFN_Y0 = (0, len(PARTS) * KD + MIX_Y)
        FFN_N0 = (0, NF)
        LAST = DEPTH

        def slot_of(layer, s):
            return layer * (LAYER_SLOTS // SLOTS) + s // SLOTS, s % SLOTS

        LAT = [(0, 0, T)]
        BOTH = [(0, 0, T), (T, 0, C)]

        def units():
            return [(n, n // PAIRS, n % PAIRS) for n in range(UNITS)]

        MIX_S0, MIX_Y0 = FFN_SLOTS, len(PARTS) * KD
        OUT_S0 = MIX_S0 + PROJ_SLOTS + ADA_SLOTS
        GAIN_MIX, GAIN_Q, GAIN_KV, GAIN_B1 = 2 * KD, 3 * KD, 3 * KD + 2, 3 * KD + 3

        CONSTS = 7 + 5 * DEPTH + 1 + 9 + 2

        def state_slot(t, way):
            order = (list(range(TCT + TT - 1)), list(range(TCT))[::-1] + list(range(TCT + 1, TCT + TT))[::-1])[way]
            return order.index(t) if t in order else None

        def states_before(t):
            return sum(state_slot(i, way) is not None for i in range(t) for way in range(2))

        def halves(hi, lo):
            return (lambda k: hi[:, k, :]), (lambda k: lo[:, k, :])

        def key_values(kind, h, m):
            if kind == "mla":
                return (lambda i: q_mla[0:MLA_QK, h, i]), (lambda n: k_mla[0:MLA_QK, h, 0:n]), (lambda b: v_mla[:, b, h * DV:(h + 1) * DV])
            if kind == "diff":
                r, c = 32 * ((2 * h + m) % 4), (2 * h + m) // 4
                return (lambda i: q_diff[r:r + 32, c, i]), (lambda n: k_diff[r:r + 32, c, 0:n]), (lambda b: v_diff[:, b, h * DV:(h + 1) * DV])
            g, c = h // 4, h % 4
            k, v = (k_slc, v_slc) if kind == "slc" else (k_win, v_win)
            r = DV * g
            return (lambda i: q_nsa[r:r + DV, c, i]), (lambda n: k[r:r + DV, 0:n]), (lambda b: v[:, b, r:r + DV])

        def last_turned(layer, t):
            return (probs_t_act, probs_t_dve)[t % 2](layer, t // 2 + 1)

        block = ctx.enter_context(nc.Block())

        @block.sync
        def _(sp):
            sp.dma_start(ident[:], a["c_ident"]).then_inc(consts_loaded, 16)
            sp.dma_start(ones[:], a["c_ones"]).then_inc(consts_loaded, 16)
            row = 0
            for dst, names in ((gain_rows, [(n, layer) for layer in range(DEPTH) for n in ("ffn_norm_g", "mix_norm_g", "mla_q_norm_g", "mla_kv_norm_g", "nsa_cmp_b1")]
                                + [("final_norm_g", None)]),
                               (gain_rows_2, [(n, None) for n in ("ada_b_2", "norm1_w_2", "norm2_w_2", "norm3_w_2", "final_norm_w_2",
                                                                  "ret_norm_w_2", "gla_norm_w_2", "c_2", "c_ctx_2")])):
                row = 0
                for name, layer in names:
                    src = a[name] if layer is None else a[name][layer]
                    while len(src.shape) > 1:
                        src = src.rearrange("a b ... -> (a b) ...") if len(src.shape) > 2 else src.rearrange("a b -> (a b)")
                    n = src.shape[0] // P
                    sp.dma_start(dst[row:row + n, :], src.rearrange("(r p) -> r p", p=P)).then_inc(consts_loaded, 16)
                    row += n
            for way, name in enumerate(("ret_decay_f_2", "ret_decay_b_2")):
                sp.dma_start(decay[:, way, :], a[name][0].partition_broadcast(P)).then_inc(consts_loaded, 16)
            sp.dma_start(rope[:], a["c_rope"]).then_inc(consts_loaded, 16)
            sp.dma_start(rotate[:], a["c_rotate"]).then_inc(consts_loaded, 16)
            sp.dma_start(causal[:], a["c_causal"]).then_inc(consts_loaded, 16)
            sp.dma_start(cmp_any[:], a["c_cmp_any"]).then_inc(consts_loaded, 16)
            sp.dma_start(lam_consts[:], a["c_lam"]).then_inc(consts_loaded, 16)
            sp.dma_start(x_rows[:], a["x"][0].rearrange("(t p) d -> p t d", p=P)).then_inc(x_rows_loaded, 16)

            def load_slot(turn, pos, dst, src):
                sp.wait_ge(lo_ready, turn * SLOTS + (pos + 1))
                sp.dma_start(dst, src).then_inc(slot_loaded[pos], 16)

            def slot_tile(pos, k=KD, n=P):
                return w_raw[:, pos, 0:k * n].rearrange("p (k n) -> p k n", k=k)

            def ffn(layer, s, gate, up, down):
                for f0, nf in PARTS:
                    turn, _ = slot_of(layer, s)
                    with sp.Fori(0, nf // 2) as it:
                        for i in range(SLOTS):
                            w = (gate, up)[i % 2]
                            load_slot(turn + it, i, slot_tile(i),
                                      w[:, :, bass.ds(it * (2 * P) + (f0 + i // 2) * P, P)])
                    s += 2 * nf
                    turn, _ = slot_of(layer, s)
                    with sp.Fori(0, KD // SLOTS) as it:
                        for i in range(SLOTS):
                            load_slot(turn + it, i, slot_tile(i, nf),
                                      down[:, f0:f0 + nf, bass.ds(it * (SLOTS * P) + i * P, P)])
                    s += KD

            def mixer(layer):
                w_in = a["w_in"].rearrange("l (k p) n -> l p k n", p=P)[layer]
                turn0, _ = slot_of(layer, MIX_S0)

                def load_mix(s, dst, src):
                    load_slot(turn0 + s // SLOTS, s % SLOTS, dst, src)

                def load_params():
                    sp.wait_ge(*x_updated(layer, MIX_Y0))
                    for dst, src in (
                            (cmp_mask[:], a["c_cmp_mask"]),
                            (lam_rows[:], a["diff_lambda"].rearrange("l m d -> l (m d)")[layer].partition_broadcast(P)),
                            (diff_gain[:], a["diff_norm_g"][layer].partition_broadcast(P)),
                            (gate_bias[:], a["nsa_gate_b"][layer].partition_broadcast(P)),
                            (pos_rows[:, 0:DV], a["nsa_cmp_pos"].rearrange("l v j d -> l (v j) d")[layer]),
                            (pos_rows[:, DV:P], a["nsa_cmp_pos"].rearrange("l v j d -> l (v j) d")[layer]),
                            (cmp_w2[:, 0], a["nsa_cmp_w2"].rearrange("l v (c p) d -> (l v) p c d", p=P)[layer * 2]),
                            (cmp_w2[:, 1], a["nsa_cmp_w2"].rearrange("l v (c p) d -> (l v) p c d", p=P)[layer * 2 + 1])):
                        sp.dma_start(dst, src).then_inc(params_loaded.sem, 16)

                def load_aux(n):
                    v, j = n // AUX_V, n % AUX_V * AUX_TAPS
                    sp.wait_ge(*aux_used(layer, n + 1 - AUX_RING))
                    src = a["nsa_cmp_w1"].rearrange("l v (j d) h -> (l v) d j h", d=DV)[layer * 2 + v][:, j:j + AUX_TAPS, :]
                    for g in range(2):
                        sp.dma_start(aux[DV * g:DV * (g + 1), n % AUX_RING, :].rearrange("d (j h) -> d j h", j=AUX_TAPS),
                                     src).then_inc(aux_loaded[n % AUX_RING].sem, 16)

                for s in range(PROJ_SLOTS):
                    if s == SLOTS:
                        load_params()
                    if s < N_T:
                        kind, col, place = TILES[s]
                        if kind == "nq":
                            two = w_raw[:, s % SLOTS, :].rearrange("p (k g d) -> p k g d", k=KD, g=2)
                            col = IN_NQ + DV * place
                            load_mix(s, two[:, :, 0, :], w_in[:, :, col:col + DV])
                            sp.dma_start(two[:, :, 1, :], w_in[:, :, col + 256:col + 256 + DV]).then_inc(nq_loaded[place].sem, 16)
                        else:
                            load_mix(s, slot_tile(s % SLOTS), w_in[:, :, col:col + P])
                    elif s < N_T + UQ_SLOTS:
                        n = 2 * MLA_QK
                        c = (s - N_T) * n
                        load_mix(s, slot_tile(s % SLOTS, 2, n), a["mla_w_uq"].rearrange("l (k p) n -> l p k n", p=P)[layer][:, :, c:c + n])
                    elif s < ROW_S0:
                        load_mix(s, w_raw[:, s % SLOTS, 0:512], a["mla_w_ukv"][layer])
                    else:
                        q = s - ROW_S0
                        for i, (col, at, n) in enumerate(ROWS):
                            dst = slot_tile(s % SLOTS, ROW_K, 4 * P)[:, :, at:at + n]
                            src = w_in[:, q * ROW_K:(q + 1) * ROW_K, col:col + n]
                            if i == 0:
                                load_mix(s, dst, src)
                            else:
                                sp.dma_start(dst, src).then_inc(rows_loaded[q].sem, 16)
                    for n in AUX_AT.get(s - 2, ()):
                        load_aux(n)
                ada_w = a["ada_w_2"][0].rearrange("(k p) n -> p k n", p=P)
                with sp.Fori(0, ADA_SLOTS // SLOTS) as it:
                    for i in range(SLOTS):
                        load_slot(turn0 + PROJ_SLOTS // SLOTS + it, i, slot_tile(i, ADA_K, 2 * P),
                                  ada_w[:, i % 2 * ADA_K:(i % 2 + 1) * ADA_K,
                                        bass.ds(layer * (ADA_SLOTS * P) + it * (SLOTS * P) + i // 2 * 2 * P, 2 * P)])
                w_out = a["w_out"].rearrange("l (k p) n -> l p k n", p=P)[layer]
                for c in range(KD):
                    load_mix(PROJ_SLOTS + ADA_SLOTS + c, slot_tile((PROJ_SLOTS + ADA_SLOTS + c) % SLOTS), w_out[:, :, c * P:(c + 1) * P])

            ffn_gate = a["ffn_w_gate"].rearrange("l j (k p) f -> (l j) p k f", p=P)
            ffn_up = a["ffn_w_up"].rearrange("l j (k p) f -> (l j) p k f", p=P)
            ffn_down = a["ffn_w_down"].rearrange("l j (k p) f -> (l j) p k f", p=P)
            with sp.Fori(0, DEPTH) as layer:
                for j in range(2):
                    n = layer * 2 + j
                    ffn(layer, FFN_S0[j], ffn_gate[n], ffn_up[n], ffn_down[n])
                    if j == 0:
                        mixer(layer)

            sp.wait_ge(*x_updated(LAST, 0))
            sp.dma_start(ctx_rows[:], a["ctx_2"][0].rearrange("(t p) d -> p t d", p=P)).then_inc(ctx_loaded, 16)
            sp.dma_start(grid[:], a["c_grid"]).then_inc(block2_loaded, 16)
            sp.dma_start(key_pos[:], a["c_key_pos"]).then_inc(block2_loaded, 16)
            f1, f2 = ([a[f"ffn{i}_w{j}_2"][0].rearrange("(k p) f -> p k f", p=P) for j in (1, 3, 2)] for i in (1, 2))
            ffn(LAST, S_FFN1, *f1)

            def load_mix_2(s, src, k=KD, n=P):
                turn, pos = slot_of(LAST, S_MIX2 + s)
                load_slot(turn, pos, slot_tile(pos, k, n), src)

            w_in_2 = a["w_in_2"][0].rearrange("(k p) n -> p k n", p=P)
            w_out_2 = a["w_out_2"][0].rearrange("(k p) n -> p k n", p=P)
            for s, (kind, j, k0, nk, n) in enumerate(SLOTS_2):
                c = IN_2[kind] + (j * P if nk == KD else 0)
                load_mix_2(s, w_in_2[:, k0:k0 + nk, c:c + n], nk, n)
            for c in range(SLOTS):
                load_mix_2(len(SLOTS_2) + c, w_out_2[:, :, c * P:(c + 1) * P])
            sp.wait_ge(gate_w_zeroed, 1)
            for way, name in enumerate(("f", "b")):
                at = slice(way * 2 * P, (way + 1) * 2 * P)
                sp.dma_start(gate_w[GATE_ROW + way * GLA_RANK:GATE_ROW + (way + 1) * GLA_RANK, at], a[f"gla_gate_w_{name}_2"][0]).then_inc(gate_w_loaded, 16)
                sp.dma_start(gate_b[:, at], a[f"gla_gate_b_{name}_2"][0].partition_broadcast(P)).then_inc(gate_w_loaded, 16)
            sp.wait_ge(roped_2, 2 * RET_H)
            sp.wait_ge(copied_2, N_2)
            sp.dma_start(distance[:], a["c_distance"]).then_inc(ret_consts_loaded, 16)
            sp.dma_start(row_pos[:], a["c_row_pos"]).then_inc(ret_consts_loaded, 16)
            sp.dma_start(masks[:], a["c_masks"]).then_inc(gla_consts_loaded, 16)
            sp.wait_ge(ret_state_done, 2)
            sp.dma_start(tri[:], a["c_tri"]).then_inc(gla_consts_loaded, 16)
            for c in range(SLOTS, KD):
                load_mix_2(len(SLOTS_2) + c, w_out_2[:, :, c * P:(c + 1) * P])
            sp.wait_ge(ret_o_done, RET_H)
            sp.dma_start(sums_f[:], a["c_sums_f"]).then_inc(sums_loaded, 16)
            sp.dma_start(sums_b[:], a["c_sums_b"]).then_inc(sums_loaded, 16)
            ffn(LAST, S_FFN2, *f2)
            for t in range(TT):
                sp.wait_ge(y_rows_ready, t + 1)
                sp.dma_start(out[0, t * P:(t + 1) * P, :], y_rows[:, t % 2, :]).then_inc(stored[t % 2], 16)
            for t in range(2):
                sp.wait_ge(stored[t], 32)

        @block.gpsimd
        def _(pool):
            for i in range(SLOTS):
                nc.gpsimd.memset(w_raw[:, i, :], 0.0).then_inc(lo_ready, 1)
            with pool.Fori(0, SLOTS_ALL // SLOTS) as turn:
                for i in range(SLOTS):
                    pool.wait_ge(hi_ready, turn * SLOTS + (i + 1))
                    nc.gpsimd.tensor_tensor(w_lo[:, i, :], w_raw[:, i, :], w_hi[:, i, :].bitcast(F32),
                                            ALU.subtract).then_inc(lo_ready, 1)

        @block.scalar
        def _(act):
            def split(turn, pos):
                act.wait_ge(slot_loaded[pos], turn * 16 + 16)
                act.wait_ge(slot_used, turn * SLOTS + (pos + 1))
                nc.scalar.activation(w_hi[:, pos, :], w_raw[:, pos, :], ACT.Copy).then_inc(hi_ready, 1)

            def norm_statistics(layer, v, y, groups):
                for c in range(KD):
                    act.wait_ge(*x_updated(layer, y - KD + c + 1))
                    act.wait_ge(*sq_used(layer, v * KD + c - 1))
                    for x, o, n in groups:
                        last = nc.scalar.activation(squares[:, c % 2, o:o + n], x[:, c, :], ACT.Square)
                    last.then_inc(sq_ready.sem, 1)
                act.wait_ge(*sq_used(layer, v * KD + KD))
                for g, (x, o, n) in enumerate(groups):
                    last = nc.scalar.activation(rstd[:, o:o + n], psum[:, g, 0:n], ACT.Sqrt,
                                                bias=eps[:, 0:1], scale=1.0 / D)
                last.then_inc(std_ready.sem, 1)

            def norm_high(layer, v, groups, shift=None):
                for c in range(KD):
                    act.wait_ge(*normed_ready(layer, v * KD + c + 1))
                    for g, (hi, o, n) in enumerate(groups):
                        if shift is None:
                            last = nc.scalar.activation(hi[:, c, :], normed[:, c % 2, o:o + n], ACT.Copy)
                        else:
                            last = nc.scalar.activation(hi[:, c, :], normed[:, c % 2, o:o + n], ACT.Identity, bias=shift(c, g))
                    last.then_inc(h_hi_ready.sem, 1)

            def ffn(layer, s, f, groups, last_ffn=False):
                width = groups[-1][0] + groups[-1][2]
                for part, (f0, nf) in enumerate(PARTS):
                    turn, _ = slot_of(layer, s + SLOTS)
                    with act.Fori(0, nf // 2) as it:
                        for i in range(2):
                            split(turn + it, 2 * i)
                            split(turn + it, 2 * i + 1)
                            tile = it * 2 + (f + f0 + i)
                            act.wait_ge(slot_used, (turn + it) * SLOTS + (2 * i + 2))
                            for g, (o, _, n) in enumerate(groups):
                                last = nc.scalar.activation(silu_g[:, i, o:o + n], psum[:, 3 * i + 2 * g, 0:n], ACT.Silu)
                            last.then_inc(silu_done.sem, 1)
                            act.wait_ge(*gated_ready(layer, tile + 1))
                            nc.scalar.activation(a_hi[:, bass.ds(it * 2 + i, 1), 0:width], gated[:, i:i + 1, 0:width],
                                                 ACT.Copy).then_inc(a_hi_ready.sem, 1)
                    s += 2 * nf
                    turn, _ = slot_of(layer, s + SLOTS)
                    with act.Fori(0, KD // SLOTS - (last_ffn and part == len(PARTS) - 1)) as it:
                        for i in range(SLOTS):
                            split(turn + it, i)
                    s += KD

            def mixer_projections(layer):
                turn0, _ = slot_of(layer, MIX_S0 + SLOTS)
                ropes = 0

                def copy(dst, src, scale=1.0):
                    return nc.scalar.activation(dst, src, ACT.Copy, scale=scale).then_inc(copied.sem, 1)

                def used(s):
                    act.wait_ge(slot_used, (turn0 - 1) * SLOTS + (SLOTS + s + 1))

                def hidden(v):
                    act.wait_ge(*aux_used(layer, (v + 1) * AUX_V))
                    for half in range(2):
                        for g in range(2):
                            last = nc.scalar.activation(cmp_hid[:, v, half, g, :], psum[:, 4 + 2 * half + g, 0:NC], ACT.Silu,
                                                        bias=layer_gains[:, GAIN_B1 + 2 * v + half:GAIN_B1 + 2 * v + half + 1])
                    last.then_inc(hid_ready.sem, 1)

                def next_split(s):
                    ahead = s + SLOTS
                    if ahead < N_T and TILES[ahead][0] == "nq":
                        act.wait_ge(*nq_loaded[TILES[ahead][2]](layer, 16))
                    if ROW_S0 <= ahead < PROJ_SLOTS:
                        act.wait_ge(*rows_loaded[ahead - ROW_S0](layer, 32))
                    split(turn0 + s // SLOTS, s % SLOTS)

                for s in range(N_T):
                    if s == VALUES_AT:
                        hidden(0)
                    next_split(s)
                    used(s)
                    bank = psum[:, s % 2, :]
                    kind, _, place = TILES[s]
                    if kind in ROPED or kind == "ng":
                        if ropes >= 2:
                            act.wait_ge(*roped(layer, ropes - 1))
                        scale = DV ** -0.5 if kind == "nq" else DIFF_QK ** -0.5 if kind == "dq" else 1.0
                        copy(rope_in[:, ropes % 2, :], bank, scale)
                        ropes += 1
                    else:
                        copy(latents[:, place, :] if kind == "cq" else tok_cmp[:, 1, :], bank)
                    if s == 1:
                        act.wait_ge(*copied(layer, 2))
                        for c in range(2):
                            last = nc.scalar.activation(squares.rearrange("p a n -> p (a n)")[:, c * T:(c + 1) * T], latents[:, c, :], ACT.Square)
                        last.then_inc(latent_sq.sem, 1)
                    if s == 2:
                        act.wait_ge(*copied(layer, 3))
                        nc.scalar.activation(squares.rearrange("p a n -> p (a n)")[:, 2 * T:3 * T], latents[:, 2, :],
                                             ACT.Square).then_inc(latent_sq.sem, 1)
                    if s == 3:
                        act.wait_ge(*latent_sum(layer, 1))
                        nc.scalar.activation(rstd[:, 0:T], psum[:, 2, :], ACT.Sqrt, bias=eps[:, 0:1],
                                             scale=1.0 / MLA_QR).then_inc(latent_std.sem, 1)
                    if s == 4:
                        act.wait_ge(*latent_sum(layer, 2))
                        nc.scalar.activation(squares[:, 0, 0:T], psum[:, 3, :], ACT.Sqrt, bias=eps[:, 0:1],
                                             scale=1.0 / MLA_KVR).then_inc(latent_std.sem, 1)
                        act.wait_ge(*lam_step(layer, 3))
                        nc.scalar.activation(lam_stats[:, 2:4], lam_stats[:, 0:2], ACT.Exp).then_inc(lam_exp.sem, 1)
                    if s == 5:
                        for c in range(3):
                            act.wait_ge(*latent_normed(layer, c + 1))
                            nc.scalar.activation(latents_hi[:, c, :], normed[:, c % 2, 0:T], ACT.Copy).then_inc(latent_hi_ready.sem, 1)
                hidden(1)
                for s in range(N_T, ROW_S0):
                    if s == ROW_S0 - 1:
                        act.wait_ge(*turn_read(layer, GATE_EVENT))
                        nc.scalar.activation(gates[:], gates[:], ACT.Exp, scale=-1.0).then_inc(gate_exp.sem, 1)
                    n0 = 2 * (s - N_T)
                    for n in range(n0, n0 + 2) if s < ROW_S0 - 1 else range(n0, LATE_ITEMS):
                        if n in SLOT_ENDS:
                            used(s)
                        else:
                            act.wait_ge(*item_done(layer, n + 1 - sum(e < n for e in SLOT_ENDS)))
                        bank = psum[:, (N_T + n) % 2, :]
                        if n < MLA_H:
                            copy(q_mla[0:MLA_QK, n, :], bank[0:MLA_QK, :], MLA_QK ** -0.5)
                        elif n < 2 * MLA_H:
                            copy(k_mla[0:MLA_NOPE, n - MLA_H, :], bank[0:MLA_NOPE, :])
                        else:
                            t = 2 * (n - 2 * MLA_H)
                            copy(v_mla[:, t:t + 2, :], bank.rearrange("p (t n) -> p t n", t=2))
                    next_split(s)
                act.wait_ge(*cmp_kv_done(layer, 1))
                nc.scalar.activation(k_cmp[:], psum[:, 4, 0:NC], ACT.Copy)
                act.wait_ge(*cmp_zeroed(layer, 1))
                for r in range(4):
                    last = nc.scalar.activation(v_cmp[32 * r:32 * r + NC, :, r * DV:(r + 1) * DV],
                                                psum[32 * r:32 * r + NC, 5, 0:2 * DV].rearrange("p (g d) -> p g d", g=2), ACT.Copy)
                last.then_inc(cmp_kv_ready.sem, 1)
                for s in range(ROW_S0, PROJ_SLOTS - 1):
                    next_split(s)
                for t in range(TT):
                    if t < TT - 1:
                        act.wait_ge(*rows_done(layer, t + 1))
                    else:
                        used(PROJ_SLOTS - 1)
                    bank = psum[:, 4 + t, :]
                    nc.scalar.activation(v_diff[:, t, :], bank[:, 0:2 * P], ACT.Copy)
                    nc.scalar.activation(v_slc[:, t, :], bank[:, 2 * P:3 * P], ACT.Copy)
                    copy(v_win[:, t, :], bank[:, 3 * P:4 * P])
                next_split(PROJ_SLOTS - 1)

            def turn_o(layer, i):
                for b in range(2):
                    act.wait_ge(*o_turned(layer, 2 * i + b + 1))
                    nc.scalar.activation(h_hi[:, 4 * b:4 * b + 4, i * P:(i + 1) * P], psum[:, 6 + b, :].rearrange("p (c q) -> p c q", c=4),
                                         ACT.Copy).then_inc(o_hi_ready.sem, 1)

            def attention(layer):
                for t in range(ATT + 1):
                    i, step = t // NH, t % NH
                    if t < ATT:
                        act.wait_ge(*max_ready(layer, t + 1))
                        if t >= 2:
                            act.wait_ge(*probs_turned(layer, t - 1))
                        n = (i + 1) * P
                        nc.scalar.activation(probs[:, t % 2, 0:n], psum[:, t % 2, 0:n], ACT.Exp, bias=neg_max[:, t:t + 1],
                                             accum_out=exp_sum[:, t:t + 1]).then_inc(exp_ready.sem, 1)
                        if step == AT_TURN + 1 and i > 0:
                            turn_o(layer, i - 1)
                        if step == AT_CMP + 2:
                            act.wait_ge(*cmp_step(layer, 2 + 7 * i + 3))
                            nc.scalar.activation(cmp_p[:, :, 0:NC], cmp_p[:, :, 0:NC], ACT.Exp).then_inc(cmp_exp.sem, 1)
                        if step == AT_DIFF + 2:
                            act.wait_ge(*diff_step(layer, 4 * i + 2))
                            nc.scalar.activation(diff_stats[:], diff_stats[:], ACT.Sqrt, bias=eps[:, 0:1],
                                                 scale=1.0 / DV).then_inc(diff_std.sem, 1)
                    p = t - 1
                    if t >= 1 and p % 2 == 0:
                        act.wait_ge(*probs_turned(layer, p + 1))
                        if p >= 2:
                            act.wait_ge(*o_done(layer, p - 1))
                        n = (p // NH + 1) * P
                        nc.scalar.activation(probs_t[:, 0, 0:n], psum[:, 2, 0:n], ACT.Copy).then_inc(probs_t_act.sem, 1)
                    for half in range(2):
                        if t - 4 - half in ADA_AT:
                            turn, pos = slot_of(layer, MIX_S0 + PROJ_SLOTS + 2 * ADA_AT[t - 4 - half] + half + SLOTS)
                            split(turn, pos)
                turn_o(layer, TT - 1)

            def mixer_output(layer):
                for c in range(KD):
                    turn, pos = slot_of(layer, OUT_S0 + SLOTS + c)
                    split(turn, pos)

            act.wait_ge(eps_set, 1)
            act.wait_ge(gains_ready, 1)
            nc.scalar.activation(cond[:], gains_2[:, ROW_COND:ROW_COND + 2 * KD].rearrange("p (g c) -> p c g", g=2), ACT.Silu).then_inc(cond_step, 1)
            act.wait_ge(cond_step, 1)
            nc.scalar.activation(cond_hi[:, 0:2 * KD], cond[:].rearrange("p c g -> p (c g)"), ACT.Copy).then_inc(cond_step, 1)
            for i in range(SLOTS):
                split(0, i)
            with act.Fori(0, DEPTH) as layer:
                for j in range(2):
                    norm_statistics(layer, FFN_V[j], FFN_Y0[j], [(x_lat, 0, T)])
                    norm_high(layer, FFN_V[j], [(h_hi, 0, T)])
                    ffn(layer, FFN_S0[j], FFN_N0[j], LAT)
                    if j == 0:
                        norm_statistics(layer, 1, MIX_Y0, [(x_lat, 0, T)])
                        norm_high(layer, 1, [(h_hi, 0, T)])
                        mixer_projections(layer)
                        attention(layer)
                        mixer_output(layer)
            norm_statistics(LAST, 0, 0, [(x_lat, 0, T)])

            act.wait_ge(log_step, 1)
            nc.scalar.activation(log_steps[:, 1, :], log_steps[:, 0, :], ACT.Exp).then_inc(log_exp, 1)
            act.wait_ge(key_step, 1)
            nc.scalar.activation(key_decay[:], key_decay[:], ACT.Exp).then_inc(key_step, 1)
            act.wait_ge(ctx_ready, KD // 2)
            norm_statistics(LAST, 1, Y_FFN1, [(x_lat, 0, T), (x_ctx, T, C)])
            norm_high(LAST, 0, [(h_hi, 0, T), (h_ctx_hi, T, C)], lambda c, g: mod[:, g, c:c + 1])
            ffn(LAST, S_FFN1, 0, BOTH)
            norm_statistics(LAST, 2, Y_MIX2, [(x_lat, 0, T), (x_ctx, T, C)])
            norm_high(LAST, 1, [(h_hi, 0, T), (h_ctx_hi, T, C)], lambda c, g: mod[:, g, 3 * KD + c:3 * KD + c + 1])

            ropes = plain = 0
            for s in range(len(SLOTS_2)):
                outs = [o for o in OUTS_2 if o[0] == s]
                turn, pos = slot_of(LAST, S_MIX2 + s)
                for i, (_, kind, j, t, b) in enumerate(outs):
                    bank = psum[:, b, :]
                    if i == len(outs) - 1 or kind == "gates":
                        act.wait_ge(slot_used, turn * SLOTS + SLOTS + pos + 1)
                    else:
                        plain += 1
                        act.wait_ge(item_done_2, plain)
                    if kind in ROPED_2:
                        if ropes >= 2:
                            act.wait_ge(roped_2, ropes - 1)
                        last = nc.scalar.activation(squares[:, ropes % 2, 0:T], bank, ACT.Copy, scale=RET_DK ** -0.5 if kind == "rq" else 1.0)
                        ropes += 1
                    elif kind in ("gq", "gk"):
                        last = nc.scalar.activation((gq if kind == "gq" else gk)[:, j, :], bank, ACT.Copy, scale=GLA_DK ** -0.5 if kind == "gq" else 1.0)
                    elif kind in ("rg", "gg"):
                        last = nc.scalar.activation((rg if kind == "rg" else gg)[:, j, :], bank, ACT.Silu)
                    elif kind in ("gates", "gates_ctx"):
                        at = slice(0, T) if kind == "gates" else slice(T, TC)
                        act.wait_ge(roped_2, 2 * RET_H)
                        last = nc.scalar.activation(gate_in[:, at], bank[:, 0:at.stop - at.start], ACT.Copy)
                    else:
                        dst = {"rv": rv, "gv": gv, "rk_ctx": rk_ctx, "rv_ctx": rv_ctx, "gk_ctx": gk_ctx, "gv_ctx": gv_ctx}[kind]
                        n = dst.shape[2]
                        last = nc.scalar.activation(dst[:, t, :], bank[:, 0:n], ACT.Copy)
                    last.then_inc(copied_2, 1)
                turn, pos = slot_of(LAST, S_MIX2 + s + SLOTS)
                split(turn, pos)

            act.wait_ge(gate_neg, 1)
            nc.scalar.activation(gate_tmp[:], gate_tmp[:], ACT.Exp).then_inc(gate_log, 1)
            act.wait_ge(gate_log, 1)
            nc.scalar.activation(gate_tmp[:], gate_tmp[:], ACT.Ln, bias=1.0).then_inc(gate_log, 1)

            act.wait_ge(ret_consts_loaded, 32)
            act.wait_ge(log_gates_ready, 1)
            for h in range(RET_H):
                fwd, bwd = log_decay[:, 0, h:h + 1], log_decay[:, 1, h:h + 1]
                nc.scalar.activation(strip[:, h, 0:MID], distance[:, 0:MID], ACT.Exp, scale=bwd)
                nc.scalar.activation(strip[:, h, MID + P:STRIP], distance[:, MID + P:STRIP], ACT.Exp, scale=fwd)
                nc.scalar.activation(strip_mid[:, 0, h, :], distance[:, MID:MID + P], ACT.Exp, scale=fwd)
                nc.scalar.activation(strip_mid[:, 1, h, :], distance[:, MID:MID + P], ACT.Exp, scale=bwd).then_inc(strip_exp, 1)
            for way in range(2):
                act.wait_ge(ret_state_done, way + 1)
                nc.scalar.activation(ret_state[:, way], psum[:, way, :].rearrange("p (h e) -> p h e", h=RET_H), ACT.Copy).then_inc(ret_state_ready, 1)
            act.wait_ge(strip_ready, 1)
            for h in range(RET_H + 1):
                if h:
                    act.wait_ge(ret_o_done, h)
                if h < RET_H:
                    for way in range(2):
                        last = nc.scalar.activation(q_dec[:, way, :], row_pos[:, way, :], ACT.Exp, scale=log_decay[:, way, h:h + 1])
                    last.then_inc(q_exp_ready, 1)
                if h:
                    nc.scalar.activation(rq[:, h - 1, :], psum[:, 4 + (h - 1) % 2, :], ACT.Copy).then_inc(ret_o_ready, 1)

            nc.scalar.activation(q_twice[:], gq[:], ACT.Copy, scale=2.0)
            for p in range(PAIRS):
                act.wait_ge(gk_turned, p + 1)
                nc.scalar.activation(gk_rows[:, :, p * P:(p + 1) * P], psum[:, p, :].rearrange("p (t n) -> p t n", t=TT), ACT.Copy).then_inc(gk_rows_ready, 1)
            act.wait_ge(totals_done, 1)
            nc.scalar.activation(chunk_decay[:], psum[:, 2, 0:(TT + TCT) * PAIRS * 4].rearrange("p (n o) -> p n o", o=2), ACT.Exp,
                                 scale=1.0 / GLA_TAU).then_inc(totals_ready, 1)
            copies = 0

            def copy_states(t):
                nonlocal copies
                for way in range(2):
                    slot = state_slot(t, way)
                    if slot is None:
                        continue
                    copies += 1
                    act.wait_ge(state_done, copies)
                    for r in range(2):
                        rows = slice(GLA_DK * r, GLA_DK * (r + 1))
                        last = nc.scalar.activation(gla_state[rows, way, :, slot, :],
                                                    psum[rows, 6 + way, :].rearrange("p (q r e) -> p q r e", q=PAIRS, r=2)[:, :, r, :], ACT.Copy)
                    last.then_inc(state_copied, 1)

            for t in range(TT + TCT):
                act.wait_ge(suffix_done, t + 1)
                if t >= 2:
                    act.wait_ge(state_done, states_before(t - 1))
                nc.scalar.activation(gk_dec[:, t % 2, :, :], psum[:, 4 + t % 2, :].rearrange("p (w n) -> p w n", w=2), ACT.Exp,
                                     scale=1.0 / GLA_TAU).then_inc(suffix_exp, 1)
                if t >= 1:
                    copy_states(t - 1)
            copy_states(TT + TCT - 1)

            def copy_gla(n, c, p):
                act.wait_ge(gla_o_done, n + 1)
                nc.scalar.activation(rk[:, 2 * p:2 * p + 2, c * P:(c + 1) * P], psum[:, 6:8, 0:P], ACT.Copy).then_inc(gla_o_ready, 1)

            for n, c, p in units():
                act.wait_ge(sums_done, n + 1)
                if n >= 2:
                    act.wait_ge(gla_o_done, n - 1)
                nc.scalar.activation(factors[:, n % 2].rearrange("p l n -> p (l n)"), psum[:, 0:4, :].rearrange("p b n -> p (b n)"), ACT.Exp,
                                     scale=1.0 / GLA_TAU).then_inc(factor_exp, 1)
                if n >= 1:
                    copy_gla(*units()[n - 1])
            copy_gla(*units()[UNITS - 1])

            for h in range(2 * RET_H + 2):
                if h < 2 * RET_H:
                    o = rq[:, h, :] if h < RET_H else rk[:, h - RET_H, :]
                    if h < RET_H:
                        act.wait_ge(centred, h + 1)
                    if h >= 2:
                        act.wait_ge(merge_sum, h - 1)
                    nc.scalar.activation(squares[:, h % 2, 0:T], o, ACT.Square).then_inc(merge_sq, 1)
                g = h - 1
                if 0 <= g < 2 * RET_H:
                    act.wait_ge(merge_sum, g + 1)
                    if g >= 2:
                        act.wait_ge(merge_normed, g - 1)
                    nc.scalar.activation(std_2[:, g % 2, :], psum[:, 2 + g % 2, :], ACT.Sqrt, bias=eps[:, 0:1], scale=1.0 / P).then_inc(merge_std, 1)
                g = h - 2
                if g >= 0:
                    act.wait_ge(merged, g + 1)
                    o = rq[:, g, :] if g < RET_H else rk[:, g - RET_H, :]
                    nc.scalar.activation(h_hi[:, g, :], o, ACT.Copy).then_inc(merge_hi, 1)
            for c in range(KD):
                turn, pos = slot_of(LAST, S_MIX2 + len(SLOTS_2) + SLOTS + c)
                split(turn, pos)
            norm_statistics(LAST, 3, Y_FFN2, [(x_lat, 0, T)])
            norm_high(LAST, 2, [(h_hi, 0, T)], lambda c, g: mod[:, 0, 6 * KD + c:6 * KD + c + 1])
            ffn(LAST, S_FFN2, NF, LAT, last_ffn=True)
            norm_statistics(LAST, 4, Y_END, [(x_lat, 0, T)])
            for t in range(TT):
                act.wait_ge(out_turned, 2 * t + 2)
                if t >= 2:
                    act.wait_ge(stored[t % 2], 16)
                nc.scalar.activation(y_rows[:, t % 2, :].rearrange("p (b n) -> p b n", b=2),
                                     psum[:, 2 + 2 * (t % 2):4 + 2 * (t % 2), :], ACT.Copy).then_inc(y_rows_ready, 1)

        @block.vector
        def _(dve):
            dve.wait_ge(consts_loaded, CONSTS * 16)
            nc.vector.tensor_copy(ident_b[:], ident[:])
            nc.vector.tensor_copy(causal_b[:], causal[:])
            for i in range(SLOTS):
                nc.vector.memset(w_hi[:, i, :].bitcast(F32), 0.0).then_inc(slot_used, 1)
            for half in (cond_hi, cond_lo):
                nc.vector.memset(half[:, 2 * KD:].bitcast(F32), 0.0)
            for i in range(2):
                for n, free in enumerate((copied, aux_used, turn_read, aux_used, sq_used, gated_ready, a_lo_ready, h_lo_ready)):
                    nc.vector.memset(credits[:, 2 * n + i:2 * n + i + 1], 0.0).then_inc(free.sem, 1)
            nc.vector.memset(eps[:], EPS).then_inc(eps_set, 1)
            for c in range(KD):
                dve.wait_ge(x_turned, c + 1)
                nc.vector.tensor_copy(x_lat[:, c, :], psum[:, c, :]).then_inc(x_updated.sem, 1)
            dve.wait_ge(gains_turned, 1)
            nc.vector.tensor_copy(gains_2[:], psum[:, 7, P + N_MOD * KD:2 * P])
            for g in range(2):
                nc.vector.tensor_copy(mod[:, g, :], psum[:, 7, P:P + N_MOD * KD])
            nc.vector.tensor_copy(gains[:, 0:70], psum[:, 7, 0:70]).then_inc(gains_ready, 1)
            dve.wait_ge(gains_ready, 1)
            dve.wait_ge(cond_step, 2)
            nc.vector.tensor_tensor(cond_lo[:, 0:2 * KD], cond[:].rearrange("p c g -> p (c g)"), cond_hi[:, 0:2 * KD].bitcast(F32), ALU.subtract).then_inc(cond_ready, 1)

            def norm_apply(layer, v, gain, xs, u=None, shift=None):
                u = v if u is None else u
                dve.wait_ge(*std_ready(layer, v + 1))
                width = sum(n for _, _, n, _, _ in xs)
                nc.vector.reciprocal(rstd[:, 0:width], rstd[:, 0:width]).then_inc(rstd_ready.sem, 1)
                dve.wait_ge(*rstd_ready(layer, v + 1))

                def low(c):
                    dve.wait_ge(*h_hi_ready(layer, u * KD + c + 1))
                    for g, (_, o, n, hi, lo) in enumerate(xs):
                        if shift is None:
                            last = nc.vector.tensor_tensor(lo[:, c, :], normed[:, c % 2, o:o + n],
                                                           hi[:, c, :].bitcast(F32), ALU.subtract)
                        else:
                            last = nc.vector.scalar_tensor_tensor(lo[:, c, :], normed[:, c % 2, o:o + n], shift(c, g),
                                                                  hi[:, c, :].bitcast(F32), ALU.add, ALU.subtract)
                    last.then_inc(h_lo_ready.sem, 1)

                for c in range(KD):
                    dve.wait_ge(*h_lo_ready(layer, u * KD + c - 1))
                    for g, (x, o, n, _, _) in enumerate(xs):
                        last = nc.vector.scalar_tensor_tensor(normed[:, c % 2, o:o + n], x[:, c, :], gain(c, g),
                                                              rstd[:, o:o + n], ALU.mult, ALU.mult)
                    last.then_inc(normed_ready.sem, 1)
                    if c >= 1:
                        low(c - 1)
                low(KD - 1)

            def ffn(layer, s, f, y, groups, gate_scale):
                width = groups[-1][0] + groups[-1][2]
                for f0, nf in PARTS:
                    with dve.Fori(0, nf // 2) as it:
                        for i in range(2):
                            tile = it * 2 + (f + f0 + i)
                            dve.wait_ge(*silu_done(layer, tile + 1))
                            dve.wait_ge(*a_lo_ready(layer, tile - 1))
                            for g, (o, _, n) in enumerate(groups):
                                up = psum[:, 3 * i + 1, 0:n] if g == 0 else psum[:, 3 * i + 2, n:2 * n]
                                last = nc.vector.tensor_tensor(gated[:, i, o:o + n], silu_g[:, i, o:o + n], up, ALU.mult)
                            last.then_inc(gated_ready.sem, 1)
                            dve.wait_ge(*a_hi_ready(layer, tile + 1))
                            nc.vector.tensor_tensor(a_lo[:, bass.ds(it * 2 + i, 1), 0:width], gated[:, i:i + 1, 0:width],
                                                    a_hi[:, bass.ds(it * 2 + i, 1), 0:width].bitcast(F32),
                                                    ALU.subtract).then_inc(a_lo_ready.sem, 1)
                    s += 2 * nf
                    for c in range(KD):
                        turn, pos = slot_of(layer, s + c)
                        dve.wait_ge(slot_used, turn * SLOTS + (SLOTS + pos + 1))
                        for g, (o, x, n) in enumerate(groups):
                            acc = psum[:, 6 + c % 2, 0:n] if g == 0 else psum[:, 2 + 3 * (c % 2), 0:n]
                            last = nc.vector.scalar_tensor_tensor(x_lat[:, c, :] if g == 0 else x_ctx[:, c, :], acc,
                                                                  gate_scale(c, g), x_lat[:, c, :] if g == 0 else x_ctx[:, c, :],
                                                                  ALU.mult, ALU.add)
                        last.then_inc(x_updated.sem, 1)
                    s += KD
                    y += KD

            def mixer_projections(layer):
                events, ropes, aux_v = 0, 0, 0

                def roped_tile(x, rows, dsts):
                    nonlocal events, ropes
                    r0, n, dim = rows
                    dve.wait_ge(*rotated(layer, ropes + 1))
                    if ropes:
                        dve.wait_ge(*roped(layer, ropes))
                    else:
                        dve.wait_ge(*latent_lo_ready(layer, 3))
                    nc.vector.tensor_tensor(normed[r0:r0 + n, 0, 0:T], x, rope[r0:r0 + n, dim, :], ALU.mult)
                    nc.vector.tensor_tensor(normed[r0:r0 + n, 1, 0:T], psum[r0:r0 + n, 2 + events % 2, :], rope[r0:r0 + n, dim + 1, :],
                                            ALU.mult).then_inc(turn_read.sem, 1)
                    events += 1
                    dve.wait_ge(*turn_read(layer, events))
                    for dst in dsts:
                        last = nc.vector.tensor_tensor(dst, normed[r0:r0 + n, 0, 0:T], normed[r0:r0 + n, 1, 0:T], ALU.add)
                    last.then_inc(roped.sem, 1)
                    ropes += 1

                def block_taps(v):
                    if v == 0:
                        dve.wait_ge(*roped(layer, 2))
                        dve.wait_ge(*pos_ready(layer, 1))
                    else:
                        dve.wait_ge(*copied(layer, 6))
                        dve.wait_ge(*aux_used(layer, AUX_V))
                    for b in range(CMP_BLOCK // CMP_STRIDE):
                        at = slice(b * CMP_STRIDE, (b + 1) * CMP_STRIDE)
                        last = nc.vector.tensor_tensor(
                            taps[:, at, :].rearrange("p j n -> p n j"),
                            tok_cmp[:, v, b * CMP_STRIDE:(b + NC) * CMP_STRIDE].rearrange("p (n j) -> p n j", j=CMP_STRIDE),
                            pos_cols[:, v * CMP_BLOCK + b * CMP_STRIDE:v * CMP_BLOCK + (b + 1) * CMP_STRIDE].rearrange("p (o j) -> p o j", o=1)
                            .broadcast_to([P, NC, CMP_STRIDE]), ALU.add)
                    last.then_inc(taps_ready.sem, 1)

                nc.vector.memset(v_cmp[:], 0.0).then_inc(cmp_zeroed.sem, 1)
                dve.wait_ge(*params_loaded(layer, PARAMS * 16))
                pairs = lam_rows[:].rearrange("p (a b d) -> p a b d", a=2, b=2)
                products = diff_half[:].rearrange("p (a d) -> p a d", a=2)
                nc.vector.tensor_tensor(products, pairs[:, :, 0, :], pairs[:, :, 1, :], ALU.mult).then_inc(lam_step.sem, 1)
                dve.wait_ge(*lam_step(layer, 1))
                nc.vector.tensor_reduce(lam_stats[:, 0:2], products, AX_X, ALU.add).then_inc(lam_step.sem, 1)
                dve.wait_ge(*lam_step(layer, 2))
                nc.vector.tensor_scalar(diff_gain[:], diff_gain[:], lam_layer[:, 1:2], None, ALU.mult).then_inc(lam_step.sem, 1)
                dve.wait_ge(*pos_turned(layer, 1))
                nc.vector.tensor_copy(pos_cols[:], psum[:, 7, 0:2 * CMP_BLOCK]).then_inc(pos_ready.sem, 1)

                root_kv = squares[:, 0, 0:T]
                for n, root in enumerate((rstd[:, 0:T], root_kv)):
                    dve.wait_ge(*latent_std(layer, n + 1))
                    nc.vector.reciprocal(root, root).then_inc(turn_read.sem, 1)
                    events += 1
                dve.wait_ge(*turn_read(layer, 2))

                def latent_low(c):
                    dve.wait_ge(*latent_hi_ready(layer, c + 1))
                    nc.vector.tensor_tensor(latents_lo[:, c, :], normed[:, c % 2, 0:T], latents_hi[:, c, :].bitcast(F32),
                                            ALU.subtract).then_inc(latent_lo_ready.sem, 1)

                for c in range(3):
                    if c == 2:
                        latent_low(0)
                        dve.wait_ge(*latent_lo_ready(layer, 1))
                    nc.vector.scalar_tensor_tensor(normed[:, c % 2, 0:T], latents[:, c, :], layer_gains[:, GAIN_Q + c:GAIN_Q + c + 1],
                                                   rstd[:, 0:T] if c < 2 else root_kv, ALU.mult, ALU.mult).then_inc(latent_normed.sem, 1)
                latent_low(1)
                latent_low(2)
                dve.wait_ge(*lam_exp(layer, 1))
                nc.vector.scalar_tensor_tensor(lam_stats[:, 4:5], lam_stats[:, 3:4], lam_layer[:, 0:1], lam_stats[:, 2:3],
                                               ALU.subtract, ALU.subtract).then_inc(lam_step.sem, 1)

                places = {"nq": lambda j: q_nsa[:, j, :], "ks": lambda j: k_slc[:], "kw": lambda j: k_win[:],
                          "dq": lambda j: q_diff[:, j, :], "dk": lambda j: k_diff[:, j, :], "ck": lambda j: tok_cmp[:, 0, :]}
                for s, (kind, _, place) in enumerate(TILES):
                    if s == VALUES_AT:
                        block_taps(1)
                    if kind == "kr":
                        roped_tile(rope_in[0:MLA_ROPE, ropes % 2, :], (0, MLA_ROPE, 0), [k_mla[MLA_NOPE:MLA_QK, h, :] for h in range(MLA_H)])
                    elif kind in ROPED:
                        roped_tile(rope_in[:, ropes % 2, :], (0, P, 0 if kind in ("dq", "dk") else 2), [places[kind](place)])
                    if kind == "ck":
                        block_taps(0)
                dve.wait_ge(*gates_turned_1(layer, 1))
                nc.vector.tensor_tensor(gates[:], psum[:, 2 + events % 2, :].rearrange("p (t n) -> p t n", t=TT)[:, :, GATE_AT:P],
                                        gate_bias[:].rearrange("p (o n) -> p o n", o=1).broadcast_to([P, TT, 3 * NSA_H]),
                                        ALU.add).then_inc(turn_read.sem, 1)
                events += 1
                for h in range(MLA_H):
                    x = q_mla[MLA_NOPE:MLA_QK, h, :]
                    roped_tile(x, (MLA_NOPE, MLA_ROPE, 0), [x])
                dve.wait_ge(*gate_exp(layer, 1))
                nc.vector.tensor_scalar(gates[:], gates[:], 1.0, None, ALU.add).then_inc(gate_step.sem, 1)
                dve.wait_ge(*gate_step(layer, 1))
                nc.vector.reciprocal(gates[:], gates[:]).then_inc(gate_step.sem, 1)

            def cmp_softmax(layer, i):
                n = 2 + 7 * i
                scores = cmp_p[:, :, 0:NC]

                def wide(x):
                    return x.rearrange("p (h o) -> p h o", o=1).broadcast_to([P, NSA_H, NC])

                dve.wait_ge(*cmp_scores_done(layer, i + 1))
                if i:
                    dve.wait_ge(*cmp_turned(layer, i))
                for g in range(NSA_G):
                    last = nc.vector.tensor_tensor(scores[:, 4 * g:4 * g + 4, :], psum[:, 6 + g, 0:4 * CMP_BLOCK].rearrange("p (h n) -> p h n", h=4)[:, :, 0:NC],
                                                   cmp_mask[:, i, :].rearrange("p (o n) -> p o n", o=1).broadcast_to([P, 4, NC]), ALU.add)
                last.then_inc(cmp_step.sem, 1)
                dve.wait_ge(*cmp_step(layer, n + 1))
                nc.vector.tensor_reduce(cmp_stats[:, 0, :], scores, AX_X, ALU.max).then_inc(cmp_step.sem, 1)
                dve.wait_ge(*cmp_step(layer, n + 2))
                nc.vector.tensor_tensor(scores, scores, wide(cmp_stats[:, 0, :]), ALU.subtract).then_inc(cmp_step.sem, 1)

            def cmp_sums(layer, i):
                n = 2 + 7 * i
                dve.wait_ge(*cmp_exp(layer, i + 1))
                nc.vector.tensor_reduce(cmp_stats[:, 1, :], cmp_p[:, :, 0:NC], AX_X, ALU.add).then_inc(cmp_step.sem, 1)
                dve.wait_ge(*cmp_step(layer, n + 4))
                nc.vector.reciprocal(cmp_stats[:, 1, :], cmp_stats[:, 1, :]).then_inc(cmp_step.sem, 1)
                dve.wait_ge(*cmp_step(layer, n + 5))
                nc.vector.tensor_tensor(cmp_stats[:, 2, :], cmp_stats[:, 1, :],
                                        gates[:, i, :].rearrange("p (h b) -> p h b", b=3)[:, :, 0], ALU.mult).then_inc(cmp_step.sem, 1)
                dve.wait_ge(*cmp_step(layer, n + 6))
                nc.vector.tensor_scalar(cmp_stats[:, 2, :], cmp_stats[:, 2, :], cmp_any[:, 0:1] if i == 0 else 1.0, None,
                                        ALU.mult).then_inc(cmp_step.sem, 1)
                dve.wait_ge(*cmp_turned(layer, i + 1))
                if i:
                    dve.wait_ge(*cmp_o_done(layer, i))
                nc.vector.tensor_copy(cmp_pt[:], psum[:, 7, 0:2 * P].rearrange("p (g q) -> p g q", g=2)).then_inc(cmp_pt_ready.sem, 1)

            def cmp_output(layer, i):
                dve.wait_ge(*cmp_o_done(layer, i + 1))
                dve.wait_ge(*cmp_step(layer, 2 + 7 * i + 7))
                if i >= 2:
                    dve.wait_ge(*o_turned(layer, 2 * (i - 1)))
                nc.vector.tensor_tensor(o_rows[:, i % 2, 2 * 256:].rearrange("p (h d) -> p h d", h=NSA_H),
                                        psum[:, 6, :].rearrange("p (h d) -> p h d", h=NSA_H),
                                        cmp_stats[:, 2, :].rearrange("p (h o) -> p h o", o=1).broadcast_to([P, NSA_H, DV]),
                                        ALU.mult).then_inc(cmp_o_ready.sem, 1)

            def diff_norm(layer, i, half):
                o = o_rows[:, i % 2, 256:512].rearrange("p (h d) -> p h d", h=DIFF_H)

                def wide(x):
                    return x.rearrange("p (h o) -> p h o", o=1).broadcast_to([P, DIFF_H, DV])

                if half == 0:
                    dve.wait_ge(*o_ready(layer, i * NH + MLA_H + 2 * DIFF_H))
                    nc.vector.tensor_tensor(diff_sq[:], o, o, ALU.mult).then_inc(diff_step.sem, 1)
                    dve.wait_ge(*diff_step(layer, 4 * i + 1))
                    nc.vector.tensor_reduce(diff_stats[:], diff_sq[:], AX_X, ALU.add).then_inc(diff_step.sem, 1)
                else:
                    dve.wait_ge(*diff_std(layer, i + 1))
                    nc.vector.reciprocal(diff_stats[:], diff_stats[:]).then_inc(diff_step.sem, 1)
                    dve.wait_ge(*diff_step(layer, 4 * i + 3))
                    nc.vector.tensor_tensor(o, o, wide(diff_stats[:]), ALU.mult).then_inc(diff_step.sem, 1)
                    dve.wait_ge(*diff_step(layer, 4 * i + 4))
                    nc.vector.tensor_tensor(o, o, diff_gain[:].rearrange("p (o d) -> p o d", o=1).broadcast_to([P, DIFF_H, DV]),
                                            ALU.mult).then_inc(diff_ready.sem, 1)

            def turn_o(layer, i):
                for b in range(2):
                    dve.wait_ge(*o_hi_ready(layer, 2 * i + b + 1))
                    at = slice(i * P, (i + 1) * P)
                    nc.vector.tensor_tensor(h_lo[:, 4 * b:4 * b + 4, at], psum[:, 6 + b, :].rearrange("p (c q) -> p c q", c=4),
                                            h_hi[:, 4 * b:4 * b + 4, at].bitcast(F32), ALU.subtract).then_inc(o_lo_ready.sem, 1)

            def attention(layer):
                scaled = 0

                def head_output(p):
                    nonlocal scaled
                    i, (kind, h, m) = p // NH, HEADS[p % NH]
                    dve.wait_ge(*o_done(layer, p + 1))
                    beside = psum[:, 4 + p % 2, DV:DV + 2 * P]
                    if p in ADA_AT:
                        nc.vector.tensor_copy(mod_rows[:], beside[0:COND_M, :])
                    if p - 2 in ADA_AT:
                        at = bass.ds(layer * ADA_SLOTS + 2 * ADA_AT[p - 2], 2)
                        nc.vector.tensor_tensor(mod[:, :, at], beside.rearrange("p (a g) -> p g a", a=2)[:, 0:2, :], mod[:, :, at], ALU.add)
                    nc.vector.reciprocal(exp_sum[:, p:p + 1], exp_sum[:, p:p + 1]).then_inc(inv_ready.sem, 1)
                    dve.wait_ge(*inv_ready(layer, p + 1))
                    o = psum[:, 4 + p % 2, 0:DV]
                    factor = exp_sum[:, p:p + 1]
                    if kind in ("slc", "win") or m == 1:
                        by = lam_stats[:, 4:5] if m else gates[:, i, 3 * h + (1 if kind == "slc" else 2):3 * h + (2 if kind == "slc" else 3)]
                        factor = scaled_inv[:, p:p + 1]
                        nc.vector.tensor_tensor(factor, exp_sum[:, p:p + 1], by, ALU.mult).then_inc(scaled_ready.sem, 1)
                        scaled += 1
                        dve.wait_ge(*scaled_ready(layer, scaled))
                    at = {"mla": 0, "diff": 256, "slc": 512, "win": 512}[kind] + DV * h
                    dst = o_rows[:, i % 2, at:at + DV]
                    if kind == "mla" or (kind == "diff" and m == 0):
                        if i >= 2 and p % NH == 0:
                            dve.wait_ge(*o_turned(layer, 2 * (i - 1)))
                        if kind == "diff" and p % NH > MLA_H:
                            dve.wait_ge(*o_ready(layer, p))
                        nc.vector.tensor_scalar(dst if kind == "mla" else diff_half[:], o, factor, None, ALU.mult).then_inc(o_ready.sem, 1)
                    else:
                        if kind == "slc":
                            dve.wait_ge(*cmp_o_ready(layer, i + 1))
                        else:
                            dve.wait_ge(*o_ready(layer, p if m else p - NSA_H + 1))
                        nc.vector.scalar_tensor_tensor(dst, o, factor, diff_half[:] if m else dst, ALU.mult, ALU.add).then_inc(o_ready.sem, 1)

                nc.vector.memset(cmp_p[:], 0.0).then_inc(cmp_step.sem, 1)
                dve.wait_ge(*cmp_step(layer, 1))
                nc.vector.memset(cmp_stats[:], 0.0).then_inc(cmp_step.sem, 1)
                dve.wait_ge(*cmp_step(layer, 2))
                for t in range(ATT + 2):
                    i, step = t // NH, t % NH
                    if t < ATT:
                        dve.wait_ge(*scores_done(layer, t + 1))
                        nc.vector.tensor_reduce(neg_max[:, t:t + 1], psum[:, t % 2, 0:(i + 1) * P], AX_X, ALU.max,
                                                negate=True).then_inc(max_ready.sem, 1)
                    p = t - 1
                    if 1 <= p < ATT and p % 2 == 1:
                        dve.wait_ge(*probs_turned(layer, p + 1))
                        if p >= 2:
                            dve.wait_ge(*o_done(layer, p - 1))
                        n = (p // NH + 1) * P
                        nc.vector.tensor_copy(probs_t[:, 1, 0:n], psum[:, 3, 0:n]).then_inc(probs_t_dve.sem, 1)
                    if t >= 2:
                        head_output(t - 2)
                    if t < ATT:
                        if step == AT_TURN + 2 and i > 0:
                            turn_o(layer, i - 1)
                        if step == AT_CMP + 1:
                            cmp_softmax(layer, i)
                        if step == AT_CMP + 5:
                            cmp_sums(layer, i)
                        if step == AT_CMP + 7:
                            cmp_output(layer, i)
                        if step == AT_DIFF:
                            diff_norm(layer, i, 0)
                        if step == AT_DIFF + 4:
                            diff_norm(layer, i, 1)
                turn_o(layer, TT - 1)

            def mixer_output(layer):
                for c in range(KD):
                    turn, pos = slot_of(layer, OUT_S0 + c)
                    dve.wait_ge(slot_used, turn * SLOTS + (SLOTS + pos + 1))
                    nc.vector.tensor_tensor(x_lat[:, c, :], psum[:, 6 + c % 2, :], x_lat[:, c, :], ALU.add).then_inc(x_updated.sem, 1)

            with dve.Fori(0, DEPTH) as layer:
                nc.vector.tensor_copy(lam_layer[:], lam_consts[:, bass.ds(layer * 2, 2)])
                nc.vector.tensor_copy(layer_gains[:], gains[:, bass.ds(layer * 31, 31)]).then_inc(layer_gains_ready.sem, 1)
                dve.wait_ge(*layer_gains_ready(layer, 1))
                for j in range(2):
                    norm_apply(layer, FFN_V[j], lambda c, g: layer_gains[:, KD * j + c:KD * j + c + 1],
                               [(x_lat, 0, T, h_hi, h_lo)])
                    ffn(layer, FFN_S0[j], FFN_N0[j], FFN_Y0[j], LAT, lambda c, g: 0.5)
                    if j == 0:
                        norm_apply(layer, 1, lambda c, g: layer_gains[:, GAIN_MIX + c:GAIN_MIX + c + 1], [(x_lat, 0, T, h_hi, h_lo)])
                        mixer_projections(layer)
                        attention(layer)
                        mixer_output(layer)

            def final_norm(v, gain):
                dve.wait_ge(*std_ready(LAST, v + 1))
                nc.vector.reciprocal(rstd[:, 0:T], rstd[:, 0:T]).then_inc(rstd_ready.sem, 1)
                dve.wait_ge(*rstd_ready(LAST, v + 1))
                for c in range(KD):
                    nc.vector.scalar_tensor_tensor(x_lat[:, c, :], x_lat[:, c, :], gain(c), rstd[:, 0:T], ALU.mult, ALU.mult).then_inc(x_updated.sem, 1)

            final_norm(0, lambda c: gains[:, 31 * DEPTH + c:31 * DEPTH + c + 1])

            flat = decay[:].rearrange("p w h -> p (w h)")
            lg = log_decay[:].rearrange("p w h -> p (w h)")
            a0, u, s, s2 = (log_steps[:, i, :] for i in range(4))
            nc.vector.scalar_tensor_tensor(a0, flat, -1.0, flat, ALU.mult, ALU.min).then_inc(log_step, 1)
            steps = 1

            def next_step(op):
                nonlocal steps
                op.then_inc(log_step, 1)
                steps += 1
                dve.wait_ge(log_step, steps)

            dve.wait_ge(log_exp, 1)
            next_step(nc.vector.tensor_scalar(s, u, 2.0, None, ALU.add))
            next_step(nc.vector.reciprocal(s, s))
            next_step(nc.vector.tensor_tensor(s, s, u, ALU.mult))
            next_step(nc.vector.tensor_tensor(s2, s, s, ALU.mult))
            next_step(nc.vector.tensor_scalar(a0, s2, 1.0 / 17.0, None, ALU.mult))
            for k in range(15, 1, -2):
                next_step(nc.vector.scalar_tensor_tensor(a0, a0, 1.0 / k, s2, ALU.add, ALU.mult))
            next_step(nc.vector.scalar_tensor_tensor(a0, a0, 1.0, s, ALU.add, ALU.mult))
            next_step(nc.vector.tensor_scalar(a0, a0, -2.0, None, ALU.mult))
            next_step(nc.vector.scalar_tensor_tensor(lg, flat, 0.0, a0, ALU.min, ALU.add))
            for n in range(3):
                nc.vector.scalar_tensor_tensor(mod_gain[:, n], mod[:, :, (3 * n + 1) * KD:(3 * n + 2) * KD].rearrange("p g c -> p c g"), 1.0,
                                               gains_2[:, ROW_NORM + n * KD:ROW_NORM + (n + 1) * KD].rearrange("p (c o) -> p c o", o=1).broadcast_to([P, KD, 2]),
                                               ALU.add, ALU.mult)
                last = nc.vector.tensor_scalar(res[:, n], mod[:, :, (3 * n + 2) * KD:(3 * n + 3) * KD].rearrange("p g c -> p c g"), 1.0 if n == 1 else 0.5, None, ALU.mult)
            last.then_inc(mod_done, 1)
            dve.wait_ge(block2_loaded, 32)
            nc.vector.tensor_tensor(key_decay[:], key_pos[:].rearrange("p w (t o) -> p w t o", o=1).broadcast_to([P, 2, TCT, RET_H]),
                                    log_decay[:].rearrange("p w (o h) -> p w o h", o=1).broadcast_to([P, 2, TCT, RET_H]), ALU.mult).then_inc(key_step, 1)
            for b in range(KD // 2):
                dve.wait_ge(ctx_turned, b + 1)
                nc.vector.tensor_copy(x_ctx[:, 2 * b:2 * b + 2, :], psum[:, 2 + b, :].rearrange("p (c n) -> p c n", c=2)).then_inc(ctx_ready, 1)
            dve.wait_ge(mod_done, 1)
            both = [(x_lat, 0, T, h_hi, h_lo), (x_ctx, T, C, h_ctx_hi, h_ctx_lo)]
            norm_apply(LAST, 1, lambda c, g: mod_gain[:, 0, c, g:g + 1], both, 0, lambda c, g: mod[:, g, c:c + 1])
            ffn(LAST, S_FFN1, 0, Y_FFN1, BOTH, lambda c, g: res[:, 0, c, g:g + 1])
            norm_apply(LAST, 2, lambda c, g: mod_gain[:, 1, c, g:g + 1], both, 1, lambda c, g: mod[:, g, 3 * KD + c:3 * KD + c + 1])

            for r in range(2 * RET_H):
                dve.wait_ge(rotated_2, r + 1)
                if r:
                    dve.wait_ge(roped_2, r)
                nc.vector.tensor_tensor(normed[:, 0, 0:T], squares[:, r % 2, 0:T], grid[:, 0, :], ALU.mult)
                nc.vector.tensor_tensor(normed[:, 1, 0:T], psum[:, 4 + r % 2, :], grid[:, 1, :], ALU.mult).then_inc(rot_read_2, 1)
                dve.wait_ge(rot_read_2, r + 1)
                dst = rk if r < RET_H else rq
                nc.vector.tensor_tensor(dst[:, r % RET_H, :], normed[:, 0, 0:T], normed[:, 1, 0:T], ALU.add).then_inc(roped_2, 1)
            dve.wait_ge(copied_2, N_2)
            nc.vector.memset(gate_w[:], 0.0).then_inc(gate_w_zeroed, 1)

            for t in range(TT + TCT):
                dve.wait_ge(gate_done, t + 1)
                nc.vector.tensor_tensor(log_gates[:, t, :], psum[:, 6 + t % 2, :], gate_b[:], ALU.add).then_inc(gate_read, 1)
            dve.wait_ge(gate_read, TT + TCT)
            nc.vector.scalar_tensor_tensor(gate_tmp[:], log_gates[:], -1.0, log_gates[:], ALU.mult, ALU.min).then_inc(gate_neg, 1)
            dve.wait_ge(gate_log, 2)
            nc.vector.scalar_tensor_tensor(log_gates[:], log_gates[:], 0.0, gate_tmp[:], ALU.min, ALU.subtract).then_inc(log_gates_ready, 1)

            dve.wait_ge(key_step, 2)
            for way in range(2):
                for t in range(TCT):
                    last = nc.vector.tensor_tensor(ctx_keys[:, way, t, :].rearrange("p (h d) -> p h d", h=RET_H),
                                                   rk_ctx[:, t, :].rearrange("p (h d) -> p h d", h=RET_H),
                                                   key_decay[:, way, t, :].rearrange("p (h o) -> p h o", o=1).broadcast_to([P, RET_H, RET_DK]), ALU.mult)
            last.then_inc(ctx_keys_ready, 1)
            dve.wait_ge(strip_exp, RET_H)
            for way in range(2):
                side = distance[:, STRIP + way * P:STRIP + (way + 1) * P].rearrange("p (o n) -> p o n", o=1).broadcast_to([P, RET_H, P])
                last = nc.vector.tensor_tensor(strip_mid[:, way], strip_mid[:, way], side, ALU.mult)
            last.then_inc(strip_step, 1)
            dve.wait_ge(strip_step, 1)
            nc.vector.tensor_tensor(strip[:, :, MID:MID + P], strip_mid[:, 0], strip_mid[:, 1], ALU.add).then_inc(strip_ready, 1)
            dve.wait_ge(strip_ready, 1)
            dve.wait_ge(ret_state_done, 2)
            for h in range(RET_H):
                if h:
                    dve.wait_ge(ret_o_done, h)
                for t in range(TT):
                    dve.wait_ge(ret_scores_done, h * TT + t + 1)
                    nc.vector.tensor_tensor(scores_r[:, t, :], psum[:, t, :], strip[:, h, MID - t * P:MID - t * P + T], ALU.mult).then_inc(ret_scores_ready, 1)
                dve.wait_ge(q_exp_ready, h + 1)
                nc.vector.tensor_tensor(q_dec[:], q_dec[:], rq[:, h:h + 1, :].broadcast_to([P, 2, T]), ALU.mult).then_inc(q_dec_ready, 1)

            for t in range(TT + TCT):
                dve.wait_ge(suffix_exp, t + 1)
                if t == TCT:
                    dve.wait_ge(gk_rows_ready, PAIRS)
                keys = gk_ctx[:, t:t + 1, :] if t < TCT else gk_rows[:, t - TCT:t - TCT + 1, :]
                nc.vector.tensor_tensor(gk_dec[:, t % 2], gk_dec[:, t % 2], keys.broadcast_to([P, 2, 2 * P]), ALU.mult).then_inc(gk_dec_ready, 1)
            dve.wait_ge(totals_ready, 1)
            dve.wait_ge(state_copied, states_before(TT + TCT))
            for i in range(1, STATES):
                if i > 1:
                    dve.wait_ge(state_step, i - 1)
                for way in range(2):
                    t = [t for t in range(TT + TCT) if state_slot(t, way) == i]
                    for p in range(PAIRS):
                        d = (t[0] * 2 + way) * PAIRS + p
                        last = nc.vector.scalar_tensor_tensor(gla_state[:, way, p, i, :], gla_state[:, way, p, i - 1, :], chunk_decay[:, d, 0:1],
                                                              gla_state[:, way, p, i, :], ALU.mult, ALU.add)
                last.then_inc(state_step, 1)
            dve.wait_ge(gla_consts_loaded, 32)
            merges = 0

            def gla_factors(n, c, p):
                dve.wait_ge(factor_exp, n + 1)
                at = slice(c * P, (c + 1) * P)
                q = gq[:, p:p + 1, at]
                f = factors[:, n % 2]
                nc.vector.tensor_tensor(f[:, 0:LEVELS + 1, :], f[:, 0:LEVELS + 1, :], q.broadcast_to([P, LEVELS + 1, P]), ALU.mult)
                nc.vector.tensor_tensor(f[:, 2 * LEVELS + 1, :], f[:, 2 * LEVELS + 1, :], gq[:, p, at], ALU.mult)
                nc.vector.tensor_tensor(f[:, LEVELS + 1:2 * LEVELS + 1, :], f[:, LEVELS + 1:2 * LEVELS + 1, :],
                                        gk[:, p:p + 1, at].broadcast_to([P, LEVELS, P]), ALU.mult).then_inc(factors_ready, 1)

            def gla_merge(n):
                nonlocal merges
                for level in range(LEVELS + 1):
                    if level % 4 == 0:
                        dve.wait_ge(gla_scores_done, 2 * n + level // 4 + 1)
                    if level == 0 and n >= 2:
                        dve.wait_ge(gla_o_done, n - 1)
                    if merges:
                        dve.wait_ge(gla_scores_step, merges)
                    nc.vector.copy_predicated(scores_g[:, n % 2], masks[:, level:level + 1, :].broadcast_to([P, 2, P]),
                                              psum[:, 4:6, level % 4 * P:(level % 4 + 1) * P]).then_inc(gla_scores_step, 1)
                    merges += 1

            for n, c, p in units():
                gla_factors(n, c, p)
                if n:
                    gla_merge(n - 1)
            gla_merge(UNITS - 1)

            def centre(h):
                dve.wait_ge(mean_done, h + 1)
                nc.vector.scalar_tensor_tensor(rq[:, h, :], psum[:, h % 2, :], -1.0 / P, rq[:, h, :], ALU.mult, ALU.add).then_inc(centred, 1)

            def merge_low(h):
                dve.wait_ge(merge_hi, h + 1)
                o = rq[:, h, :] if h < RET_H else rk[:, h - RET_H, :]
                nc.vector.tensor_tensor(h_lo[:, h, :], o, h_hi[:, h, :].bitcast(F32), ALU.subtract).then_inc(merge_lo, 1)

            centre(0)
            centre(1)
            for h in range(2 * RET_H):
                o = rq[:, h, :] if h < RET_H else rk[:, h - RET_H, :]
                dve.wait_ge(merge_std, h + 1)
                nc.vector.reciprocal(std_2[:, h % 2, :], std_2[:, h % 2, :]).then_inc(merge_inv, 1)
                dve.wait_ge(merge_inv, h + 1)
                nc.vector.scalar_tensor_tensor(normed[:, h % 2, 0:T], o, gains_2[:, ROW_RET + h:ROW_RET + h + 1], std_2[:, h % 2, :],
                                               ALU.mult, ALU.mult).then_inc(merge_normed, 1)
                dve.wait_ge(merge_normed, h + 1)
                nc.vector.tensor_tensor(o, normed[:, h % 2, 0:T], rg[:, h, :] if h < RET_H else gg[:, h - RET_H, :], ALU.mult).then_inc(merged, 1)
                if h + 2 < RET_H:
                    centre(h + 2)
                if h:
                    merge_low(h - 1)
            merge_low(2 * RET_H - 1)
            for c in range(KD):
                turn, pos = slot_of(LAST, S_MIX2 + len(SLOTS_2) + c)
                dve.wait_ge(slot_used, turn * SLOTS + (SLOTS + pos + 1))
                nc.vector.scalar_tensor_tensor(x_lat[:, c, :], psum[:, 6 + c % 2, :], res[:, 1, c, 0:1], x_lat[:, c, :], ALU.mult, ALU.add).then_inc(x_updated.sem, 1)
            norm_apply(LAST, 3, lambda c, g: mod_gain[:, 2, c, 0:1], [(x_lat, 0, T, h_hi, h_lo)], 2, lambda c, g: mod[:, 0, 6 * KD + c:6 * KD + c + 1])
            ffn(LAST, S_FFN2, NF, Y_FFN2, LAT, lambda c, g: res[:, 2, c, 0:1])
            final_norm(4, lambda c: gains_2[:, ROW_FINAL + c:ROW_FINAL + c + 1])

        @block.tensor
        def _(pe):
            pe.wait_ge(consts_loaded, CONSTS * 16)
            pe.wait_ge(x_rows_loaded, 16)
            for c in range(KD):
                for t in range(TT):
                    last = nc.tensor.transpose(psum[:, c, t * P:(t + 1) * P], x_rows[:, t, c * P:(c + 1) * P], ident[:])
                last.then_inc(x_turned, 1)
            pe.wait_ge(*x_updated(0, 0))
            nc.tensor.transpose(psum[:, 7, 0:70], gain_rows[0:70, :], ident[0:70, 0:70])
            nc.tensor.transpose(psum[:, 7, P:2 * P], gain_rows_2[:], ident[:]).then_inc(gains_turned, 1)

            def norm_sums(layer, v, widths):
                for c in range(KD):
                    pe.wait_ge(*sq_ready(layer, v * KD + c + 1))
                    for g, (o, n) in enumerate(widths):
                        last = nc.tensor.matmul(psum[:, g, 0:n], ones[:], squares[:, c % 2, o:o + n],
                                                start=c == 0, stop=c == KD - 1)
                    last.then_inc(sq_used.sem, 1)

            def dense(pos, k0, nk, rhs, outs, before=None):
                for k in range(nk):
                    if before is not None:
                        before(k)
                    for m, (w, r) in enumerate(((w_hi, 0), (w_hi, 1), (w_lo, 0))):
                        for g, dst in enumerate(outs):
                            last = nc.tensor.matmul(dst, w[:, pos, k * P:(k + 1) * P], rhs[g][r](k0 + k),
                                                    start=k == 0 and m == 0, stop=k == nk - 1 and m == 2)
                return last

            def ffn(layer, v, s, f, y, groups, rhs):
                for part, (f0, nf) in enumerate(PARTS):
                    turn, _ = slot_of(layer, s)
                    with pe.Fori(0, nf // 2) as it:
                        pe.wait_ge(*h_lo_ready(layer, v * KD + KD))
                        if len(groups) > 1:
                            pe.wait_ge(*x_updated(layer, y))
                        for i in range(2):
                            tile = it * 2 + (f + f0 + i)
                            pe.wait_ge(*gated_ready(layer, tile - 1))
                            for u in range(2):
                                pe.wait_ge(lo_ready, (turn + it) * SLOTS + (SLOTS + 2 * i + u + 1))
                                outs = [psum[:, 3 * i + u, 0:n] if g == 0 else psum[:, 3 * i + 2, u * n:u * n + n]
                                        for g, (_, _, n) in enumerate(groups)]
                                last = dense(2 * i + u, 0, KD, rhs, outs)
                                last.then_inc(slot_used, 1)
                    s += 2 * nf
                    turn, _ = slot_of(layer, s)
                    with pe.Fori(0, KD // SLOTS) as it:
                        if len(groups) > 1:
                            pe.wait_ge(*gated_ready(layer, f + f0 + nf))

                        def activations(k):
                            if k == 0 or k >= nf - 2:
                                pe.wait_ge(*a_lo_ready(layer, f + f0 + max(k, nf - 3) + 1))

                        for i in range(SLOTS):
                            pe.wait_ge(lo_ready, (turn + it) * SLOTS + (SLOTS + i + 1))
                            pe.wait_ge(*x_updated(layer, it * SLOTS + (y + i - 1)))
                            outs = [psum[:, 6 + i % 2, 0:n] if g == 0 else psum[:, 2 + 3 * (i % 2), 0:n]
                                    for g, (_, _, n) in enumerate(groups)]
                            last = dense(i, 0, nf, [tuple((lambda k, h=h, o=o, n=n: h[:, k, o:o + n]) for h in (a_hi, a_lo))
                                                    for o, _, n in groups], outs, activations if i == 0 else None)
                            last.then_inc(slot_used, 1)
                    s += KD
                    y += KD

            def mixer_projections(layer):
                turn0, _ = slot_of(layer, MIX_S0)
                events, ropes = 0, 0
                flat = squares[:].rearrange("p a n -> p (a n)")

                def weights(s):
                    pe.wait_ge(lo_ready, (turn0 + s // SLOTS) * SLOTS + (SLOTS + s % SLOTS + 1))

                def bank_of(n):
                    pe.wait_ge(*copied(layer, n - 1))
                    return psum[:, n % 2, :]

                def turn_bank():
                    nonlocal events
                    pe.wait_ge(*turn_read(layer, events - 1))
                    events += 1
                    return 2 + (events - 1) % 2

                def latent_sums(n):
                    pe.wait_ge(*latent_sq(layer, n + 1))
                    b = turn_bank()
                    chunks = ((0, 1), (2,))[n]
                    for c in chunks:
                        last = nc.tensor.matmul(psum[:, b, :], ones[:], flat[:, c * T:(c + 1) * T], start=c == chunks[0], stop=c == chunks[-1])
                    last.then_inc(latent_sum.sem, 1)

                def rotation(item, x, rows, m):
                    nonlocal ropes
                    pe.wait_ge(*copied(layer, item + 1))
                    b = turn_bank()
                    nc.tensor.matmul(psum[rows, b, :], rotate[rows, m, rows], x, start=True, stop=True).then_inc(rotated.sem, 1)
                    ropes += 1

                def rotate_tile(s):
                    kind = TILES[s][0]
                    rotation(s, rope_in[:, ropes % 2, :], slice(0, P), 0 if kind in ("kr", "dq", "dk") else 1)

                def compress(n):
                    v = n // AUX_V
                    pe.wait_ge(*aux_loaded[n % AUX_RING](layer, (n // AUX_RING + 1) * 32))
                    if n % AUX_V == 0:
                        pe.wait_ge(*taps_ready(layer, v + 1))
                        if v:
                            pe.wait_ge(*hid_ready(layer, 1))
                    for j in range(AUX_TAPS):
                        tap = n % AUX_V * AUX_TAPS + j
                        for half in range(2):
                            for g in range(2):
                                rows = slice(DV * g, DV * (g + 1))
                                w = aux[rows, n % AUX_RING, j * CMP_HID + half * P:j * CMP_HID + (half + 1) * P]
                                last = nc.tensor.matmul(psum[:, 4 + 2 * half + g, 0:NC], w, taps[rows, tap, :],
                                                        start=tap == 0, stop=tap == CMP_BLOCK - 1)
                    last.then_inc(aux_used.sem, 1)

                pe.wait_ge(*h_lo_ready(layer, 2 * KD))
                pe.wait_ge(*params_loaded(layer, PARAMS * 16))
                pe.wait_ge(*x_updated(layer, MIX_Y0))
                for s in range(N_T):
                    weights(s)
                    dense(s % SLOTS, 0, KD, [lat], [bank_of(s)]).then_inc(slot_used, 1)
                    if s == 0:
                        nc.tensor.transpose(psum[:, 7, 0:2 * CMP_BLOCK], pos_rows[:], ident[0:2 * CMP_BLOCK, 0:2 * CMP_BLOCK]).then_inc(pos_turned.sem, 1)
                    if s in (2, 3):
                        latent_sums(s - 2)
                    if s >= 1 and TILES[s - 1][0] in ROPED:
                        rotate_tile(s - 1)
                    for n in AUX_AT.get(s, ()):
                        if n == 0:
                            pe.wait_ge(*pos_ready(layer, 1))
                        compress(n)
                pe.wait_ge(*latent_lo_ready(layer, 3))
                halves3 = ((w_hi, latents_hi), (w_hi, latents_lo), (w_lo, latents_hi))
                for n in range(LATE_ITEMS):
                    s = N_T + n // 2 if n < MLA_H else ROW_S0 - 1
                    pos = s % SLOTS
                    if n in (0, 2, MLA_H):
                        weights(s)
                    bank = bank_of(N_T + n)
                    if n < MLA_H:
                        for k in range(2):
                            for m, (w, x) in enumerate(halves3):
                                at = k * 2 * MLA_QK + n % 2 * MLA_QK
                                last = nc.tensor.matmul(bank[0:MLA_QK, :], w[:, pos, at:at + MLA_QK], x[:, k, :],
                                                        start=k == 0 and m == 0, stop=k == 1 and m == 2)
                    elif n < 2 * MLA_H:
                        at = (n - MLA_H) * P
                        for m, (w, x) in enumerate(halves3):
                            last = nc.tensor.matmul(bank, w[:, pos, at:at + P], x[:, 2, :], start=m == 0, stop=m == 2)
                    else:
                        for t in range(2):
                            tok = slice((2 * (n - 2 * MLA_H) + t) * P, (2 * (n - 2 * MLA_H) + t + 1) * P)
                            for m, (w, x) in enumerate(halves3):
                                last = nc.tensor.matmul(bank[:, t * 256:(t + 1) * 256], x[:, 2, tok],
                                                        w[:, pos, 0:512].rearrange("p (h n) -> p h n", h=MLA_H)[:, :, MLA_NOPE:],
                                                        start=m == 0, stop=m == 2)
                    last.then_inc(slot_used if n in SLOT_ENDS else item_done.sem, 1)
                    if n == 0:
                        pe.wait_ge(*copied(layer, N_T))
                        b = turn_bank()
                        for t in range(TT):
                            last = nc.tensor.transpose(psum[:, b, t * P:(t + 1) * P], rope_in[:, ropes % 2, t * P:(t + 1) * P], ident[:])
                        last.then_inc(gates_turned_1.sem, 1)
                    if 1 <= n <= MLA_H:
                        rotation(N_T + n - 1, q_mla[0:MLA_QK, n - 1, :], slice(0, MLA_QK), 0)
                pe.wait_ge(*hid_ready(layer, 2))
                for g in range(2):
                    for half in range(2):
                        nc.tensor.matmul(psum[DV * g:DV * (g + 1), 4, 0:NC], cmp_w2[:, 0, half, :], cmp_hid[:, 0, half, g, :],
                                         start=half == 0, stop=half == 1)
                for r in range(4):
                    for g in range(2):
                        for half in range(2):
                            last = nc.tensor.matmul(psum[32 * r:32 * r + NC, 5, g * DV:(g + 1) * DV], cmp_hid[:, 1, half, g, :],
                                                    cmp_w2[:, 1, half, :], start=half == 0, stop=half == 1)
                last.then_inc(cmp_kv_done.sem, 1)
                pe.wait_ge(*cmp_kv_ready(layer, 1))
                for q in range(N_R):
                    weights(ROW_S0 + q)
                    pos = (ROW_S0 + q) % SLOTS
                    for t in range(TT):
                        for k in range(ROW_K):
                            for m, (x, w) in enumerate(((h_hi, w_hi), (h_hi, w_lo), (h_lo, w_hi))):
                                last = nc.tensor.matmul(psum[:, 4 + t, :], x[:, q * ROW_K + k, t * P:(t + 1) * P], w[:, pos, k * 512:(k + 1) * 512],
                                                        start=q == 0 and k == 0 and m == 0, stop=q == N_R - 1 and k == ROW_K - 1 and m == 2)
                        if t == TT - 1:
                            last.then_inc(slot_used, 1)
                        elif q == N_R - 1:
                            last.then_inc(rows_done.sem, 1)

            def turn_o(layer, i):
                pe.wait_ge(*o_ready(layer, (i + 1) * NH))
                pe.wait_ge(*diff_ready(layer, i + 1))
                pe.wait_ge(*cmp_o_ready(layer, i + 1))
                for b in range(2):
                    for c in range(4):
                        last = nc.tensor.transpose(psum[:, 6 + b, c * P:(c + 1) * P], o_rows[:, i % 2, (4 * b + c) * P:(4 * b + c + 1) * P], ident[:])
                    last.then_inc(o_turned.sem, 1)

            def attention(layer):
                pe.wait_ge(*copied(layer, ITEMS))
                pe.wait_ge(*roped(layer, EVENTS - 3))
                pe.wait_ge(*turn_read(layer, EVENTS))
                pe.wait_ge(*cmp_kv_ready(layer, 1))
                pe.wait_ge(cond_ready, 1)
                for t in range(ATT + 2):
                    i, step = t // NH, t % NH
                    if t < ATT:
                        q, k, _ = key_values(*HEADS[step])
                        if t >= 2:
                            pe.wait_ge(*exp_ready(layer, t - 1))
                        n = (i + 1) * P
                        nc.tensor.matmul(psum[:, t % 2, 0:n], q(slice(i * P, (i + 1) * P)), k(n), start=True, stop=False)
                        nc.tensor.matmul(psum[:, t % 2, n - P:n], ident_b[:], causal_b[:], start=False, stop=True).then_inc(scores_done.sem, 1)
                        if step == AT_TURN and i > 0:
                            turn_o(layer, i - 1)
                        if step == AT_CMP:
                            if i:
                                pe.wait_ge(*o_lo_ready(layer, 2 * i))
                            for h in range(NSA_H):
                                g, c = h // 4, h % 4
                                rows = slice(DV * g, DV * (g + 1))
                                last = nc.tensor.matmul(psum[:, 6 + g, c * CMP_BLOCK:c * CMP_BLOCK + NC], q_nsa[rows, c, i * P:(i + 1) * P],
                                                        k_cmp[rows, :], start=True, stop=True)
                            last.then_inc(cmp_scores_done.sem, 1)
                        if step == AT_CMP + 4:
                            pe.wait_ge(*cmp_exp(layer, i + 1))
                            for g in range(2):
                                last = nc.tensor.transpose(psum[:, 7, g * P:(g + 1) * P],
                                                           cmp_p[:, 4 * g:4 * g + 4, :].rearrange("p h n -> p (h n)"), ident[:])
                            last.then_inc(cmp_turned.sem, 1)
                        if step == AT_CMP + 6:
                            pe.wait_ge(*cmp_pt_ready(layer, i + 1))
                            for g in range(NSA_G):
                                last = nc.tensor.matmul(psum[:, 6, g * 4 * DV:(g + 1) * 4 * DV], cmp_pt[:, g, :], v_cmp[:, g, :],
                                                        start=True, stop=True)
                            last.then_inc(cmp_o_done.sem, 1)
                    p = t - 1
                    if 0 <= p < ATT:
                        pe.wait_ge(*exp_ready(layer, p + 1))
                        if p >= 2:
                            pe.wait_ge(*last_turned(layer, p - 2))
                        for b in range(p // NH + 1):
                            last = nc.tensor.transpose(psum[:, 2 + p % 2, b * P:(b + 1) * P], probs[:, p % 2, b * P:(b + 1) * P], ident[:])
                        last.then_inc(probs_turned.sem, 1)
                    p = t - 2
                    if p >= 0:
                        _, _, v = key_values(*HEADS[p % NH])
                        pe.wait_ge(*last_turned(layer, p))
                        if p >= 2:
                            pe.wait_ge(*o_ready(layer, p - 1))
                        beside = psum[:, 4 + p % 2, DV:DV + 2 * P]
                        if p in ADA_AT:
                            for half in range(2):
                                turn, pos = slot_of(layer, MIX_S0 + PROJ_SLOTS + 2 * ADA_AT[p] + half)
                                pe.wait_ge(lo_ready, turn * SLOTS + (SLOTS + pos + 1))
                                for k in range(ADA_K):
                                    for m, (x, w) in enumerate(((cond_hi, w_hi), (cond_hi, w_lo), (cond_lo, w_hi))):
                                        last = nc.tensor.matmul(beside[0:COND_M, :], x[:, 2 * (half * ADA_K + k):2 * (half * ADA_K + k) + COND_M],
                                                                w[:, pos, k * 2 * P:(k + 1) * 2 * P],
                                                                start=half == 0 and k == 0 and m == 0, stop=half == 1 and k == ADA_K - 1 and m == 2)
                                last.then_inc(slot_used, 1)
                        if p - 2 in ADA_AT:
                            for b in range(2):
                                nc.tensor.transpose(beside[:, b * P:b * P + COND_M], mod_rows[:, b * P:(b + 1) * P], ident[0:COND_M, 0:COND_M])
                        for b in range(p // NH + 1):
                            last = nc.tensor.matmul(psum[:, 4 + p % 2, 0:DV], probs_t[:, p % 2, b * P:(b + 1) * P], v(b),
                                                    start=b == 0, stop=b == p // NH)
                        last.then_inc(o_done.sem, 1)
                turn_o(layer, TT - 1)

            def mixer_output(layer):
                pe.wait_ge(*o_lo_ready(layer, 2 * TT))
                for c in range(KD):
                    turn, pos = slot_of(layer, OUT_S0 + c)
                    pe.wait_ge(lo_ready, turn * SLOTS + (SLOTS + pos + 1))
                    if c >= 2:
                        pe.wait_ge(*x_updated(layer, MIX_Y0 + c - 1))
                    dense(pos, 0, KD, [lat], [psum[:, 6 + c % 2, :]]).then_inc(slot_used, 1)

            lat = halves(h_hi, h_lo)
            with pe.Fori(0, DEPTH) as layer:
                for j in range(2):
                    norm_sums(layer, FFN_V[j], [(0, T)])
                    ffn(layer, FFN_V[j], FFN_S0[j], FFN_N0[j], FFN_Y0[j], LAT, [lat])
                    if j == 0:
                        norm_sums(layer, 1, [(0, T)])
                        mixer_projections(layer)
                        attention(layer)
                        mixer_output(layer)
            norm_sums(LAST, 0, [(0, T)])

            pe.wait_ge(ctx_loaded, 16)
            for c in range(KD):
                for t in range(TCT):
                    last = nc.tensor.transpose(psum[:, 2 + c // 2, (c % 2 * TCT + t) * P:(c % 2 * TCT + t + 1) * P], ctx_rows[:, t, c * P:(c + 1) * P], ident[:])
                if c % 2:
                    last.then_inc(ctx_turned, 1)
            context = halves(h_ctx_hi, h_ctx_lo)
            norm_sums(LAST, 1, [(0, T), (T, C)])
            ffn(LAST, 0, S_FFN1, 0, Y_FFN1, BOTH, [lat, context])
            norm_sums(LAST, 2, [(0, T), (T, C)])

            def rotation(r, n):
                pe.wait_ge(copied_2, n + 1)
                if r >= 2:
                    pe.wait_ge(rot_read_2, r - 1)
                nc.tensor.matmul(psum[:, 4 + r % 2, :], rotate[:, 1, :], squares[:, r % 2, 0:T], start=True, stop=True).then_inc(rotated_2, 1)

            def bank_free(n):
                before = [i for i in range(n) if OUTS_2[i][4] == OUTS_2[n][4]]
                if before:
                    pe.wait_ge(copied_2, before[-1] + 1)

            pe.wait_ge(*h_lo_ready(LAST, 2 * KD))
            ropes = outs_done = 0
            rows_of = {False: (h_hi, h_lo), True: (h_ctx_hi, h_ctx_lo)}
            for s, (kind, j, k0, nk, cols) in enumerate(SLOTS_2):
                turn, pos = slot_of(LAST, S_MIX2 + s)
                pe.wait_ge(lo_ready, turn * SLOTS + (SLOTS + pos + 1))
                end = k0 + nk == KD
                final = next(i for i in range(s, len(SLOTS_2)) if SLOTS_2[i][2] + SLOTS_2[i][3] == KD)
                outs = [n for n, o in enumerate(OUTS_2) if o[0] == final]
                if k0 == 0:
                    for n in outs:
                        bank_free(n)
                if nk == KD:
                    last = dense(pos, 0, KD, [lat], [psum[:, OUTS_2[outs[0]][4], :]])
                elif kind == "gates":
                    for k in range(nk):
                        for m, (w, r) in enumerate(((w_hi, 0), (w_hi, 1), (w_lo, 0))):
                            for n, x, size in zip(outs, (lat, context), (T, C)):
                                last = nc.tensor.matmul(psum[:, OUTS_2[n][4], 0:size], w[:, pos, k * P:(k + 1) * P], x[r](k0 + k),
                                                        start=k0 + k == 0 and m == 0, stop=k0 + k == KD - 1 and m == 2)
                else:
                    for n in outs:
                        _, out_kind, _, t, b = OUTS_2[n]
                        xs = rows_of[out_kind.endswith("_ctx")]
                        for k in range(nk):
                            for m, (r, w) in enumerate(((0, w_hi), (0, w_lo), (1, w_hi))):
                                last = nc.tensor.matmul(psum[:, b, 0:cols], xs[r][:, k0 + k, t * P:(t + 1) * P], w[:, pos, k * cols:(k + 1) * cols],
                                                        start=k0 + k == 0 and m == 0, stop=k0 + k == KD - 1 and m == 2)
                        if end and n != outs[-1]:
                            last.then_inc(item_done_2, 1)
                last.then_inc(slot_used, 1)
                if outs_done and OUTS_2[outs_done - 1][1] in ROPED_2:
                    rotation(ropes, outs_done - 1)
                    ropes += 1
                outs_done = outs[-1] + 1 if end else 0

            pe.wait_ge(gate_w_loaded, 64)
            for t in range(TT + TCT):
                tok = (t + TT) % (TT + TCT) if t < TCT else t - TCT
                if t >= 2:
                    pe.wait_ge(gate_read, t - 1)
                elif t == 0:
                    pe.wait_ge(copied_2, N_2)
                nc.tensor.matmul(psum[:, 6 + t % 2, :], gate_in[:, tok * P:(tok + 1) * P], gate_w[:], start=True, stop=True).then_inc(gate_done, 1)

            pe.wait_ge(ctx_keys_ready, 1)
            for way in range(2):
                for h in range(RET_H):
                    cols = slice(h * P, (h + 1) * P)
                    for t in range(TCT):
                        last = nc.tensor.matmul(psum[:, way, cols], ctx_keys[:, way, t, cols], rv_ctx[:, t, cols], start=t == 0, stop=t == TCT - 1)
                last.then_inc(ret_state_done, 1)

            def ret_scores(h):
                for t in range(TT):
                    if h:
                        pe.wait_ge(ret_scores_ready, (h - 1) * TT + t + 1)
                    elif t < 2:
                        pe.wait_ge(ret_state_ready, t + 1)
                    nc.tensor.matmul(psum[:, t, :], rk[:, h, t * P:(t + 1) * P], rq[:, h, :], start=True, stop=True).then_inc(ret_scores_done, 1)

            pe.wait_ge(roped_2, 2 * RET_H)
            ret_scores(0)
            for h in range(RET_H):
                if h + 1 < RET_H:
                    ret_scores(h + 1)
                o = psum[:, 4 + h % 2, :]
                if h >= 2:
                    pe.wait_ge(ret_o_ready, h - 1)
                for t in range(TT):
                    pe.wait_ge(ret_scores_ready, h * TT + t + 1)
                    nc.tensor.matmul(o, rv[:, t, h * P:(h + 1) * P], scores_r[:, t, :], start=t == 0, stop=False)
                pe.wait_ge(q_dec_ready, h + 1)
                pe.wait_ge(ret_state_ready, 2)
                nc.tensor.matmul(o, ret_state[:, 0, h, :], q_dec[:, 0, :], start=False, stop=False)
                nc.tensor.matmul(o, ret_state[:, 1, h, :], q_dec[:, 1, :], start=False, stop=True).then_inc(ret_o_done, 1)

            pe.wait_ge(ret_o_ready, RET_H)
            for p in range(PAIRS):
                for t in range(TT):
                    last = nc.tensor.transpose(psum[:, p, t * P:(t + 1) * P], gk[:, p, t * P:(t + 1) * P], ident[:])
                last.then_inc(gk_turned, 1)
            for t in range(TT + TCT):
                for way in range(2):
                    for p in range(PAIRS):
                        d = (t * 2 + way) * PAIRS + p
                        last = nc.tensor.matmul(psum[:, 2, 2 * d:2 * d + 2], log_gates[:, t, (way * PAIRS + p) * P:(way * PAIRS + p + 1) * P], ones[:, 0:2],
                                                start=True, stop=True)
            last.then_inc(totals_done, 1)
            pe.wait_ge(gla_consts_loaded, 32)

            def suffixes(t):
                if t >= 2:
                    pe.wait_ge(suffix_exp, t - 1)
                for way in range(2):
                    last = nc.tensor.matmul(psum[:, 4 + t % 2, way * 2 * P:(way + 1) * 2 * P], tri[:, way, :], log_gates[:, t, way * 2 * P:(way + 1) * 2 * P],
                                            start=True, stop=True)
                last.then_inc(suffix_done, 1)

            made = [0, 0]
            total = 0
            suffixes(0)
            for t in range(TT + TCT):
                if t + 1 < TT + TCT:
                    suffixes(t + 1)
                pe.wait_ge(gk_dec_ready, t + 1)
                for way in range(2):
                    if state_slot(t, way) is None:
                        continue
                    if made[way]:
                        pe.wait_ge(state_copied, made[way])
                    total += 1
                    made[way] = total
                    v = gv_ctx[:, t, :] if t < TCT else gv[:, t - TCT, :]
                    for p in range(PAIRS):
                        last = nc.tensor.matmul(psum[:, 6 + way, p * 2 * P:(p + 1) * 2 * P], gk_dec[:, t % 2, way, p * P:(p + 1) * P],
                                                v[:, p * 2 * P:(p + 1) * 2 * P], start=True, stop=True)
                    last.then_inc(state_done, 1)

            def gla_sums(n, c, p):
                if n:
                    pe.wait_ge(factor_exp, n)
                for b in range(4):
                    at = slice(b * 512, (b + 1) * 512)
                    nc.tensor.matmul(psum[:, b, :], log_gates[:, TCT + c, p * P:(p + 1) * P], sums_f[:, at], start=True, stop=False)
                    last = nc.tensor.matmul(psum[:, b, :], log_gates[:, TCT + c, (PAIRS + p) * P:(PAIRS + p + 1) * P], sums_b[:, at], start=False, stop=True)
                last.then_inc(sums_done, 1)

            def gla_scores(n, c, p, half):
                at = slice(c * P, (c + 1) * P)
                if half == 0:
                    pe.wait_ge(factors_ready, n + 1)
                if n or half:
                    pe.wait_ge(gla_scores_step, (2 * n + half) * 4)
                for i in range(4):
                    level = 4 * half + i
                    for r in range(2):
                        rows = slice(GLA_DK * r, GLA_DK * (r + 1))
                        k = factors[rows, n % 2, LEVELS + 1 + level, :] if level < LEVELS else gk[rows, p, at]
                        q = factors[rows, n % 2, level, :] if level < LEVELS else q_twice[rows, p, at]
                        last = nc.tensor.matmul(psum[:, 4 + r, i * P:(i + 1) * P], k, q, start=True, stop=True)
                last.then_inc(gla_scores_done, 1)

            def gla_output(n, c, p):
                pe.wait_ge(gla_scores_step, (n + 1) * (LEVELS + 1))
                if n:
                    pe.wait_ge(gla_o_ready, n)
                for r in range(2):
                    rows = slice(GLA_DK * r, GLA_DK * (r + 1))
                    o = psum[:, 6 + r, 0:P]
                    nc.tensor.matmul(o, gv[:, c, (2 * p + r) * P:(2 * p + r + 1) * P], scores_g[:, n % 2, r, :], start=True, stop=False)
                    nc.tensor.matmul(o, gla_state[rows, 0, p, TCT - 1 + c, :], factors[rows, n % 2, LEVELS, :], start=False, stop=False)
                    last = nc.tensor.matmul(o, gla_state[rows, 1, p, TCT + TT - 2 - c, :], factors[rows, n % 2, 2 * LEVELS + 1, :], start=False, stop=True)
                last.then_inc(gla_o_done, 1)

            pe.wait_ge(sums_loaded, 32)
            pe.wait_ge(state_step, STATES - 1)
            gla_sums(*units()[0])
            for n, c, p in units():
                if n + 1 < UNITS:
                    gla_sums(*units()[n + 1])
                gla_scores(n, c, p, 0)
                if n:
                    gla_output(*units()[n - 1])
                gla_scores(n, c, p, 1)
            gla_output(*units()[UNITS - 1])

            pe.wait_ge(gla_o_ready, UNITS)
            for h in range(2 * RET_H + 1):
                if h < RET_H:
                    if h >= 2:
                        pe.wait_ge(centred, h - 1)
                    nc.tensor.matmul(psum[:, h % 2, :], ones[:], rq[:, h, :], start=True, stop=True).then_inc(mean_done, 1)
                g = h - 1
                if g >= 0:
                    pe.wait_ge(merge_sq, g + 1)
                    if g >= 2:
                        pe.wait_ge(merge_std, g - 1)
                    nc.tensor.matmul(psum[:, 2 + g % 2, :], ones[:], squares[:, g % 2, 0:T], start=True, stop=True).then_inc(merge_sum, 1)
            pe.wait_ge(merge_lo, 2 * RET_H)
            for c in range(KD):
                turn, pos = slot_of(LAST, S_MIX2 + len(SLOTS_2) + c)
                pe.wait_ge(lo_ready, turn * SLOTS + (SLOTS + pos + 1))
                if c >= 2:
                    pe.wait_ge(*x_updated(LAST, Y_MIX2 + c - 1))
                dense(pos, 0, KD, [lat], [psum[:, 6 + c % 2, :]]).then_inc(slot_used, 1)
            norm_sums(LAST, 3, [(0, T)])
            ffn(LAST, 2, S_FFN2, NF, Y_FFN2, LAT, [lat])
            norm_sums(LAST, 4, [(0, T)])
            for t in range(TT):
                if t >= 2:
                    pe.wait_ge(y_rows_ready, t - 1)
                for c in range(KD):
                    pe.wait_ge(*x_updated(LAST, Y_END + c + 1))
                    last = nc.tensor.transpose(psum[:, 2 + 2 * (t % 2) + c // 4, (c % 4) * P:(c % 4 + 1) * P],
                                               x_lat[:, c, t * P:(t + 1) * P], ident[:])
                    if c % 4 == 3:
                        last.then_inc(out_turned, 1)


def rope_table(dim):
    inv = np.float32(10000.0) ** (-np.arange(0, dim, 2, dtype=np.float32) / np.float32(dim))
    ang = (np.arange(T, dtype=np.float32)[:, None] * inv[None, :]).astype(np.float32)
    rows = np.arange(P) % (dim // 2)
    return np.cos(ang)[:, rows].T, np.sin(ang)[:, rows].T


def rotation_matrix(dim):
    r = np.zeros((P, P), np.float32)
    for i in range(P):
        if i % dim < dim // 2:
            r[i + dim // 2, i] = -1.0
        else:
            r[i - dim // 2, i] = 1.0
    return r


def constants_2():
    tok = np.arange(T)
    freqs = np.float32(10000.0) ** (-np.arange(32, dtype=np.float32) / np.float32(32))
    row, col = (tok // GRID_W).astype(np.float32), (tok % GRID_W).astype(np.float32)
    dims = np.arange(P)
    ang = np.where(dims[:, None] < P // 2, row[None, :], col[None, :]).astype(np.float32) * freqs[dims % 32][:, None]
    gap = np.arange(STRIP)[None, :] - MID - dims[:, None]
    mid = gap[:, MID:MID + P]
    ctx_tok = (np.arange(TCT)[None, :] * P + dims[:, None])
    j, i = dims[:, None], dims[None, :]
    q_f, q_b, k_f, k_b, masks = [], [], [], [], []
    for level in range(LEVELS):
        size = P >> level
        middle = i // size * size + size // 2
        second = i >= middle
        q_f.append(second & (j >= middle) & (j <= i))
        q_b.append(~second & (j >= i) & (j < middle))
        k_f.append(~second & (j > i) & (j < middle))
        k_b.append(second & (j >= middle) & (j < i))
        masks.append((j // size == i // size) & (j // (size // 2) != i // (size // 2)))
    masks.append(i == j)
    none = np.zeros((P, P), bool)
    f32 = np.float32
    return {
        "c_grid": np.stack([np.cos(ang), np.sin(ang)], 1).astype(f32),
        "c_key_pos": np.stack([C - 1 - ctx_tok, ctx_tok], 1).astype(f32),
        "c_distance": np.concatenate([np.abs(gap), mid >= 0, mid <= 0], 1).astype(f32),
        "c_row_pos": np.tile(np.stack([tok + 1, T - tok]).astype(f32), (P, 1, 1)),
        "c_masks": np.stack(masks, 1).astype(np.uint32),
        "c_tri": np.stack([j > i, j < i], 1).astype(f32),
        "c_sums_f": np.concatenate(q_f + [j <= i] + k_f + [none], 1).astype(f32),
        "c_sums_b": np.concatenate(q_b + [none] + k_b + [j >= i], 1).astype(f32),
    }


def constants():
    causal = np.where(np.arange(P)[None, :] <= np.arange(P)[:, None], 0.0, NEG).astype(np.float32)
    ends = np.arange(NC) * CMP_STRIDE + CMP_BLOCK - 1
    tokens = np.arange(T).reshape(TT, P).T
    lam0 = [0.8 - 0.6 * np.exp(-0.3 * i) for i in range(DEPTH)]
    return {
        "c_ident": np.eye(P, dtype=np.float32),
        "c_ones": np.ones((P, P), np.float32),
        "c_rope": np.stack([*rope_table(32), *rope_table(64)], 1).astype(np.float32),
        "c_rotate": np.stack([rotation_matrix(32), rotation_matrix(64)], 1),
        "c_causal": causal,
        "c_cmp_mask": np.where(ends[None, None, :] <= tokens[:, :, None], 0.0, NEG).astype(np.float32),
        "c_cmp_any": (np.arange(P)[:, None] >= ends[0]).astype(np.float32),
        **constants_2(),
        "c_lam": np.tile(np.array([v for x in lam0 for v in (x, 1.0 - x)], np.float32), (P, 1)),
    }


INPUTS = """x ffn_norm_g ffn_w_gate ffn_w_up ffn_w_down mix_norm_g w_in mla_q_norm_g mla_w_uq mla_kv_norm_g mla_w_ukv
diff_lambda diff_norm_g nsa_cmp_pos nsa_cmp_w1 nsa_cmp_b1 nsa_cmp_w2 nsa_gate_b w_out final_norm_g c_2 ctx_2 c_ctx_2
ada_w_2 ada_b_2 norm1_w_2 ffn1_w1_2 ffn1_w3_2 ffn1_w2_2 norm2_w_2 w_in_2 ret_decay_f_2 ret_decay_b_2 ret_norm_w_2
gla_gate_w_f_2 gla_gate_b_f_2 gla_gate_w_b_2 gla_gate_b_b_2 gla_norm_w_2 w_out_2 norm3_w_2 ffn2_w1_2 ffn2_w3_2
ffn2_w2_2 final_norm_w_2""".split()


def kernel(**inputs):
    import concourse.bacc as bacc
    from concourse.bass_utils import run_bass_kernel_spmd

    nc = bacc.Bacc("TRN2", target_bir_lowering=False, num_devices=1)
    arrays = {name: np.ascontiguousarray(inputs[name]) for name in INPUTS}
    arrays.update(constants())
    aps = {name: nc.dram_tensor(name, v.shape, mybir.dt.from_np(v.dtype), kind="ExternalInput").ap()
           for name, v in arrays.items()}
    out = nc.dram_tensor("out", (1, T, D), F32, kind="ExternalOutput").ap()
    build(nc, aps, out)
    return run_bass_kernel_spmd(nc, [arrays], core_ids=[0]).results[0]["out"]
```

```python
from contextlib import ExitStack

import numpy as np

import concourse.bass as bass
from concourse import mybir

F32 = mybir.dt.float32
F32R = mybir.dt.float32r
BF16 = mybir.dt.bfloat16
ALU = mybir.AluOpType
ACT = mybir.ActivationFunctionType
AX_X = mybir.AxisListType.X

P = 128
D = 1024
KD = D // P
T = 512
TT = T // P
C = 256
TC = T + C
DEPTH = 2
D_FF = 2816
NF = D_FF // P
EPS = 1e-6
SLOTS = 4
SLOT = KD * P
PARTS = ((0, 8), (8, 8), (16, 6))
FFN_SLOTS = 2 * NF + KD * len(PARTS)
MLA_H, MLA_NOPE, MLA_ROPE = 4, 64, 32
MLA_QK = MLA_NOPE + MLA_ROPE
MLA_QR, MLA_KVR = 256, 128
DIFF_H, DIFF_QK = 4, 32
NSA_H, NSA_G = 8, 2
DV = 64
CMP_BLOCK, CMP_STRIDE, CMP_HID = 32, 16, 256
NC = (T - CMP_BLOCK) // CMP_STRIDE + 1
NEG = -1e30
assert T // 64 <= 16 and T <= 512
IN_CQ, IN_CKV, IN_KR, IN_DQ, IN_DK, IN_DV, IN_NQ, IN_NKV, IN_NG = (
    int(v) for v in np.cumsum((0, MLA_QR, MLA_KVR, MLA_ROPE, 256, 256, 256, 512, 768)))
N_IN = IN_NG + 3 * NSA_H
GATE_AT = P - 3 * NSA_H
CMP_K, CMP_V, SLC_K, SLC_V, WIN_K, WIN_V = (IN_NKV + P * i for i in range(6))
TILES = ([("cq", IN_CQ, 0), ("cq", IN_CQ + P, 1), ("cq", IN_CKV, 2), ("kr", IN_KR, 0), ("ck", CMP_K, 0), ("cv", CMP_V, 0)]
         + [("nq", IN_NQ + DV * j, j) for j in range(4)] + [("ks", SLC_K, 0), ("kw", WIN_K, 0)]
         + [("dq", IN_DQ + P * i, i) for i in range(2)] + [("dk", IN_DK + P * i, i) for i in range(2)] + [("ng", N_IN - P, 0)])
ROWS = ((IN_DV, 0, 2 * P), (SLC_V, 2 * P, P), (WIN_V, 3 * P, P))
ROW_K = 2
N_T, N_R = len(TILES), KD // ROW_K
UQ_SLOTS = 2
ROW_S0 = N_T + UQ_SLOTS + 1
PROJ_SLOTS = ROW_S0 + N_R
LATE_ITEMS = 2 * MLA_H + 2
ITEMS = N_T + LATE_ITEMS + TT
SLOT_ENDS = (1, 3, LATE_ITEMS - 1)
N_MOD = 9
ADA_SLOTS = N_MOD * KD // DEPTH
MIX_SLOTS = PROJ_SLOTS + ADA_SLOTS + KD
LAYER_SLOTS = 2 * FFN_SLOTS + MIX_SLOTS
ROPED = ("kr", "ck", "nq", "ks", "kw", "dq", "dk")
PAIR_TAPS = CMP_BLOCK // 2
AUX_PAIRS, AUX_RING = 2, 4
AUX_V = PAIR_TAPS // AUX_PAIRS
KEYS_AT, VALUES_AT = 7, 12
AUX_AT = {at + i: range(v * AUX_V + 2 * i, v * AUX_V + 2 * i + 2) for v, at in enumerate((KEYS_AT, VALUES_AT)) for i in range(AUX_V // 2)}
PARAMS = 9
HEADS = ([("mla", h, 0) for h in range(MLA_H)] + [("diff", h, m) for h in range(DIFF_H) for m in range(2)]
         + [("slc", h, 0) for h in range(NSA_H)] + [("win", h, 0) for h in range(NSA_H)])
NH = len(HEADS)
ATT = NH * TT
SCALED = 2 * DIFF_H // 2 + 2 * NSA_H
ADA_AT = {6 * i + 1: i for i in range(ADA_SLOTS // 2)}
ADA_K = KD // 2
COND_M = 66
assert max(ADA_AT) + 5 < ATT
AT_TURN, AT_CMP, AT_DIFF = 3, 6, 14
MIX_Y = KD
RET_H, RET_DK = 4, 128
GLA_H, GLA_DK, GLA_RANK, GLA_TAU = 4, 64, 16, 16.0
PAIRS = GLA_H // 2
GRID_W = 64
TCT = C // P
IN_2 = dict(zip(("rq", "rk", "rv", "rg", "gq", "gk", "gv", "gg", "gates"),
                (int(v) for v in np.cumsum((0, 512, 512, 512, 512, 256, 256, 512, 512 + 2 * GLA_RANK - P)))))
IN_2.update(rk_ctx=IN_2["rk"], gk_ctx=IN_2["gk"])
GATE_ROW = P - 2 * GLA_RANK
SLOTS_2 = []
for _kind, _slots in (("rk", 4), ("rq", 4), ("rk_ctx", 4), ("rv", 4), ("gk", 2), ("gq", 2), ("gk_ctx", 2), ("gv", 4),
                      ("gates", 2), ("rg", 4), ("gg", 4)):
    for _j in range(_slots):
        _wide = {"rk_ctx": (2, 4 * P), "rv": (2, 4 * P), "gv": (2, 4 * P), "gk_ctx": (4, 2 * P), "gates": (4, P)}
        _nk, _n = _wide.get(_kind, (KD, P))
        SLOTS_2.append((_kind, _j, _j * _nk if _kind in _wide else 0, _nk, _n))
OUTS_2 = []
_tiles = 0
for _s, (_kind, _j, _k0, _nk, _n) in enumerate(SLOTS_2):
    if _k0 + _nk < KD:
        continue
    if _kind in ("rv", "gv"):
        OUTS_2 += [(_s, _kind, 0, _t, _t) for _t in range(TT)]
    if _kind in ("rv", "gv", "rk_ctx", "gk_ctx"):
        OUTS_2 += [(_s, _kind.removesuffix("_ctx") + "_ctx", 0, _t, 6 + _t) for _t in range(TCT)]
    else:
        OUTS_2.append((_s, _kind, _j, 0, _tiles % 4))
        _tiles += 1
        if _kind == "gates":
            OUTS_2.append((_s, "gates_ctx", 0, 0, 6))
N_2 = len(OUTS_2)
ROPED_2 = ("rk", "rq")
S_FFN1 = 0
S_MIX2 = S_FFN1 + FFN_SLOTS
S_FFN2 = S_MIX2 + len(SLOTS_2) + KD
SLOTS_ALL = DEPTH * LAYER_SLOTS + S_FFN2 + FFN_SLOTS
assert S_MIX2 % SLOTS == 0 and S_FFN2 % SLOTS == 0
Y_FFN1 = KD
Y_MIX2 = Y_FFN1 + len(PARTS) * KD
Y_FFN2 = Y_MIX2 + KD
Y_END = Y_FFN2 + len(PARTS) * KD
ROW_NORM, ROW_FINAL, ROW_RET, ROW_GLA, ROW_COND = (int(v) for v in np.cumsum((0, 3 * KD, KD, 4, 4)))
STRIP = 2 * T - P
MID = T - P
LEVELS = 7
GATE_HALVES = (slice(0, (TT + TCT) // 2), slice((TT + TCT) // 2, TT + TCT))
UNITS = TT * PAIRS
STATES = TCT + TT - 1
NORMS = 3


class Signal:

    def __init__(self, sem, per_layer, start=0):
        self.sem, self.per_layer, self.start = sem, per_layer, start

    def __call__(self, layer, n):
        return self.sem, layer * self.per_layer + (self.start + n)


def build(nc, a, out):
    ctx = ExitStack()
    with ctx:
        top = [(nc.sbuf_base + 63) // 64 * 64]

        def put(name, shape, dt=F32):
            t = nc.alloc_sbuf_tensor_at(name, shape, dt, offset=top[0])
            size = int(np.prod(shape[1:])) * (2 if dt == BF16 else 4)
            top[0] += (size + 31) // 32 * 32
            assert top[0] <= nc.sbuf_usable_end, (name, top[0])
            return t

        def sem(name):
            return ctx.enter_context(nc.semaphore(name))

        def signal(name, per_layer, start=0):
            return Signal(sem(name), per_layer, start)

        x_lat = put("x_lat", [P, KD, T])
        w_raw = put("w_raw", [P, SLOTS, SLOT])
        w_hi = put("w_hi", [P, SLOTS, SLOT], F32R)
        w_lo = put("w_lo", [P, SLOTS, SLOT], F32R)
        h_at = top[0]
        h_hi = put("h_hi", [P, KD, T], F32R)
        h_lo = put("h_lo", [P, KD, T], F32R)
        squares_at = top[0]
        squares = put("squares", [P, 2, TC])
        normed_at = top[0]
        normed = put("normed", [P, 2, TC])
        rstd = put("rstd", [P, TC])
        ident = put("ident", [P, P])
        ones = put("ones", [P, P])
        gains = put("gains", [P, 70])
        layer_gains = put("layer_gains", [P, 31])
        eps = put("eps", [P, 1])
        rope_at = top[0]
        rope = put("rope", [P, 4, T])
        rotate = put("rotate", [P, 2, P])
        ident_b = put("ident_b", [P, P], BF16)
        causal_b = put("causal_b", [P, P], BF16)
        cmp_any = put("cmp_any", [P, 1])
        lam_consts = put("lam_consts", [P, 2 * DEPTH])
        lam_layer = put("lam_layer", [P, 2])
        credits = put("credits", [P, 20])
        gains_2 = put("gains_2", [P, 56])
        mod = put("mod", [P, 2, N_MOD * KD])
        cond_parts = put("cond_parts", [P, 4 * KD + COND_M], F32R)
        cond_halves = cond_parts[:, 0:4 * KD].rearrange("p (c h g) -> p c h g", h=2, g=2)
        cond_sum = put("cond_sum", [P, 2])
        decay = put("decay", [P, 2, RET_H])
        zone = top[0]

        a_hi = put("a_hi", [P, PARTS[0][1], TC], F32R)
        a_lo = put("a_lo", [P, PARTS[0][1], TC], F32R)
        silu_g = put("silu_g", [P, 2, TC])
        gated = put("gated", [P, 2, TC])
        x_ctx = put("x_ctx", [P, KD, C])
        h_ctx_hi = put("h_ctx_hi", [P, KD, C], F32R)
        h_ctx_lo = put("h_ctx_lo", [P, KD, C], F32R)
        top[0] = zone
        x_rows = put("x_rows", [P, TT, D])
        gain_rows = put("gain_rows", [P, P])
        gain_rows_2 = put("gain_rows_2", [P, P])
        cond = put("cond", [P, KD, 2])
        causal = put("causal", [P, P])
        top[0] = zone
        y_rows = put("y_rows", [P, 2, D])

        top[0] = zone
        aux = nc.alloc_sbuf_tensor_at("aux", [P, AUX_RING, AUX_PAIRS * CMP_HID], F32, offset=zone)
        q_mla = put("q_mla", [P, MLA_H, T])
        k_mla = put("k_mla", [P, MLA_H, T])
        v_mla = put("v_mla", [P, TT, MLA_H * DV])
        q_diff = put("q_diff", [P, 2, T])
        k_diff = put("k_diff", [P, 2, T])
        v_diff = put("v_diff", [P, TT, 2 * P])
        q_nsa = put("q_nsa", [P, 4, T])
        k_slc = put("k_slc", [P, T])
        k_win = put("k_win", [P, T])
        v_slc = put("v_slc", [P, TT, P])
        hid_rows = nc.alloc_sbuf_tensor_at("hid_rows", [NC, NSA_G, CMP_HID], F32, offset=top[0])
        v_win = put("v_win", [P, TT, P])
        taps = put("taps", [P, NSA_G, PAIR_TAPS, NC])
        rope_in = put("rope_in", [P, 2, T])
        v_cmp = put("v_cmp", [P, 2, 4 * DV])
        swap = put("swap", [P, P])
        lam_rows = put("lam_rows", [P, 4 * DIFF_QK])
        lam_stats = put("lam_stats", [P, 8])
        diff_gain = put("diff_gain", [P, DV])
        gate_bias = put("gate_bias", [P, 3 * NSA_H])
        gates = put("gates", [P, TT, 3 * NSA_H])
        pos_rows = put("pos_rows", [2 * CMP_BLOCK, P])
        pos_cols = put("pos_cols", [P, 2 * CMP_BLOCK])
        cmp_w2 = put("cmp_w2", [P, 2, 2, DV])
        cmp_mask = put("cmp_mask", [P, TT, NC])
        cmp_hid = put("cmp_hid", [P, 2, 2, 2, NC])
        k_cmp = put("k_cmp", [P, NC])
        neg_max = put("neg_max", [P, ATT])
        exp_sum = put("exp_sum", [P, ATT])
        scaled_inv = put("scaled_inv", [P, ATT])
        cmp_stats = put("cmp_stats", [P, 3, NSA_H])
        diff_stats = put("diff_stats", [P, DIFF_H])
        latents_at = top[0]
        latents = put("latents", [P, 3, T])
        latents_hi = put("latents_hi", [P, 3, T], F32R)
        latents_lo = put("latents_lo", [P, 3, T], F32R)
        tok_cmp = nc.alloc_sbuf_tensor_at("tok_cmp", [P, 2, T], F32, offset=zone + 4 * 2 * MLA_H * T)
        top[0] = zone + 4 * (2 * MLA_H * T + TT * MLA_H * DV + 2 * 2 * T + TT * 2 * P + 4 * T + 2 * T + 2 * TT * P)
        cmp_p = put("cmp_p", [P, NSA_H, CMP_BLOCK])
        cmp_pt = put("cmp_pt", [P, 2, P])
        diff_sq = put("diff_sq", [P, DIFF_H, DV])
        top[0] = latents_at
        probs = put("probs", [P, 2, T])
        probs_t = put("probs_t", [P, 2, T])
        o_rows = put("o_rows", [P, 2, D])
        diff_half = put("diff_half", [P, DV])
        mod_rows = put("mod_rows", [COND_M, 2 * P])

        top[0] = rope_at
        grid = put("grid", [P, 2, T])
        mod_gain = put("mod_gain", [P, 3, KD, 2])
        res = put("res", [P, 3, KD, 2])
        log_decay = put("log_decay", [P, 2, RET_H])
        log_steps = put("log_steps", [P, 4, 2 * RET_H])
        merge_gains = put("merge_gains", [P, 2 * RET_H])
        key_decay = put("key_decay", [P, 2, TCT, RET_H])
        key_pos = put("key_pos", [P, 2, TCT])
        chunk_decay = put("chunk_decay", [P, (TT + TCT) * PAIRS * 2, 2])
        gk_ctx = put("gk_ctx", [P, TCT, 2 * P])
        assert top[0] <= rope_at + 4 * 4 * T
        top[0] = zone
        ctx_rows = nc.alloc_sbuf_tensor_at("ctx_rows", [P, TCT, D], F32, offset=zone)
        rq = put("rq", [P, RET_H, T])
        rk = put("rk", [P, RET_H, T])
        rv = put("rv", [P, TT, RET_H * P])
        rv_ctx = put("rv_ctx", [P, TCT, RET_H * P])
        rk_ctx = put("rk_ctx", [P, TCT, RET_H * P])
        gv = put("gv", [P, TT, GLA_H * P])
        gv_ctx = put("gv_ctx", [P, TCT, GLA_H * P])
        gq = put("gq", [P, PAIRS, T])
        gk = put("gk", [P, PAIRS, T])
        gg = put("gg", [P, GLA_H, T])
        rg = put("rg", [P, RET_H, T])
        log_gates_at = top[0]
        log_gates = put("log_gates", [P, TT + TCT, 2 * 2 * P])
        row_pos = put("row_pos", [P, 2, T])
        assert top[0] <= nc.sbuf_usable_end

        def over(name, shape, at, dt=F32):
            return nc.alloc_sbuf_tensor_at(name, shape, dt, offset=at)

        gate_in = over("gate_in", [P, TC], normed_at)
        strip = over("strip", [P, RET_H, STRIP], h_at)
        scores_r = over("scores_r", [P, TT, T], h_at + 14336)
        ctx_keys = over("ctx_keys", [P, 2, TCT, RET_H * P], h_at + 14336)
        q_dec = over("q_dec", [P, 2, T], h_at + 22528)
        strip_mid = over("strip_mid", [P, 2, RET_H, P], rope_at)
        ret_state = over("ret_state", [P, 2, RET_H, P], h_at + 26624)
        gate_w = over("gate_w", [P, 4 * P], h_at + 30720)
        gate_b = over("gate_b", [P, 4 * P], h_at + 24576)
        gate_tmp = over("gate_tmp", [P, TT + TCT, 4 * P], h_at + 14336)
        distance = over("distance", [P, STRIP + 2 * P], squares_at)
        sums_raw = [over(f"sums_{way}_raw", [P, 2 * (LEVELS + 1) * P], h_at + 8192 * i) for i, way in enumerate("fb")]
        sums_f, sums_b = (over(f"sums_{way}", [P, 2 * (LEVELS + 1) * P], h_at + 8192 * i, F32R) for i, way in enumerate("fb"))
        factors = over("factors", [P, 2, 2 * (LEVELS + 1), P], h_at + 16384)
        masks = over("masks", [P, LEVELS + 1, P], rope_at, mybir.dt.uint32)
        gla_state = over("gla_state", [P, 2, PAIRS, STATES, P], zone + 16384)
        scores_g = over("scores_g", [P, 2, 2, P], zone + 28672)
        tri = over("tri", [P, 2, P], zone + 28672 + 2048)
        gk_dec = over("gk_dec", [P, 2, 2, 2 * P], squares_at)
        gk_rows = over("gk_rows", [P, TT, 2 * P], squares_at + 4096)
        log_gates_hi = over("log_gates_hi", [P, TT, 2 * 2 * P], squares_at, F32R)
        log_gates_lo = over("log_gates_lo", [P, TT, 2 * 2 * P], log_gates_at + TCT * 2 * 2 * P * 4, F32R)
        q_twice = over("q_twice", [P, PAIRS, T], squares_at + 8192)
        inv_2 = over("inv_2", [P, 2, T], rope_at)

        psum = ctx.enter_context(nc.psum_tensor("psum", [P, 8, 512], F32))

        consts_loaded = sem("consts_loaded")
        x_rows_loaded = sem("x_rows_loaded")
        eps_set = sem("eps_set")
        x_turned = sem("x_turned")
        gains_turned = sem("gains_turned")
        gains_ready = sem("gains_ready")
        layer_gains_ready = signal("layer_gains_ready", 1)
        slot_loaded = [sem(f"slot_loaded{i}") for i in range(SLOTS)]
        hi_ready = sem("hi_ready")
        lo_ready = sem("lo_ready")
        slot_used = sem("slot_used")
        sq_ready = signal("sq_ready", NORMS * KD)
        sq_used = signal("sq_used", NORMS * (KD - 1), 1)
        sum_done = signal("sum_done", NORMS)
        std_ready = signal("std_ready", 2 * NORMS)
        rstd_ready = signal("rstd_ready", 2 * NORMS)
        normed_ready = signal("normed_ready", NORMS * KD)
        h_hi_ready = signal("h_hi_ready", NORMS * KD)
        h_lo_ready = signal("h_lo_ready", NORMS * KD, 2)
        silu_done = signal("silu_done", 2 * NF)
        gated_ready = signal("gated_ready", 2 * NF, 2)
        a_hi_ready = signal("a_hi_ready", 2 * NF)
        a_lo_ready = signal("a_lo_ready", 2 * NF, 2)
        LAYER_Y = 2 * len(PARTS) * KD + MIX_Y
        x_updated = signal("x_updated", LAYER_Y, KD)
        params_loaded = signal("params_loaded", PARAMS * 16)
        aux_loaded = [signal(f"aux_loaded{i}", 2 * AUX_V // AUX_RING * 16) for i in range(AUX_RING)]
        aux_used = signal("aux_used", 2 * AUX_V, AUX_RING)
        copied = signal("copied", ITEMS, 2)
        item_done = signal("item_done", LATE_ITEMS - len(SLOT_ENDS))
        latent_sq = signal("latent_sq", 2)
        latent_sum = signal("latent_sum", 2)
        latent_std = signal("latent_std", 2)
        latent_normed = signal("latent_normed", 3)
        latent_hi_ready = signal("latent_hi_ready", 3)
        latent_lo_ready = signal("latent_lo_ready", 3)
        part_loaded = [signal(f"part_loaded{i}", 48) for i in range(N_R)]
        rows_done = signal("rows_done", TT - 1)
        gates_turned_1 = signal("gates_turned_1", 1)
        swapped = signal("swapped", 2)
        hid_copied = signal("hid_copied", 2)
        hid_turned = signal("hid_turned", 2)
        GATE_EVENT = 4 + sum(k in ROPED for k, _, _ in TILES) + 1
        EVENTS = GATE_EVENT + MLA_H
        rotated = signal("rotated", EVENTS - 5)
        turn_read = signal("turn_read", EVENTS, 2)
        roped = signal("roped", EVENTS - 5)
        lam_step = signal("lam_step", 4)
        lam_exp = signal("lam_exp", 1)
        pos_turned = signal("pos_turned", 1)
        pos_ready = signal("pos_ready", 1)
        taps_ready = signal("taps_ready", 2)
        hid_ready = signal("hid_ready", 2)
        cmp_kv_done = signal("cmp_kv_done", 1)
        cmp_kv_ready = signal("cmp_kv_ready", 1)
        gate_exp = signal("gate_exp", 1)
        gate_step = signal("gate_step", 2)
        scores_done = signal("scores_done", ATT)
        max_ready = signal("max_ready", ATT)
        exp_ready = signal("exp_ready", ATT)
        probs_turned = signal("probs_turned", ATT)
        probs_t_act = signal("probs_t_act", ATT // 2)
        probs_t_dve = signal("probs_t_dve", ATT // 2)
        o_done = signal("o_done", ATT)
        inv_ready = signal("inv_ready", ATT)
        scaled_ready = signal("scaled_ready", SCALED * TT)
        o_ready = signal("o_ready", ATT)
        cmp_scores_done = signal("cmp_scores_done", TT)
        cmp_step = signal("cmp_step", 7 * TT + 2)
        cmp_exp = signal("cmp_exp", TT)
        cmp_turned = signal("cmp_turned", TT)
        cmp_pt_ready = signal("cmp_pt_ready", TT)
        cmp_o_done = signal("cmp_o_done", TT)
        cmp_o_ready = signal("cmp_o_ready", TT)
        diff_step = signal("diff_step", 4 * TT)
        diff_std = signal("diff_std", TT)
        diff_ready = signal("diff_ready", TT)
        o_turned = signal("o_turned", 2 * TT)
        o_hi_ready = signal("o_hi_ready", 2 * TT)
        o_lo_ready = signal("o_lo_ready", 2 * TT)
        cond_step = sem("cond_step")
        log_step = sem("log_step")
        log_exp = sem("log_exp")
        key_step = sem("key_step")
        cond_ready = sem("cond_ready")
        mod_done = sem("mod_done")
        block2_loaded = sem("block2_loaded")
        ctx_loaded = sem("ctx_loaded")
        ctx_turned = sem("ctx_turned")
        ctx_ready = sem("ctx_ready")
        item_done_2 = sem("item_done_2")
        copied_2 = sem("copied_2")
        rotated_2 = sem("rotated_2")
        rot_read_2 = sem("rot_read_2")
        roped_2 = sem("roped_2")
        gate_w_zeroed = sem("gate_w_zeroed")
        gate_w_loaded = sem("gate_w_loaded")
        ret_consts_loaded = sem("ret_consts_loaded")
        tri_loaded = sem("tri_loaded")
        sums_loaded = sem("sums_loaded")
        gate_done = sem("gate_done")
        gate_read = sem("gate_read")
        gate_neg = sem("gate_neg")
        gate_log = sem("gate_log")
        log_gates_ready = sem("log_gates_ready")
        sums_act_ready = sem("sums_act_ready")
        sums_dve_ready = sem("sums_dve_ready")
        strip_exp = sem("strip_exp")
        strip_step = sem("strip_step")
        strip_ready = sem("strip_ready")
        ctx_keys_ready = sem("ctx_keys_ready")
        ret_state_done = sem("ret_state_done")
        ret_state_ready = sem("ret_state_ready")
        ret_scores_done = sem("ret_scores_done")
        ret_scores_ready = sem("ret_scores_ready")
        q_exp_ready = sem("q_exp_ready")
        q_dec_ready = sem("q_dec_ready")
        ret_o_done = sem("ret_o_done")
        ret_o_ready = sem("ret_o_ready")
        gk_turned = sem("gk_turned")
        gk_rows_ready = sem("gk_rows_ready")
        totals_done = sem("totals_done")
        totals_ready = sem("totals_ready")
        suffix_done = sem("suffix_done")
        suffix_exp = sem("suffix_exp")
        gk_dec_ready = sem("gk_dec_ready")
        state_done = sem("state_done")
        state_copied = sem("state_copied")
        state_step = sem("state_step")
        sums_done = sem("sums_done")
        factor_exp = sem("factor_exp")
        factors_ready = sem("factors_ready")
        gla_scores_done = sem("gla_scores_done")
        gla_scores_step = sem("gla_scores_step")
        gla_o_done = sem("gla_o_done")
        gla_o_ready = sem("gla_o_ready")
        mean_done = sem("mean_done")
        centred = sem("centred")
        merge_sq = sem("merge_sq")
        merge_sum = sem("merge_sum")
        merge_std = sem("merge_std")
        merge_inv = sem("merge_inv")
        merge_normed = sem("merge_normed")
        merged = sem("merged")
        merge_hi = sem("merge_hi")
        merge_lo = sem("merge_lo")
        out_turned = sem("out_turned")
        y_rows_ready = sem("y_rows_ready")
        stored = [sem("stored0"), sem("stored1")]

        FFN_S0 = (0, FFN_SLOTS + MIX_SLOTS)
        FFN_Y0 = (0, len(PARTS) * KD + MIX_Y)
        FFN_N0 = (0, NF)
        LAST = DEPTH

        def slot_of(layer, s):
            return layer * (LAYER_SLOTS // SLOTS) + s // SLOTS, s % SLOTS

        LAT = [(0, 0, T)]
        BOTH = [(0, 0, T), (T, 0, C)]

        def units():
            return [(n, n // PAIRS, n % PAIRS) for n in range(UNITS)]

        MIX_S0, MIX_Y0 = FFN_SLOTS, len(PARTS) * KD
        OUT_S0 = MIX_S0 + PROJ_SLOTS + ADA_SLOTS
        GAIN_MIX, GAIN_Q, GAIN_KV, GAIN_B1 = 2 * KD, 3 * KD, 3 * KD + 2, 3 * KD + 3

        CONSTS = 6 + 5 * DEPTH + 1 + 9 + 2

        def state_slot(t, way):
            order = (list(range(TCT + TT - 1)), list(range(TCT))[::-1] + list(range(TCT + 1, TCT + TT))[::-1])[way]
            return order.index(t) if t in order else None

        def states_before(t):
            return sum(state_slot(i, way) is not None for i in range(t) for way in range(2))

        def halves(hi, lo):
            return (lambda k: hi[:, k, :]), (lambda k: lo[:, k, :])

        def key_values(kind, h, m):
            if kind == "mla":
                return (lambda i: q_mla[0:MLA_QK, h, i]), (lambda n: k_mla[0:MLA_QK, h, 0:n]), (lambda b: v_mla[:, b, h * DV:(h + 1) * DV])
            if kind == "diff":
                r, c = 32 * ((2 * h + m) % 4), (2 * h + m) // 4
                return (lambda i: q_diff[r:r + 32, c, i]), (lambda n: k_diff[r:r + 32, c, 0:n]), (lambda b: v_diff[:, b, h * DV:(h + 1) * DV])
            g, c = h // 4, h % 4
            k, v = (k_slc, v_slc) if kind == "slc" else (k_win, v_win)
            r = DV * g
            return (lambda i: q_nsa[r:r + DV, c, i]), (lambda n: k[r:r + DV, 0:n]), (lambda b: v[:, b, r:r + DV])

        def last_turned(layer, t):
            return (probs_t_act, probs_t_dve)[t % 2](layer, t // 2 + 1)

        block = ctx.enter_context(nc.Block())

        @block.sync
        def _(sp):
            sp.dma_start(ident[:], a["c_ident"]).then_inc(x_rows_loaded, 16)
            sp.dma_start(x_rows[:], a["x"][0].rearrange("(t p) d -> p t d", p=P)).then_inc(x_rows_loaded, 16)
            sp.dma_start(ones[:], a["c_ones"]).then_inc(consts_loaded, 16)
            row = 0
            for dst, names in ((gain_rows, [(n, layer) for layer in range(DEPTH) for n in ("ffn_norm_g", "mix_norm_g", "mla_q_norm_g", "mla_kv_norm_g", "nsa_cmp_b1")]
                                + [("final_norm_g", None)]),
                               (gain_rows_2, [(n, None) for n in ("ada_b_2", "norm1_w_2", "norm2_w_2", "norm3_w_2", "final_norm_w_2",
                                                                  "ret_norm_w_2", "gla_norm_w_2", "c_2", "c_ctx_2")])):
                row = 0
                for name, layer in names:
                    src = a[name] if layer is None else a[name][layer]
                    while len(src.shape) > 1:
                        src = src.rearrange("a b ... -> (a b) ...") if len(src.shape) > 2 else src.rearrange("a b -> (a b)")
                    n = src.shape[0] // P
                    sp.dma_start(dst[row:row + n, :], src.rearrange("(r p) -> r p", p=P)).then_inc(consts_loaded, 16)
                    row += n
            for way, name in enumerate(("ret_decay_f_2", "ret_decay_b_2")):
                sp.dma_start(decay[:, way, :], a[name][0].partition_broadcast(P)).then_inc(consts_loaded, 16)
            sp.dma_start(rope[:], a["c_rope"]).then_inc(consts_loaded, 16)
            sp.dma_start(rotate[:], a["c_rotate"]).then_inc(consts_loaded, 16)
            sp.dma_start(causal[:], a["c_causal"]).then_inc(consts_loaded, 16)
            sp.dma_start(cmp_any[:], a["c_cmp_any"]).then_inc(consts_loaded, 16)
            sp.dma_start(lam_consts[:], a["c_lam"]).then_inc(consts_loaded, 16)

            def load_slot(turn, pos, dst, src):
                sp.wait_ge(lo_ready, turn * SLOTS + (pos + 1))
                sp.dma_start(dst, src).then_inc(slot_loaded[pos], 16)

            def slot_tile(pos, k=KD, n=P):
                return w_raw[:, pos, 0:k * n].rearrange("p (k n) -> p k n", k=k)

            def gate_and_up(turn, f, gate, up):
                for i in range(SLOTS):
                    load_slot(turn, i, slot_tile(i), (gate, up)[i % 2][:, :, bass.ds(f + i // 2 * P, P)])

            def ffn(layer, s, gate, up, down, done=0):
                for f0, nf in PARTS:
                    turn, _ = slot_of(layer, s)
                    with sp.Fori(done if f0 == 0 else 0, nf // 2) as it:
                        gate_and_up(turn + it, it * (2 * P) + f0 * P, gate, up)
                    s += 2 * nf
                    turn, _ = slot_of(layer, s)
                    with sp.Fori(0, KD // SLOTS) as it:
                        for i in range(SLOTS):
                            load_slot(turn + it, i, slot_tile(i, nf),
                                      down[:, f0:f0 + nf, bass.ds(it * (SLOTS * P) + i * P, P)])
                    s += KD

            def mixer(layer):
                w_in = a["w_in"].rearrange("l (k p) n -> l p k n", p=P)[layer]
                turn0, _ = slot_of(layer, MIX_S0)

                def load_mix(s, dst, src):
                    load_slot(turn0 + s // SLOTS, s % SLOTS, dst, src)

                def load_params():
                    sp.wait_ge(*x_updated(layer, MIX_Y0))
                    for dst, src in (
                            (cmp_mask[:], a["c_cmp_mask"]),
                            (swap[:], a["c_swap"]),
                            (lam_rows[:], a["diff_lambda"].rearrange("l m d -> l (m d)")[layer].partition_broadcast(P)),
                            (diff_gain[:], a["diff_norm_g"][layer].partition_broadcast(P)),
                            (gate_bias[:], a["nsa_gate_b"][layer].partition_broadcast(P)),
                            (pos_rows[:, 0:DV], a["nsa_cmp_pos"].rearrange("l v j d -> l (v j) d")[layer]),
                            (pos_rows[:, DV:P], a["nsa_cmp_pos"].rearrange("l v j d -> l (v j) d")[layer]),
                            (cmp_w2[:, 0], a["nsa_cmp_w2"].rearrange("l v (c p) d -> (l v) p c d", p=P)[layer * 2]),
                            (cmp_w2[:, 1], a["nsa_cmp_w2"].rearrange("l v (c p) d -> (l v) p c d", p=P)[layer * 2 + 1])):
                        sp.dma_start(dst, src).then_inc(params_loaded.sem, 16)

                def load_aux(n):
                    v, c = n // AUX_V, n % AUX_V * AUX_PAIRS
                    sp.wait_ge(*aux_used(layer, n + 1 - AUX_RING))
                    sp.dma_start(aux[:, n % AUX_RING, :].rearrange("p (c h) -> p c h", c=AUX_PAIRS),
                                 a["nsa_cmp_w1"].rearrange("l v (c p) h -> (l v) p c h", p=P)[layer * 2 + v][:, c:c + AUX_PAIRS, :]
                                 ).then_inc(aux_loaded[n % AUX_RING].sem, 16)

                for s in range(PROJ_SLOTS):
                    if s == SLOTS:
                        load_params()
                    if s < N_T:
                        kind, col, place = TILES[s]
                        if kind == "nq":
                            two = w_raw[:, s % SLOTS, :].rearrange("p (k g d) -> p k g d", k=KD, g=2)
                            col = IN_NQ + DV * place
                            load_mix(s, two[:, :, 0, :], w_in[:, :, col:col + DV])
                            sp.dma_start(two[:, :, 1, :], w_in[:, :, col + 256:col + 256 + DV]).then_inc(part_loaded[place].sem, 16)
                        else:
                            load_mix(s, slot_tile(s % SLOTS), w_in[:, :, col:col + P])
                    elif s < N_T + UQ_SLOTS:
                        n = 2 * MLA_QK
                        c = (s - N_T) * n
                        load_mix(s, slot_tile(s % SLOTS, 2, n), a["mla_w_uq"].rearrange("l (k p) n -> l p k n", p=P)[layer][:, :, c:c + n])
                    elif s < ROW_S0:
                        load_mix(s, w_raw[:, s % SLOTS, 0:512], a["mla_w_ukv"][layer])
                    else:
                        q = s - ROW_S0
                        for i, (col, at, n) in enumerate(ROWS):
                            dst = slot_tile(s % SLOTS, ROW_K, 4 * P)[:, :, at:at + n]
                            src = w_in[:, q * ROW_K:(q + 1) * ROW_K, col:col + n]
                            if i == 0:
                                load_mix(s, dst, src)
                            else:
                                sp.dma_start(dst, src).then_inc(part_loaded[q].sem, 16)
                    for n in AUX_AT.get(s - 2, ()):
                        load_aux(n)
                ada_w = a["ada_w_2"][0].rearrange("(k p) n -> p k n", p=P)
                with sp.Fori(0, ADA_SLOTS // SLOTS) as it:
                    for i in range(SLOTS):
                        load_slot(turn0 + PROJ_SLOTS // SLOTS + it, i, slot_tile(i, ADA_K, 2 * P),
                                  ada_w[:, i % 2 * ADA_K:(i % 2 + 1) * ADA_K,
                                        bass.ds(layer * (ADA_SLOTS * P) + it * (SLOTS * P) + i // 2 * 2 * P, 2 * P)])
                w_out = a["w_out"].rearrange("l (k p) n -> l p k n", p=P)[layer]
                for c in range(KD):
                    load_mix(PROJ_SLOTS + ADA_SLOTS + c, slot_tile((PROJ_SLOTS + ADA_SLOTS + c) % SLOTS), w_out[:, :, c * P:(c + 1) * P])

            ffn_gate = a["ffn_w_gate"].rearrange("l j (k p) f -> (l j) p k f", p=P)
            ffn_up = a["ffn_w_up"].rearrange("l j (k p) f -> (l j) p k f", p=P)
            ffn_down = a["ffn_w_down"].rearrange("l j (k p) f -> (l j) p k f", p=P)
            with sp.Fori(0, DEPTH) as layer:
                for j in range(2):
                    n = layer * 2 + j
                    ffn(layer, FFN_S0[j], ffn_gate[n], ffn_up[n], ffn_down[n])
                    if j == 0:
                        mixer(layer)

            f1, f2 = ([a[f"ffn{i}_w{j}_2"][0].rearrange("(k p) f -> p k f", p=P) for j in (1, 3, 2)] for i in (1, 2))
            gate_and_up(slot_of(LAST, S_FFN1)[0], 0, *f1[0:2])
            sp.wait_ge(*x_updated(LAST, 0))
            sp.dma_start(ctx_rows[:], a["ctx_2"][0].rearrange("(t p) d -> p t d", p=P)).then_inc(ctx_loaded, 16)
            sp.dma_start(grid[:], a["c_grid"]).then_inc(block2_loaded, 16)
            sp.dma_start(key_pos[:], a["c_key_pos"]).then_inc(block2_loaded, 16)
            ffn(LAST, S_FFN1, *f1, done=1)

            def load_mix_2(s, src, k=KD, n=P):
                turn, pos = slot_of(LAST, S_MIX2 + s)
                load_slot(turn, pos, slot_tile(pos, k, n), src)

            w_in_2 = a["w_in_2"][0].rearrange("(k p) n -> p k n", p=P)
            w_out_2 = a["w_out_2"][0].rearrange("(k p) n -> p k n", p=P)
            for s, (kind, j, k0, nk, n) in enumerate(SLOTS_2):
                c = IN_2[kind] + (j * P if nk == KD else 0)
                load_mix_2(s, w_in_2[:, k0:k0 + nk, c:c + n], nk, n)
            for c in range(SLOTS):
                load_mix_2(len(SLOTS_2) + c, w_out_2[:, :, c * P:(c + 1) * P])
            sp.wait_ge(gate_w_zeroed, 1)
            for way, name in enumerate(("f", "b")):
                at = slice(way * 2 * P, (way + 1) * 2 * P)
                sp.dma_start(gate_w[GATE_ROW + way * GLA_RANK:GATE_ROW + (way + 1) * GLA_RANK, at], a[f"gla_gate_w_{name}_2"][0]).then_inc(gate_w_loaded, 16)
                sp.dma_start(gate_b[:, at], a[f"gla_gate_b_{name}_2"][0].partition_broadcast(P)).then_inc(gate_w_loaded, 16)
            sp.wait_ge(roped_2, 2 * RET_H)
            sp.wait_ge(copied_2, N_2)
            sp.dma_start(distance[:], a["c_distance"]).then_inc(ret_consts_loaded, 16)
            sp.dma_start(row_pos[:], a["c_row_pos"]).then_inc(ret_consts_loaded, 16)
            sp.wait_ge(ret_state_done, 2)
            sp.dma_start(tri[:], a["c_tri"]).then_inc(tri_loaded, 16)
            for c in range(SLOTS, KD):
                load_mix_2(len(SLOTS_2) + c, w_out_2[:, :, c * P:(c + 1) * P])
            sp.wait_ge(ret_scores_ready, RET_H * TT)
            sp.dma_start(sums_raw[0][:], a["c_sums_f"]).then_inc(sums_loaded, 16)
            sp.wait_ge(ret_o_done, RET_H)
            sp.dma_start(sums_raw[1][:], a["c_sums_b"]).then_inc(sums_loaded, 16)
            sp.dma_start(masks[:], a["c_masks"]).then_inc(ret_consts_loaded, 16)
            ffn(LAST, S_FFN2, *f2)
            for t in range(TT):
                sp.wait_ge(y_rows_ready, t + 1)
                sp.dma_start(out[0, t * P:(t + 1) * P, :], y_rows[:, t % 2, :]).then_inc(stored[t % 2], 16)
            for t in range(2):
                sp.wait_ge(stored[t], 32)

        @block.gpsimd
        def _(pool):
            for i in range(SLOTS):
                nc.gpsimd.memset(w_raw[:, i, :], 0.0).then_inc(lo_ready, 1)
            with pool.Fori(0, SLOTS_ALL // SLOTS) as turn:
                for i in range(SLOTS):
                    pool.wait_ge(hi_ready, turn * SLOTS + (i + 1))
                    nc.gpsimd.tensor_tensor(w_lo[:, i, :], w_raw[:, i, :], w_hi[:, i, :].bitcast(F32),
                                            ALU.subtract).then_inc(lo_ready, 1)

        @block.scalar
        def _(act):
            def split(turn, pos):
                act.wait_ge(slot_loaded[pos], turn * 16 + 16)
                act.wait_ge(slot_used, turn * SLOTS + (pos + 1))
                nc.scalar.activation(w_hi[:, pos, :], w_raw[:, pos, :], ACT.Copy).then_inc(hi_ready, 1)

            def square(layer, v, y, c, groups):
                act.wait_ge(*x_updated(layer, y - KD + c + 1))
                act.wait_ge(*sq_used(layer, v * (KD - 1) + (0 if c < 2 else max(1, c - 2))))
                for x, o, n in groups:
                    last = nc.scalar.activation(squares[:, c % 2, o:o + n], x[:, c, :], ACT.Square)
                last.then_inc(sq_ready.sem, 1)

            def norm_statistics(layer, v, y, groups, done=0):
                for c in range(done, KD):
                    square(layer, v, y, c, groups)
                act.wait_ge(*sum_done(layer, v + 1))
                for g, (x, o, n) in enumerate(groups):
                    last = nc.scalar.activation(rstd[:, o:o + n], psum[:, g, 0:n], ACT.Abs_reciprocal_sqrt,
                                                bias=eps[:, 0:1], scale=-1.0 / D)
                last.then_inc(std_ready.sem, 1)
                act.wait_ge(*std_ready(layer, 2 * v + 1))
                nc.scalar.activation(squares[:, 0, 0:groups[-1][1] + groups[-1][2]], rstd[:, 0:groups[-1][1] + groups[-1][2]], ACT.Square,
                                     scale=(0.5 / D) ** 0.5).then_inc(std_ready.sem, 1)

            def norm_high(layer, v, groups, shift=None):
                for c in range(KD):
                    act.wait_ge(*normed_ready(layer, v * KD + c + 1))
                    for g, (hi, o, n) in enumerate(groups):
                        if shift is None:
                            last = nc.scalar.activation(hi[:, c, :], normed[:, c % 2, o:o + n], ACT.Copy)
                        else:
                            last = nc.scalar.activation(hi[:, c, :], normed[:, c % 2, o:o + n], ACT.Identity, bias=shift(c, g))
                    last.then_inc(h_hi_ready.sem, 1)

            def ffn(layer, s, f, groups, then, last_ffn=False):
                width = groups[-1][0] + groups[-1][2]
                for part, (f0, nf) in enumerate(PARTS):
                    turn, _ = slot_of(layer, s + SLOTS)
                    with act.Fori(0, nf // 2) as it:
                        for i in range(2):
                            split(turn + it, 2 * i)
                            split(turn + it, 2 * i + 1)
                            tile = it * 2 + (f + f0 + i)
                            act.wait_ge(slot_used, (turn + it) * SLOTS + (2 * i + 2))
                            for g, (o, _, n) in enumerate(groups):
                                last = nc.scalar.activation(silu_g[:, i, o:o + n], psum[:, 3 * i + 2 * g, 0:n], ACT.Silu)
                            last.then_inc(silu_done.sem, 1)
                            act.wait_ge(*gated_ready(layer, tile + 1))
                            nc.scalar.activation(a_hi[:, bass.ds(it * 2 + i, 1), 0:width], gated[:, i:i + 1, 0:width],
                                                 ACT.Copy).then_inc(a_hi_ready.sem, 1)
                    s += 2 * nf
                    turn, _ = slot_of(layer, s + SLOTS)
                    if part < len(PARTS) - 1:
                        with act.Fori(0, KD // SLOTS) as it:
                            for i in range(SLOTS):
                                split(turn + it, i)
                    else:
                        for c in range(KD):
                            if c < SLOTS or not last_ffn:
                                split(turn + c // SLOTS, c % SLOTS)
                            if c:
                                then(c - 1)
                    s += KD

            def mixer_projections(layer):
                turn0, _ = slot_of(layer, MIX_S0 + SLOTS)
                ropes = 0

                def copy(dst, src, scale=1.0):
                    return nc.scalar.activation(dst, src, ACT.Copy, scale=scale).then_inc(copied.sem, 1)

                def used(s):
                    act.wait_ge(slot_used, (turn0 - 1) * SLOTS + (SLOTS + s + 1))

                def copy_hidden(v):
                    act.wait_ge(*aux_used(layer, (v + 1) * AUX_V))
                    if v:
                        act.wait_ge(*hid_turned(layer, 1))
                    nc.scalar.activation(hid_rows[:], psum[0:NC, 4:6, 0:CMP_HID], ACT.Copy).then_inc(hid_copied.sem, 1)

                def hidden(v):
                    act.wait_ge(*hid_turned(layer, v + 1))
                    for half in range(2):
                        last = nc.scalar.activation(cmp_hid[:, v, half, :, :], psum[:, 6, half * 64:(half + 1) * 64].rearrange("p (g n) -> p g n", g=2)[:, :, 0:NC],
                                                    ACT.Silu, bias=layer_gains[:, GAIN_B1 + 2 * v + half:GAIN_B1 + 2 * v + half + 1])
                    last.then_inc(hid_ready.sem, 1)

                def next_split(s):
                    ahead = s + SLOTS
                    if ahead < N_T and TILES[ahead][0] == "nq":
                        act.wait_ge(*part_loaded[TILES[ahead][2]](layer, 16))
                    if ROW_S0 <= ahead < PROJ_SLOTS:
                        act.wait_ge(*part_loaded[ahead - ROW_S0](layer, 48))
                    split(turn0 + s // SLOTS, s % SLOTS)

                for s in range(N_T):
                    if s == KEYS_AT + AUX_V // 2:
                        copy_hidden(0)
                    if s == VALUES_AT + 1:
                        hidden(0)
                    if s == VALUES_AT + AUX_V // 2:
                        copy_hidden(1)
                    next_split(s)
                    used(s)
                    bank = psum[:, s % 2, :]
                    kind, _, place = TILES[s]
                    if kind in ROPED or kind == "ng":
                        if ropes >= 2:
                            act.wait_ge(*roped(layer, ropes - 1))
                        scale = DV ** -0.5 if kind == "nq" else DIFF_QK ** -0.5 if kind == "dq" else 1.0
                        copy(rope_in[:, ropes % 2, :], bank, scale)
                        ropes += 1
                    else:
                        copy(latents[:, place, :] if kind == "cq" else tok_cmp[:, 1, :], bank)
                    if s == 1:
                        act.wait_ge(*copied(layer, 2))
                        for c in range(2):
                            last = nc.scalar.activation(squares.rearrange("p a n -> p (a n)")[:, c * T:(c + 1) * T], latents[:, c, :], ACT.Square)
                        last.then_inc(latent_sq.sem, 1)
                    if s == 2:
                        act.wait_ge(*copied(layer, 3))
                        nc.scalar.activation(squares.rearrange("p a n -> p (a n)")[:, 2 * T:3 * T], latents[:, 2, :],
                                             ACT.Square).then_inc(latent_sq.sem, 1)
                    if s == 3:
                        act.wait_ge(*latent_sum(layer, 1))
                        nc.scalar.activation(rstd[:, 0:T], psum[:, 2, :], ACT.Sqrt, bias=eps[:, 0:1],
                                             scale=1.0 / MLA_QR).then_inc(latent_std.sem, 1)
                    if s == 4:
                        act.wait_ge(*latent_sum(layer, 2))
                        nc.scalar.activation(squares[:, 0, 0:T], psum[:, 3, :], ACT.Sqrt, bias=eps[:, 0:1],
                                             scale=1.0 / MLA_KVR).then_inc(latent_std.sem, 1)
                        act.wait_ge(*lam_step(layer, 3))
                        nc.scalar.activation(lam_stats[:, 2:4], lam_stats[:, 0:2], ACT.Exp).then_inc(lam_exp.sem, 1)
                    if s == 5:
                        for c in range(3):
                            act.wait_ge(*latent_normed(layer, c + 1))
                            nc.scalar.activation(latents_hi[:, c, :], normed[:, c % 2, 0:T], ACT.Copy).then_inc(latent_hi_ready.sem, 1)
                hidden(1)
                for s in range(N_T, ROW_S0):
                    if s == ROW_S0 - 1:
                        act.wait_ge(*turn_read(layer, GATE_EVENT))
                        nc.scalar.activation(gates[:], gates[:], ACT.Exp, scale=-1.0).then_inc(gate_exp.sem, 1)
                    n0 = 2 * (s - N_T)
                    for n in range(n0, n0 + 2) if s < ROW_S0 - 1 else range(n0, LATE_ITEMS):
                        if n in SLOT_ENDS:
                            used(s)
                        else:
                            act.wait_ge(*item_done(layer, n + 1 - sum(e < n for e in SLOT_ENDS)))
                        bank = psum[:, (N_T + n) % 2, :]
                        if n < MLA_H:
                            copy(q_mla[0:MLA_QK, n, :], bank[0:MLA_QK, :], MLA_QK ** -0.5)
                        elif n < 2 * MLA_H:
                            copy(k_mla[0:MLA_NOPE, n - MLA_H, :], bank[0:MLA_NOPE, :])
                        else:
                            t = 2 * (n - 2 * MLA_H)
                            copy(v_mla[:, t:t + 2, :], bank.rearrange("p (t n) -> p t n", t=2))
                    next_split(s)
                act.wait_ge(*cmp_kv_done(layer, 1))
                nc.scalar.activation(k_cmp[:], psum[:, 4, 0:NC], ACT.Copy)
                act.wait_ge(*lam_step(layer, 3))
                for r in range(4):
                    last = nc.scalar.activation(v_cmp[32 * r:32 * r + NC, :, r * DV:(r + 1) * DV],
                                                psum[32 * r:32 * r + NC, 5, 0:2 * DV].rearrange("p (g d) -> p g d", g=2), ACT.Copy)
                last.then_inc(cmp_kv_ready.sem, 1)
                for s in range(ROW_S0, PROJ_SLOTS - 1):
                    next_split(s)
                for t in range(TT):
                    if t < TT - 1:
                        act.wait_ge(*rows_done(layer, t + 1))
                    else:
                        used(PROJ_SLOTS - 1)
                    bank = psum[:, 4 + t, :]
                    nc.scalar.activation(v_diff[:, t, :], bank[:, 0:2 * P], ACT.Copy)
                    nc.scalar.activation(v_slc[:, t, :], bank[:, 2 * P:3 * P], ACT.Copy)
                    copy(v_win[:, t, :], bank[:, 3 * P:4 * P])
                next_split(PROJ_SLOTS - 1)

            def turn_o(layer, i):
                for b in range(2):
                    act.wait_ge(*o_turned(layer, 2 * i + b + 1))
                    nc.scalar.activation(h_hi[:, 4 * b:4 * b + 4, i * P:(i + 1) * P], psum[:, 6 + b, :].rearrange("p (c q) -> p c q", c=4),
                                         ACT.Copy).then_inc(o_hi_ready.sem, 1)

            def attention(layer):
                for t in range(ATT + 1):
                    i, step = t // NH, t % NH
                    if t < ATT:
                        act.wait_ge(*max_ready(layer, t + 1))
                        if t >= 2:
                            act.wait_ge(*probs_turned(layer, t - 1))
                        n = (i + 1) * P
                        nc.scalar.activation(probs[:, t % 2, 0:n], psum[:, t % 2, 0:n], ACT.Exp, bias=neg_max[:, t:t + 1],
                                             accum_out=exp_sum[:, t:t + 1]).then_inc(exp_ready.sem, 1)
                        if step == AT_TURN + 1 and i > 0:
                            turn_o(layer, i - 1)
                        if step == AT_CMP + 2:
                            act.wait_ge(*cmp_step(layer, 2 + 7 * i + 3))
                            nc.scalar.activation(cmp_p[:, :, 0:NC], cmp_p[:, :, 0:NC], ACT.Exp).then_inc(cmp_exp.sem, 1)
                        if step == AT_DIFF + 2:
                            act.wait_ge(*diff_step(layer, 4 * i + 2))
                            nc.scalar.activation(diff_stats[:], diff_stats[:], ACT.Sqrt, bias=eps[:, 0:1],
                                                 scale=1.0 / DV).then_inc(diff_std.sem, 1)
                    p = t - 1
                    if t >= 1 and p % 2 == 0:
                        act.wait_ge(*probs_turned(layer, p + 1))
                        if p >= 2:
                            act.wait_ge(*o_done(layer, p - 1))
                        n = (p // NH + 1) * P
                        nc.scalar.activation(probs_t[:, 0, 0:n], psum[:, 2, 0:n], ACT.Copy).then_inc(probs_t_act.sem, 1)
                    for half in range(2):
                        if t - 4 - half in ADA_AT:
                            turn, pos = slot_of(layer, MIX_S0 + PROJ_SLOTS + 2 * ADA_AT[t - 4 - half] + half + SLOTS)
                            split(turn, pos)
                turn_o(layer, TT - 1)

            def mixer_output(layer):
                for c in range(KD):
                    turn, pos = slot_of(layer, OUT_S0 + SLOTS + c)
                    split(turn, pos)
                    if c:
                        square(layer, 2, FFN_Y0[1], c - 1, [(x_lat, 0, T)])

            act.wait_ge(eps_set, 1)
            rows = [(x_lat, 0, T)]
            for c in range(KD - 1):
                square(0, 0, 0, c, rows)
            act.wait_ge(gains_ready, 1)
            nc.scalar.activation(cond[:], gains_2[:, ROW_COND:ROW_COND + 2 * KD].rearrange("p (g c) -> p c g", g=2), ACT.Silu).then_inc(cond_step, 1)
            act.wait_ge(cond_step, 1)
            nc.scalar.activation(cond_halves[:, :, 0, :], cond[:], ACT.Copy).then_inc(cond_step, 1)
            for i in range(SLOTS):
                split(0, i)
            with act.Fori(0, DEPTH) as layer:
                norm_statistics(layer, 0, 0, rows, KD - 1)
                norm_high(layer, 0, [(h_hi, 0, T)])
                ffn(layer, FFN_S0[0], FFN_N0[0], LAT, lambda c: square(layer, 1, MIX_Y0, c, rows))
                norm_statistics(layer, 1, MIX_Y0, rows, KD - 1)
                norm_high(layer, 1, [(h_hi, 0, T)])
                mixer_projections(layer)
                attention(layer)
                mixer_output(layer)
                norm_statistics(layer, 2, FFN_Y0[1], rows, KD - 1)
                norm_high(layer, 2, [(h_hi, 0, T)])
                ffn(layer, FFN_S0[1], FFN_N0[1], LAT, lambda c: square(layer + 1, 0, 0, c, rows))
            norm_statistics(LAST, 0, 0, rows, KD - 1)

            act.wait_ge(ctx_ready, KD // 2)
            both = [(x_lat, 0, T), (x_ctx, T, C)]
            norm_statistics(LAST, 1, Y_FFN1, both)
            norm_high(LAST, 0, [(h_hi, 0, T), (h_ctx_hi, T, C)], lambda c, g: mod[:, g, c:c + 1])
            ffn(LAST, S_FFN1, 0, BOTH, lambda c: square(LAST, 2, Y_MIX2, c, both))
            norm_statistics(LAST, 2, Y_MIX2, both, KD - 1)
            norm_high(LAST, 1, [(h_hi, 0, T), (h_ctx_hi, T, C)], lambda c, g: mod[:, g, 3 * KD + c:3 * KD + c + 1])

            ropes = plain = 0
            for s in range(len(SLOTS_2)):
                outs = [o for o in OUTS_2 if o[0] == s]
                turn, pos = slot_of(LAST, S_MIX2 + s)
                for i, (_, kind, j, t, b) in enumerate(outs):
                    bank = psum[:, b, :]
                    if i == len(outs) - 1 or kind == "gates":
                        act.wait_ge(slot_used, turn * SLOTS + SLOTS + pos + 1)
                    else:
                        plain += 1
                        act.wait_ge(item_done_2, plain)
                    if kind in ROPED_2:
                        if ropes >= 2:
                            act.wait_ge(roped_2, ropes - 1)
                        last = nc.scalar.activation(squares[:, ropes % 2, 0:T], bank, ACT.Copy, scale=RET_DK ** -0.5 if kind == "rq" else 1.0)
                        ropes += 1
                    elif kind in ("gq", "gk"):
                        last = nc.scalar.activation((gq if kind == "gq" else gk)[:, j, :], bank, ACT.Copy, scale=GLA_DK ** -0.5 if kind == "gq" else 1.0)
                    elif kind in ("rg", "gg"):
                        last = nc.scalar.activation((rg if kind == "rg" else gg)[:, j, :], bank, ACT.Silu)
                    elif kind in ("gates", "gates_ctx"):
                        at = slice(0, T) if kind == "gates" else slice(T, TC)
                        act.wait_ge(roped_2, 2 * RET_H)
                        last = nc.scalar.activation(gate_in[:, at], bank[:, 0:at.stop - at.start], ACT.Copy)
                    else:
                        dst = {"rv": rv, "gv": gv, "rk_ctx": rk_ctx, "rv_ctx": rv_ctx, "gk_ctx": gk_ctx, "gv_ctx": gv_ctx}[kind]
                        n = dst.shape[2]
                        last = nc.scalar.activation(dst[:, t, :], bank[:, 0:n], ACT.Copy)
                    last.then_inc(copied_2, 1)
                turn, pos = slot_of(LAST, S_MIX2 + s + SLOTS)
                split(turn, pos)
                if s == len(SLOTS_2) - 5:
                    act.wait_ge(log_step, 1)
                    nc.scalar.activation(log_steps[:, 1, :], log_steps[:, 0, :], ACT.Exp).then_inc(log_exp, 1)
                if s == len(SLOTS_2) - 2:
                    act.wait_ge(key_step, 1)
                    nc.scalar.activation(key_decay[:], key_decay[:], ACT.Exp).then_inc(key_step, 1)

            act.wait_ge(ret_consts_loaded, 32)
            for h in range(RET_H):
                fwd, bwd = log_decay[:, 0, h:h + 1], log_decay[:, 1, h:h + 1]
                nc.scalar.activation(strip_mid[:, 0, h, :], distance[:, MID:MID + P], ACT.Exp, scale=fwd)
                nc.scalar.activation(strip_mid[:, 1, h, :], distance[:, MID:MID + P], ACT.Exp, scale=bwd)
                nc.scalar.activation(strip[:, h, 0:MID], distance[:, 0:MID], ACT.Exp, scale=bwd)
                nc.scalar.activation(strip[:, h, MID + P:STRIP], distance[:, MID + P:STRIP], ACT.Exp, scale=fwd).then_inc(strip_exp, 1)
            for way in range(2):
                act.wait_ge(ret_state_done, way + 1)
                nc.scalar.activation(ret_state[:, way], psum[:, way, :].rearrange("p (h e) -> p h e", h=RET_H), ACT.Copy).then_inc(ret_state_ready, 1)
            for half, tiles in enumerate(GATE_HALVES):
                act.wait_ge(gate_neg, half + 1)
                nc.scalar.activation(gate_tmp[:, tiles, :], gate_tmp[:, tiles, :], ACT.Exp).then_inc(gate_log, 1)
            for half, tiles in enumerate(GATE_HALVES):
                act.wait_ge(gate_log, half + 1)
                nc.scalar.activation(gate_tmp[:, tiles, :], gate_tmp[:, tiles, :], ACT.Ln, bias=1.0).then_inc(gate_log, 1)
            act.wait_ge(log_gates_ready, len(GATE_HALVES))
            for h in range(RET_H + 1):
                if h:
                    act.wait_ge(ret_o_done, h)
                if h < RET_H:
                    for way in range(2):
                        last = nc.scalar.activation(q_dec[:, way, :], row_pos[:, way, :], ACT.Exp, scale=log_decay[:, way, h:h + 1])
                    last.then_inc(q_exp_ready, 1)
                if h:
                    nc.scalar.activation(rq[:, h - 1, :], psum[:, 4 + (h - 1) % 2, :], ACT.Copy).then_inc(ret_o_ready, 1)

            nc.scalar.activation(q_twice[:], gq[:], ACT.Copy, scale=2.0)
            for p in range(PAIRS):
                act.wait_ge(gk_turned, p + 1)
                nc.scalar.activation(gk_rows[:, :, p * P:(p + 1) * P], psum[:, p, :].rearrange("p (t n) -> p t n", t=TT), ACT.Copy).then_inc(gk_rows_ready, 1)
            act.wait_ge(totals_done, 1)
            nc.scalar.activation(chunk_decay[:], psum[:, 2, 0:(TT + TCT) * PAIRS * 4].rearrange("p (n o) -> p n o", o=2), ACT.Exp,
                                 scale=1.0 / GLA_TAU).then_inc(totals_ready, 1)
            copies = 0

            def copy_states(t):
                nonlocal copies
                for way in range(2):
                    slot = state_slot(t, way)
                    if slot is None:
                        continue
                    copies += 1
                    act.wait_ge(state_done, copies)
                    for r in range(2):
                        rows = slice(GLA_DK * r, GLA_DK * (r + 1))
                        last = nc.scalar.activation(gla_state[rows, way, :, slot, :],
                                                    psum[rows, 6 + way, :].rearrange("p (q r e) -> p q r e", q=PAIRS, r=2)[:, :, r, :], ACT.Copy)
                    last.then_inc(state_copied, 1)

            for t in range(TT + TCT):
                act.wait_ge(suffix_done, t + 1)
                if t >= 2:
                    act.wait_ge(state_done, states_before(t - 1))
                nc.scalar.activation(gk_dec[:, t % 2, :, :], psum[:, 4 + t % 2, :].rearrange("p (w n) -> p w n", w=2), ACT.Exp,
                                     scale=1.0 / GLA_TAU).then_inc(suffix_exp, 1)
                if t >= 1:
                    copy_states(t - 1)
            copy_states(TT + TCT - 1)
            for c in range(TT):
                nc.scalar.activation(log_gates_hi[:, c, :], log_gates[:, TCT + c, :], ACT.Copy).then_inc(sums_act_ready, 1)
            act.wait_ge(sums_loaded, 32)
            for b in range(4):
                at = slice(b * 512, (b + 1) * 512)
                nc.scalar.activation(sums_f[:, at], sums_raw[0][:, at], ACT.Copy).then_inc(sums_act_ready, 1)

            def copy_gla(n, c, p):
                act.wait_ge(gla_o_done, n + 1)
                nc.scalar.activation(rk[:, 2 * p:2 * p + 2, c * P:(c + 1) * P], psum[:, 6:8, 0:P], ACT.Copy).then_inc(gla_o_ready, 1)

            for n, c, p in units():
                act.wait_ge(sums_done, n + 1)
                if n >= 2:
                    act.wait_ge(gla_o_done, n - 1)
                nc.scalar.activation(factors[:, n % 2].rearrange("p l n -> p (l n)"), psum[:, 0:4, :].rearrange("p b n -> p (b n)"), ACT.Exp,
                                     scale=1.0 / GLA_TAU).then_inc(factor_exp, 1)
                if n >= 2:
                    copy_gla(*units()[n - 2])
            copy_gla(*units()[UNITS - 2])

            for h in range(2 * RET_H + 2):
                if h < 2 * RET_H:
                    o = rq[:, h, :] if h < RET_H else rk[:, h - RET_H, :]
                    if h < RET_H:
                        act.wait_ge(centred, h + 1)
                    if h == 2:
                        copy_gla(*units()[UNITS - 1])
                    if h >= 2:
                        act.wait_ge(merge_sum, h - 1)
                    nc.scalar.activation(squares[:, h % 2, 0:T], o, ACT.Square).then_inc(merge_sq, 1)
                g = h - 1
                if 0 <= g < 2 * RET_H:
                    act.wait_ge(merge_sum, g + 1)
                    if g >= 2:
                        act.wait_ge(merge_normed, g - 1)
                    nc.scalar.activation(inv_2[:, g % 2, :], psum[:, 2 + g % 2, :], ACT.Abs_reciprocal_sqrt, bias=eps[:, 0:1], scale=1.0 / P).then_inc(merge_std, 1)
                    act.wait_ge(merge_std, 2 * g + 1)
                    nc.scalar.activation(gk[:, g % 2, :], inv_2[:, g % 2, :], ACT.Square, scale=(0.5 / P) ** 0.5).then_inc(merge_std, 1)
                g = h - 2
                if g >= 0:
                    act.wait_ge(merged, g + 1)
                    o = rq[:, g, :] if g < RET_H else rk[:, g - RET_H, :]
                    nc.scalar.activation(h_hi[:, g, :], o, ACT.Copy).then_inc(merge_hi, 1)
            for c in range(KD):
                turn, pos = slot_of(LAST, S_MIX2 + len(SLOTS_2) + SLOTS + c)
                split(turn, pos)
                if c:
                    square(LAST, 3, Y_FFN2, c - 1, rows)
            norm_statistics(LAST, 3, Y_FFN2, rows, KD - 1)
            norm_high(LAST, 2, [(h_hi, 0, T)], lambda c, g: mod[:, 0, 6 * KD + c:6 * KD + c + 1])
            ffn(LAST, S_FFN2, NF, LAT, lambda c: square(LAST, 4, Y_END, c, rows), last_ffn=True)
            norm_statistics(LAST, 4, Y_END, rows, KD - 1)
            for t in range(TT):
                act.wait_ge(out_turned, 2 * t + 2)
                if t >= 2:
                    act.wait_ge(stored[t % 2], 16)
                nc.scalar.activation(y_rows[:, t % 2, :].rearrange("p (b n) -> p b n", b=2),
                                     psum[:, 2 + 2 * (t % 2):4 + 2 * (t % 2), :], ACT.Copy).then_inc(y_rows_ready, 1)

        @block.vector
        def _(dve):
            for i in range(SLOTS):
                nc.vector.memset(w_hi[:, i, :].bitcast(F32), 0.0).then_inc(slot_used, 1)
            nc.vector.memset(cond_parts[:, 4 * KD:].bitcast(F32), 0.0)
            for i in range(2):
                for n, free in enumerate((copied, aux_used, turn_read, aux_used, gated_ready, a_lo_ready, h_lo_ready)):
                    nc.vector.memset(credits[:, 2 * n + i:2 * n + i + 1], 0.0).then_inc(free.sem, 1)
            nc.vector.memset(credits[:, 15:16], 0.0).then_inc(sq_used.sem, 1)
            nc.vector.memset(eps[:], EPS).then_inc(eps_set, 1)
            def norm_add(layer, v, c, width):
                dve.wait_ge(*sq_ready(layer, v * KD + c + 1))
                if c > 1:
                    dve.wait_ge(*sq_used(layer, v * (KD - 1) + c - 1))
                if c == 1:
                    last = nc.vector.scalar_tensor_tensor(rstd[:, 0:width], squares[:, 0, 0:width], -1.0, squares[:, 1, 0:width], ALU.mult, ALU.subtract)
                else:
                    last = nc.vector.tensor_tensor(rstd[:, 0:width], rstd[:, 0:width], squares[:, c % 2, 0:width], ALU.subtract)
                last.then_inc(sq_used.sem, 1)

            def inverse_root(layer, v, groups):
                dve.wait_ge(*std_ready(layer, 2 * v + 2))
                for g, (o, n) in enumerate(groups):
                    last = nc.vector.scalar_tensor_tensor(squares[:, 0, o:o + n], psum[:, g, 0:n], -D * EPS, squares[:, 0, o:o + n], ALU.add, ALU.mult)
                last.then_inc(rstd_ready.sem, 1)
                dve.wait_ge(*rstd_ready(layer, 2 * v + 1))
                nc.vector.scalar_tensor_tensor(rstd[:, 0:o + n], squares[:, 0, 0:o + n], 1.5, rstd[:, 0:o + n], ALU.add, ALU.mult).then_inc(rstd_ready.sem, 1)
                dve.wait_ge(*rstd_ready(layer, 2 * v + 2))

            for c in range(KD):
                dve.wait_ge(x_turned, c + 1)
                nc.vector.tensor_copy(x_lat[:, c, :], psum[:, c, :]).then_inc(x_updated.sem, 1)
                if c >= 2:
                    norm_add(0, 0, c - 1, T)
            dve.wait_ge(consts_loaded, CONSTS * 16)
            nc.vector.tensor_copy(ident_b[:], ident[:])
            nc.vector.tensor_copy(causal_b[:], causal[:])
            dve.wait_ge(gains_turned, 1)
            nc.vector.tensor_copy(gains_2[:], psum[:, 7, P + N_MOD * KD:2 * P])
            for g in range(2):
                nc.vector.tensor_copy(mod[:, g, :], psum[:, 7, P:P + N_MOD * KD])
            nc.vector.tensor_copy(gains[:, 0:70], psum[:, 7, 0:70]).then_inc(gains_ready, 1)
            dve.wait_ge(gains_ready, 1)
            dve.wait_ge(cond_step, 2)
            nc.vector.tensor_tensor(cond_halves[:, :, 1, :], cond[:], cond_halves[:, :, 0, :].bitcast(F32), ALU.subtract).then_inc(cond_ready, 1)
            nc.vector.tensor_tensor(cond_sum[:], ident[:, 0:2], ident[:, 2:4], ALU.add).then_inc(cond_ready, 1)

            def norm_apply(layer, v, gain, xs, u=None, shift=None):
                u = v if u is None else u
                width = sum(n for _, _, n, _, _ in xs)
                norm_add(layer, v, KD - 1, width)
                inverse_root(layer, v, [(o, n) for _, o, n, _, _ in xs])

                def low(c):
                    dve.wait_ge(*h_hi_ready(layer, u * KD + c + 1))
                    for g, (_, o, n, hi, lo) in enumerate(xs):
                        if shift is None:
                            last = nc.vector.tensor_tensor(lo[:, c, :], normed[:, c % 2, o:o + n],
                                                           hi[:, c, :].bitcast(F32), ALU.subtract)
                        else:
                            last = nc.vector.scalar_tensor_tensor(lo[:, c, :], normed[:, c % 2, o:o + n], shift(c, g),
                                                                  hi[:, c, :].bitcast(F32), ALU.add, ALU.subtract)
                    last.then_inc(h_lo_ready.sem, 1)

                for c in range(KD):
                    dve.wait_ge(*h_lo_ready(layer, u * KD + c - 1))
                    for g, (x, o, n, _, _) in enumerate(xs):
                        last = nc.vector.scalar_tensor_tensor(normed[:, c % 2, o:o + n], x[:, c, :], gain(c, g),
                                                              rstd[:, o:o + n], ALU.mult, ALU.mult)
                    last.then_inc(normed_ready.sem, 1)
                    if c >= 1:
                        low(c - 1)
                low(KD - 1)

            def ffn(layer, s, f, y, groups, gate_scale, then):
                width = groups[-1][0] + groups[-1][2]
                for part, (f0, nf) in enumerate(PARTS):
                    with dve.Fori(0, nf // 2) as it:
                        for i in range(2):
                            tile = it * 2 + (f + f0 + i)
                            dve.wait_ge(*silu_done(layer, tile + 1))
                            dve.wait_ge(*a_lo_ready(layer, tile - 1))
                            for g, (o, _, n) in enumerate(groups):
                                up = psum[:, 3 * i + 1, 0:n] if g == 0 else psum[:, 3 * i + 2, n:2 * n]
                                last = nc.vector.tensor_tensor(gated[:, i, o:o + n], silu_g[:, i, o:o + n], up, ALU.mult)
                            last.then_inc(gated_ready.sem, 1)
                            dve.wait_ge(*a_hi_ready(layer, tile + 1))
                            nc.vector.tensor_tensor(a_lo[:, bass.ds(it * 2 + i, 1), 0:width], gated[:, i:i + 1, 0:width],
                                                    a_hi[:, bass.ds(it * 2 + i, 1), 0:width].bitcast(F32),
                                                    ALU.subtract).then_inc(a_lo_ready.sem, 1)
                    s += 2 * nf
                    for c in range(KD):
                        turn, pos = slot_of(layer, s + c)
                        dve.wait_ge(slot_used, turn * SLOTS + (SLOTS + pos + 1))
                        for g, (o, x, n) in enumerate(groups):
                            acc = psum[:, 6 + c % 2, 0:n] if g == 0 else psum[:, 2 + 3 * (c % 2), 0:n]
                            last = nc.vector.scalar_tensor_tensor(x_lat[:, c, :] if g == 0 else x_ctx[:, c, :], acc,
                                                                  gate_scale(c, g), x_lat[:, c, :] if g == 0 else x_ctx[:, c, :],
                                                                  ALU.mult, ALU.add)
                        last.then_inc(x_updated.sem, 1)
                        if part == len(PARTS) - 1 and c >= 2:
                            then(c - 1)
                    s += KD
                    y += KD

            def mixer_projections(layer):
                events, ropes, aux_v = 0, 0, 0

                def roped_tile(x, rows, dsts):
                    nonlocal events, ropes
                    r0, n, dim = rows
                    dve.wait_ge(*rotated(layer, ropes + 1))
                    if ropes:
                        dve.wait_ge(*roped(layer, ropes))
                    else:
                        dve.wait_ge(*latent_lo_ready(layer, 3))
                    nc.vector.tensor_tensor(normed[r0:r0 + n, 0, 0:T], x, rope[r0:r0 + n, dim, :], ALU.mult)
                    nc.vector.tensor_tensor(normed[r0:r0 + n, 1, 0:T], psum[r0:r0 + n, 2 + events % 2, :], rope[r0:r0 + n, dim + 1, :],
                                            ALU.mult).then_inc(turn_read.sem, 1)
                    events += 1
                    dve.wait_ge(*turn_read(layer, events))
                    for dst in dsts:
                        last = nc.vector.tensor_tensor(dst, normed[r0:r0 + n, 0, 0:T], normed[r0:r0 + n, 1, 0:T], ALU.add)
                    last.then_inc(roped.sem, 1)
                    ropes += 1

                def block_taps(v):
                    nonlocal events
                    dve.wait_ge(*swapped(layer, v + 1))
                    dve.wait_ge(*pos_ready(layer, 1))
                    if v:
                        dve.wait_ge(*aux_used(layer, AUX_V))

                    def place(g, odd, x):
                        rows = slice(DV * odd, DV * (odd + 1))
                        for b in range(CMP_BLOCK // CMP_STRIDE):
                            half = CMP_STRIDE // 2
                            pos = pos_cols[rows, v * CMP_BLOCK + b * CMP_STRIDE:v * CMP_BLOCK + (b + 1) * CMP_STRIDE]
                            last = nc.vector.tensor_tensor(
                                taps[rows, g, b * half:(b + 1) * half, :].rearrange("p j n -> p n j"),
                                x[rows, b * CMP_STRIDE:(b + NC) * CMP_STRIDE].rearrange("p (n j o) -> p n j o", j=half, o=2)[:, :, :, odd],
                                pos.rearrange("p (a j o) -> p a j o", a=1, o=2)[:, :, :, odd].broadcast_to([DV, NC, half]), ALU.add)
                        return last

                    place(0, 1, psum[:, 2 + events % 2, :])
                    place(1, 0, psum[:, 2 + events % 2, :]).then_inc(turn_read.sem, 1)
                    events += 1
                    place(0, 0, tok_cmp[:, v, :])
                    place(1, 1, tok_cmp[:, v, :]).then_inc(taps_ready.sem, 1)

                nc.vector.memset(v_cmp[:], 0.0)
                dve.wait_ge(*params_loaded(layer, PARAMS * 16))
                pairs = lam_rows[:].rearrange("p (a b d) -> p a b d", a=2, b=2)
                products = diff_half[:].rearrange("p (a d) -> p a d", a=2)
                nc.vector.tensor_tensor(products, pairs[:, :, 0, :], pairs[:, :, 1, :], ALU.mult).then_inc(lam_step.sem, 1)
                dve.wait_ge(*lam_step(layer, 1))
                nc.vector.tensor_reduce(lam_stats[:, 0:2], products, AX_X, ALU.add).then_inc(lam_step.sem, 1)
                dve.wait_ge(*lam_step(layer, 2))
                nc.vector.tensor_scalar(diff_gain[:], diff_gain[:], lam_layer[:, 1:2], None, ALU.mult).then_inc(lam_step.sem, 1)
                dve.wait_ge(*pos_turned(layer, 1))
                nc.vector.tensor_copy(pos_cols[:], psum[:, 7, 0:2 * CMP_BLOCK]).then_inc(pos_ready.sem, 1)

                root_kv = squares[:, 0, 0:T]
                for n, root in enumerate((rstd[:, 0:T], root_kv)):
                    dve.wait_ge(*latent_std(layer, n + 1))
                    nc.vector.reciprocal(root, root).then_inc(turn_read.sem, 1)
                    events += 1
                dve.wait_ge(*turn_read(layer, 2))

                def latent_low(c):
                    dve.wait_ge(*latent_hi_ready(layer, c + 1))
                    nc.vector.tensor_tensor(latents_lo[:, c, :], normed[:, c % 2, 0:T], latents_hi[:, c, :].bitcast(F32),
                                            ALU.subtract).then_inc(latent_lo_ready.sem, 1)

                for c in range(3):
                    if c == 2:
                        latent_low(0)
                        dve.wait_ge(*latent_lo_ready(layer, 1))
                    nc.vector.scalar_tensor_tensor(normed[:, c % 2, 0:T], latents[:, c, :], layer_gains[:, GAIN_Q + c:GAIN_Q + c + 1],
                                                   rstd[:, 0:T] if c < 2 else root_kv, ALU.mult, ALU.mult).then_inc(latent_normed.sem, 1)
                latent_low(1)
                latent_low(2)
                dve.wait_ge(*lam_exp(layer, 1))
                nc.vector.scalar_tensor_tensor(lam_stats[:, 4:5], lam_stats[:, 3:4], lam_layer[:, 0:1], lam_stats[:, 2:3],
                                               ALU.subtract, ALU.subtract).then_inc(lam_step.sem, 1)

                places = {"nq": lambda j: q_nsa[:, j, :], "ks": lambda j: k_slc[:], "kw": lambda j: k_win[:],
                          "dq": lambda j: q_diff[:, j, :], "dk": lambda j: k_diff[:, j, :], "ck": lambda j: tok_cmp[:, 0, :]}
                for s, (kind, _, place) in enumerate(TILES):
                    if kind == "kr":
                        roped_tile(rope_in[0:MLA_ROPE, ropes % 2, :], (0, MLA_ROPE, 0), [k_mla[MLA_NOPE:MLA_QK, h, :] for h in range(MLA_H)])
                    elif kind in ROPED:
                        roped_tile(rope_in[:, ropes % 2, :], (0, P, 0 if kind in ("dq", "dk") else 2), [places[kind](place)])
                    if kind == "ck":
                        block_taps(0)
                    if s == VALUES_AT - 2:
                        block_taps(1)
                dve.wait_ge(*gates_turned_1(layer, 1))
                nc.vector.tensor_tensor(gates[:], psum[:, 2 + events % 2, :].rearrange("p (t n) -> p t n", t=TT)[:, :, GATE_AT:P],
                                        gate_bias[:].rearrange("p (o n) -> p o n", o=1).broadcast_to([P, TT, 3 * NSA_H]),
                                        ALU.add).then_inc(turn_read.sem, 1)
                events += 1
                for h in range(MLA_H):
                    x = q_mla[MLA_NOPE:MLA_QK, h, :]
                    roped_tile(x, (MLA_NOPE, MLA_ROPE, 0), [x])
                dve.wait_ge(*gate_exp(layer, 1))
                nc.vector.tensor_scalar(gates[:], gates[:], 1.0, None, ALU.add).then_inc(gate_step.sem, 1)
                dve.wait_ge(*gate_step(layer, 1))
                nc.vector.reciprocal(gates[:], gates[:]).then_inc(gate_step.sem, 1)

            def cmp_softmax(layer, i):
                n = 2 + 7 * i
                scores = cmp_p[:, :, 0:NC]

                def wide(x):
                    return x.rearrange("p (h o) -> p h o", o=1).broadcast_to([P, NSA_H, NC])

                dve.wait_ge(*cmp_scores_done(layer, i + 1))
                if i:
                    dve.wait_ge(*cmp_turned(layer, i))
                for g in range(NSA_G):
                    last = nc.vector.tensor_tensor(scores[:, 4 * g:4 * g + 4, :], psum[:, 6 + g, 0:4 * CMP_BLOCK].rearrange("p (h n) -> p h n", h=4)[:, :, 0:NC],
                                                   cmp_mask[:, i, :].rearrange("p (o n) -> p o n", o=1).broadcast_to([P, 4, NC]), ALU.add)
                last.then_inc(cmp_step.sem, 1)
                dve.wait_ge(*cmp_step(layer, n + 1))
                nc.vector.tensor_reduce(cmp_stats[:, 0, :], scores, AX_X, ALU.max).then_inc(cmp_step.sem, 1)
                dve.wait_ge(*cmp_step(layer, n + 2))
                nc.vector.tensor_tensor(scores, scores, wide(cmp_stats[:, 0, :]), ALU.subtract).then_inc(cmp_step.sem, 1)

            def cmp_sums(layer, i):
                n = 2 + 7 * i
                dve.wait_ge(*cmp_exp(layer, i + 1))
                nc.vector.tensor_reduce(cmp_stats[:, 1, :], cmp_p[:, :, 0:NC], AX_X, ALU.add).then_inc(cmp_step.sem, 1)
                dve.wait_ge(*cmp_step(layer, n + 4))
                nc.vector.reciprocal(cmp_stats[:, 1, :], cmp_stats[:, 1, :]).then_inc(cmp_step.sem, 1)
                dve.wait_ge(*cmp_step(layer, n + 5))
                nc.vector.tensor_tensor(cmp_stats[:, 2, :], cmp_stats[:, 1, :],
                                        gates[:, i, :].rearrange("p (h b) -> p h b", b=3)[:, :, 0], ALU.mult).then_inc(cmp_step.sem, 1)
                dve.wait_ge(*cmp_step(layer, n + 6))
                nc.vector.tensor_scalar(cmp_stats[:, 2, :], cmp_stats[:, 2, :], cmp_any[:, 0:1] if i == 0 else 1.0, None,
                                        ALU.mult).then_inc(cmp_step.sem, 1)
                dve.wait_ge(*cmp_turned(layer, i + 1))
                if i:
                    dve.wait_ge(*cmp_o_done(layer, i))
                nc.vector.tensor_copy(cmp_pt[:], psum[:, 7, 0:2 * P].rearrange("p (g q) -> p g q", g=2)).then_inc(cmp_pt_ready.sem, 1)

            def cmp_output(layer, i):
                dve.wait_ge(*cmp_o_done(layer, i + 1))
                dve.wait_ge(*cmp_step(layer, 2 + 7 * i + 7))
                if i >= 2:
                    dve.wait_ge(*o_turned(layer, 2 * (i - 1)))
                nc.vector.tensor_tensor(o_rows[:, i % 2, 2 * 256:].rearrange("p (h d) -> p h d", h=NSA_H),
                                        psum[:, 6, :].rearrange("p (h d) -> p h d", h=NSA_H),
                                        cmp_stats[:, 2, :].rearrange("p (h o) -> p h o", o=1).broadcast_to([P, NSA_H, DV]),
                                        ALU.mult).then_inc(cmp_o_ready.sem, 1)

            def diff_norm(layer, i, half):
                o = o_rows[:, i % 2, 256:512].rearrange("p (h d) -> p h d", h=DIFF_H)

                def wide(x):
                    return x.rearrange("p (h o) -> p h o", o=1).broadcast_to([P, DIFF_H, DV])

                if half == 0:
                    dve.wait_ge(*o_ready(layer, i * NH + MLA_H + 2 * DIFF_H))
                    nc.vector.tensor_tensor(diff_sq[:], o, o, ALU.mult).then_inc(diff_step.sem, 1)
                    dve.wait_ge(*diff_step(layer, 4 * i + 1))
                    nc.vector.tensor_reduce(diff_stats[:], diff_sq[:], AX_X, ALU.add).then_inc(diff_step.sem, 1)
                else:
                    dve.wait_ge(*diff_std(layer, i + 1))
                    nc.vector.reciprocal(diff_stats[:], diff_stats[:]).then_inc(diff_step.sem, 1)
                    dve.wait_ge(*diff_step(layer, 4 * i + 3))
                    nc.vector.tensor_tensor(o, o, wide(diff_stats[:]), ALU.mult).then_inc(diff_step.sem, 1)
                    dve.wait_ge(*diff_step(layer, 4 * i + 4))
                    nc.vector.tensor_tensor(o, o, diff_gain[:].rearrange("p (o d) -> p o d", o=1).broadcast_to([P, DIFF_H, DV]),
                                            ALU.mult).then_inc(diff_ready.sem, 1)

            def turn_o(layer, i):
                for b in range(2):
                    dve.wait_ge(*o_hi_ready(layer, 2 * i + b + 1))
                    at = slice(i * P, (i + 1) * P)
                    nc.vector.tensor_tensor(h_lo[:, 4 * b:4 * b + 4, at], psum[:, 6 + b, :].rearrange("p (c q) -> p c q", c=4),
                                            h_hi[:, 4 * b:4 * b + 4, at].bitcast(F32), ALU.subtract).then_inc(o_lo_ready.sem, 1)

            def attention(layer):
                scaled = 0

                def head_output(p):
                    nonlocal scaled
                    i, (kind, h, m) = p // NH, HEADS[p % NH]
                    dve.wait_ge(*o_done(layer, p + 1))
                    beside = psum[:, 4 + p % 2, DV:DV + 2 * P]
                    if p in ADA_AT:
                        nc.vector.tensor_copy(mod_rows[:], beside[0:COND_M, :])
                    if p - 2 in ADA_AT:
                        at = bass.ds(layer * ADA_SLOTS + 2 * ADA_AT[p - 2], 2)
                        nc.vector.tensor_tensor(mod[:, :, at], beside.rearrange("p (a g) -> p g a", a=2)[:, 0:2, :], mod[:, :, at], ALU.add)
                    nc.vector.reciprocal(exp_sum[:, p:p + 1], exp_sum[:, p:p + 1]).then_inc(inv_ready.sem, 1)
                    dve.wait_ge(*inv_ready(layer, p + 1))
                    o = psum[:, 4 + p % 2, 0:DV]
                    factor = exp_sum[:, p:p + 1]
                    if kind in ("slc", "win") or m == 1:
                        by = lam_stats[:, 4:5] if m else gates[:, i, 3 * h + (1 if kind == "slc" else 2):3 * h + (2 if kind == "slc" else 3)]
                        factor = scaled_inv[:, p:p + 1]
                        nc.vector.tensor_tensor(factor, exp_sum[:, p:p + 1], by, ALU.mult).then_inc(scaled_ready.sem, 1)
                        scaled += 1
                        dve.wait_ge(*scaled_ready(layer, scaled))
                    at = {"mla": 0, "diff": 256, "slc": 512, "win": 512}[kind] + DV * h
                    dst = o_rows[:, i % 2, at:at + DV]
                    if kind == "mla" or (kind == "diff" and m == 0):
                        if i >= 2 and p % NH == 0:
                            dve.wait_ge(*o_turned(layer, 2 * (i - 1)))
                        if kind == "diff" and p % NH > MLA_H:
                            dve.wait_ge(*o_ready(layer, p))
                        nc.vector.tensor_scalar(dst if kind == "mla" else diff_half[:], o, factor, None, ALU.mult).then_inc(o_ready.sem, 1)
                    else:
                        if kind == "slc":
                            dve.wait_ge(*cmp_o_ready(layer, i + 1))
                        else:
                            dve.wait_ge(*o_ready(layer, p if m else p - NSA_H + 1))
                        nc.vector.scalar_tensor_tensor(dst, o, factor, diff_half[:] if m else dst, ALU.mult, ALU.add).then_inc(o_ready.sem, 1)

                nc.vector.memset(cmp_p[:], 0.0).then_inc(cmp_step.sem, 1)
                dve.wait_ge(*cmp_step(layer, 1))
                nc.vector.memset(cmp_stats[:], 0.0).then_inc(cmp_step.sem, 1)
                dve.wait_ge(*cmp_step(layer, 2))
                for t in range(ATT + 3):
                    i, step = t // NH, t % NH
                    if t < ATT:
                        dve.wait_ge(*scores_done(layer, t + 1))
                        nc.vector.tensor_reduce(neg_max[:, t:t + 1], psum[:, t % 2, 0:(i + 1) * P], AX_X, ALU.max,
                                                negate=True).then_inc(max_ready.sem, 1)
                    if t >= 3:
                        head_output(t - 3)
                    p = t - 1
                    if 1 <= p < ATT and p % 2 == 1:
                        dve.wait_ge(*probs_turned(layer, p + 1))
                        if p >= 2:
                            dve.wait_ge(*o_done(layer, p - 1))
                        n = (p // NH + 1) * P
                        nc.vector.tensor_copy(probs_t[:, 1, 0:n], psum[:, 3, 0:n]).then_inc(probs_t_dve.sem, 1)
                    if t < ATT:
                        if step == AT_TURN + 2 and i > 0:
                            turn_o(layer, i - 1)
                        if step == AT_CMP + 1:
                            cmp_softmax(layer, i)
                        if step == AT_CMP + 5:
                            cmp_sums(layer, i)
                        if step == AT_CMP + 7:
                            cmp_output(layer, i)
                        if step == AT_DIFF:
                            diff_norm(layer, i, 0)
                        if step == AT_DIFF + 4:
                            diff_norm(layer, i, 1)
                turn_o(layer, TT - 1)

            def mixer_output(layer):
                for c in range(KD):
                    turn, pos = slot_of(layer, OUT_S0 + c)
                    dve.wait_ge(slot_used, turn * SLOTS + (SLOTS + pos + 1))
                    nc.vector.tensor_tensor(x_lat[:, c, :], psum[:, 6 + c % 2, :], x_lat[:, c, :], ALU.add).then_inc(x_updated.sem, 1)
                    if c >= 2:
                        norm_add(layer, 2, c - 1, T)

            with dve.Fori(0, DEPTH) as layer:
                nc.vector.tensor_copy(lam_layer[:], lam_consts[:, bass.ds(layer * 2, 2)])
                nc.vector.tensor_copy(layer_gains[:], gains[:, bass.ds(layer * 31, 31)]).then_inc(layer_gains_ready.sem, 1)
                dve.wait_ge(*layer_gains_ready(layer, 1))
                lats = [(x_lat, 0, T, h_hi, h_lo)]
                norm_apply(layer, 0, lambda c, g: layer_gains[:, c:c + 1], lats)
                ffn(layer, FFN_S0[0], FFN_N0[0], FFN_Y0[0], LAT, lambda c, g: 0.5, lambda c: norm_add(layer, 1, c, T))
                norm_apply(layer, 1, lambda c, g: layer_gains[:, GAIN_MIX + c:GAIN_MIX + c + 1], lats)
                mixer_projections(layer)
                attention(layer)
                mixer_output(layer)
                norm_apply(layer, 2, lambda c, g: layer_gains[:, KD + c:KD + c + 1], lats)
                ffn(layer, FFN_S0[1], FFN_N0[1], FFN_Y0[1], LAT, lambda c, g: 0.5, lambda c: norm_add(layer + 1, 0, c, T))

            def final_norm(v, gain):
                norm_add(LAST, v, KD - 1, T)
                inverse_root(LAST, v, [(0, T)])
                for c in range(KD):
                    nc.vector.scalar_tensor_tensor(x_lat[:, c, :], x_lat[:, c, :], gain(c), rstd[:, 0:T], ALU.mult, ALU.mult).then_inc(x_updated.sem, 1)

            final_norm(0, lambda c: gains[:, 31 * DEPTH + c:31 * DEPTH + c + 1])

            nc.vector.tensor_scalar(merge_gains[:], gains_2[:, ROW_RET:ROW_RET + 2 * RET_H], -1.0, None, ALU.mult)
            for n in range(3):
                nc.vector.scalar_tensor_tensor(mod_gain[:, n], mod[:, :, (3 * n + 1) * KD:(3 * n + 2) * KD].rearrange("p g c -> p c g"), 1.0,
                                               gains_2[:, ROW_NORM + n * KD:ROW_NORM + (n + 1) * KD].rearrange("p (c o) -> p c o", o=1).broadcast_to([P, KD, 2]),
                                               ALU.add, ALU.mult)
                last = nc.vector.tensor_scalar(res[:, n], mod[:, :, (3 * n + 2) * KD:(3 * n + 3) * KD].rearrange("p g c -> p c g"), 1.0 if n == 1 else 0.5, None, ALU.mult)
            last.then_inc(mod_done, 1)
            for b in range(KD // 2):
                dve.wait_ge(ctx_turned, b + 1)
                nc.vector.tensor_copy(x_ctx[:, 2 * b:2 * b + 2, :], psum[:, 2 + b, :].rearrange("p (c n) -> p c n", c=2)).then_inc(ctx_ready, 1)
            dve.wait_ge(mod_done, 1)
            both = [(x_lat, 0, T, h_hi, h_lo), (x_ctx, T, C, h_ctx_hi, h_ctx_lo)]
            for c in range(1, KD - 1):
                norm_add(LAST, 1, c, TC)
            norm_apply(LAST, 1, lambda c, g: mod_gain[:, 0, c, g:g + 1], both, 0, lambda c, g: mod[:, g, c:c + 1])
            ffn(LAST, S_FFN1, 0, Y_FFN1, BOTH, lambda c, g: res[:, 0, c, g:g + 1], lambda c: norm_add(LAST, 2, c, TC))
            norm_apply(LAST, 2, lambda c, g: mod_gain[:, 1, c, g:g + 1], both, 1, lambda c, g: mod[:, g, 3 * KD + c:3 * KD + c + 1])

            for r in range(2 * RET_H):
                dve.wait_ge(rotated_2, r + 1)
                if r:
                    dve.wait_ge(roped_2, r)
                nc.vector.tensor_tensor(normed[:, 0, 0:T], squares[:, r % 2, 0:T], grid[:, 0, :], ALU.mult)
                nc.vector.tensor_tensor(normed[:, 1, 0:T], psum[:, 4 + r % 2, :], grid[:, 1, :], ALU.mult).then_inc(rot_read_2, 1)
                dve.wait_ge(rot_read_2, r + 1)
                dst = rk if r < RET_H else rq
                nc.vector.tensor_tensor(dst[:, r % RET_H, :], normed[:, 0, 0:T], normed[:, 1, 0:T], ALU.add).then_inc(roped_2, 1)
            flat = decay[:].rearrange("p w h -> p (w h)")
            lg = log_decay[:].rearrange("p w h -> p (w h)")
            a0, u, s, s2 = (log_steps[:, i, :] for i in range(4))
            nc.vector.scalar_tensor_tensor(a0, flat, -1.0, flat, ALU.mult, ALU.min).then_inc(log_step, 1)
            steps = 1

            def next_step(op):
                nonlocal steps
                op.then_inc(log_step, 1)
                steps += 1
                dve.wait_ge(log_step, steps)

            dve.wait_ge(log_exp, 1)
            next_step(nc.vector.tensor_scalar(s, u, 2.0, None, ALU.add))
            next_step(nc.vector.reciprocal(s, s))
            next_step(nc.vector.tensor_tensor(s, s, u, ALU.mult))
            next_step(nc.vector.tensor_tensor(s2, s, s, ALU.mult))
            next_step(nc.vector.tensor_scalar(a0, s2, 1.0 / 17.0, None, ALU.mult))
            for k in range(15, 1, -2):
                next_step(nc.vector.scalar_tensor_tensor(a0, a0, 1.0 / k, s2, ALU.add, ALU.mult))
            next_step(nc.vector.scalar_tensor_tensor(a0, a0, 1.0, s, ALU.add, ALU.mult))
            next_step(nc.vector.tensor_scalar(a0, a0, -2.0, None, ALU.mult))
            next_step(nc.vector.scalar_tensor_tensor(lg, flat, 0.0, a0, ALU.min, ALU.add))
            dve.wait_ge(block2_loaded, 32)
            nc.vector.tensor_tensor(key_decay[:], key_pos[:].rearrange("p w (t o) -> p w t o", o=1).broadcast_to([P, 2, TCT, RET_H]),
                                    log_decay[:].rearrange("p w (o h) -> p w o h", o=1).broadcast_to([P, 2, TCT, RET_H]), ALU.mult).then_inc(key_step, 1)
            dve.wait_ge(copied_2, N_2)
            nc.vector.memset(gate_w[:], 0.0).then_inc(gate_w_zeroed, 1)
            dve.wait_ge(key_step, 2)
            for way in range(2):
                for t in range(TCT):
                    last = nc.vector.tensor_tensor(ctx_keys[:, way, t, :].rearrange("p (h d) -> p h d", h=RET_H),
                                                   rk_ctx[:, t, :].rearrange("p (h d) -> p h d", h=RET_H),
                                                   key_decay[:, way, t, :].rearrange("p (h o) -> p h o", o=1).broadcast_to([P, RET_H, RET_DK]), ALU.mult)
            last.then_inc(ctx_keys_ready, 1)

            for half, tiles in enumerate(GATE_HALVES):
                for t in range(tiles.start, tiles.stop):
                    dve.wait_ge(gate_done, t + 1)
                    nc.vector.tensor_tensor(log_gates[:, t, :], psum[:, 6 + t % 2, :], gate_b[:], ALU.add).then_inc(gate_read, 1)
                dve.wait_ge(gate_read, tiles.stop)
                dve.wait_ge(ret_state_done, 2)
                nc.vector.scalar_tensor_tensor(gate_tmp[:, tiles, :], log_gates[:, tiles, :], -1.0, log_gates[:, tiles, :], ALU.mult, ALU.min).then_inc(gate_neg, 1)
            dve.wait_ge(strip_exp, RET_H)
            for way in range(2):
                side = distance[:, STRIP + way * P:STRIP + (way + 1) * P].rearrange("p (o n) -> p o n", o=1).broadcast_to([P, RET_H, P])
                last = nc.vector.tensor_tensor(strip_mid[:, way], strip_mid[:, way], side, ALU.mult)
            last.then_inc(strip_step, 1)
            dve.wait_ge(strip_step, 1)
            nc.vector.tensor_tensor(strip[:, :, MID:MID + P], strip_mid[:, 0], strip_mid[:, 1], ALU.add).then_inc(strip_ready, 1)
            for half, tiles in enumerate(GATE_HALVES):
                dve.wait_ge(gate_log, len(GATE_HALVES) + half + 1)
                nc.vector.scalar_tensor_tensor(log_gates[:, tiles, :], log_gates[:, tiles, :], 0.0, gate_tmp[:, tiles, :], ALU.min, ALU.subtract).then_inc(log_gates_ready, 1)
            dve.wait_ge(strip_ready, 1)
            dve.wait_ge(log_gates_ready, len(GATE_HALVES))
            for h in range(RET_H):
                if h:
                    dve.wait_ge(ret_o_done, h)
                for t in range(TT):
                    dve.wait_ge(ret_scores_done, h * TT + t + 1)
                    nc.vector.tensor_tensor(scores_r[:, t, :], psum[:, t, :], strip[:, h, MID - t * P:MID - t * P + T], ALU.mult).then_inc(ret_scores_ready, 1)
                dve.wait_ge(q_exp_ready, h + 1)
                nc.vector.tensor_tensor(q_dec[:], q_dec[:], rq[:, h:h + 1, :].broadcast_to([P, 2, T]), ALU.mult).then_inc(q_dec_ready, 1)

            for t in range(TT + TCT):
                dve.wait_ge(suffix_exp, t + 1)
                if t == TCT:
                    dve.wait_ge(gk_rows_ready, PAIRS)
                keys = gk_ctx[:, t:t + 1, :] if t < TCT else gk_rows[:, t - TCT:t - TCT + 1, :]
                nc.vector.tensor_tensor(gk_dec[:, t % 2], gk_dec[:, t % 2], keys.broadcast_to([P, 2, 2 * P]), ALU.mult).then_inc(gk_dec_ready, 1)
            for c in range(TT):
                dve.wait_ge(sums_act_ready, c + 1)
                nc.vector.tensor_tensor(log_gates_lo[:, c, :], log_gates[:, TCT + c, :], log_gates_hi[:, c, :].bitcast(F32), ALU.subtract).then_inc(sums_dve_ready, 1)
            dve.wait_ge(totals_ready, 1)
            dve.wait_ge(state_copied, states_before(TT + TCT))
            for i in range(1, STATES):
                if i > 1:
                    dve.wait_ge(state_step, i - 1)
                for way in range(2):
                    t = [t for t in range(TT + TCT) if state_slot(t, way) == i]
                    for p in range(PAIRS):
                        d = (t[0] * 2 + way) * PAIRS + p
                        last = nc.vector.scalar_tensor_tensor(gla_state[:, way, p, i, :], gla_state[:, way, p, i - 1, :], chunk_decay[:, d, 0:1],
                                                              gla_state[:, way, p, i, :], ALU.mult, ALU.add)
                last.then_inc(state_step, 1)
            dve.wait_ge(sums_loaded, 32)
            for b in range(4):
                at = slice(b * 512, (b + 1) * 512)
                nc.vector.tensor_copy(sums_b[:, at], sums_raw[1][:, at]).then_inc(sums_dve_ready, 1)
            dve.wait_ge(ret_consts_loaded, 48)
            merges = 0

            def gla_factors(n, c, p):
                dve.wait_ge(factor_exp, n + 1)
                at = slice(c * P, (c + 1) * P)
                q = gq[:, p:p + 1, at]
                f = factors[:, n % 2]
                nc.vector.tensor_tensor(f[:, 0:LEVELS + 1, :], f[:, 0:LEVELS + 1, :], q.broadcast_to([P, LEVELS + 1, P]), ALU.mult)
                nc.vector.tensor_tensor(f[:, 2 * LEVELS + 1, :], f[:, 2 * LEVELS + 1, :], gq[:, p, at], ALU.mult)
                nc.vector.tensor_tensor(f[:, LEVELS + 1:2 * LEVELS + 1, :], f[:, LEVELS + 1:2 * LEVELS + 1, :],
                                        gk[:, p:p + 1, at].broadcast_to([P, LEVELS, P]), ALU.mult).then_inc(factors_ready, 1)

            def gla_merge(n, half):
                nonlocal merges
                dve.wait_ge(gla_scores_done, 2 * n + half + 1)
                if half == 0 and n >= 2:
                    dve.wait_ge(gla_o_done, n - 1)
                for level in range(4 * half, 4 * half + 4):
                    if merges:
                        dve.wait_ge(gla_scores_step, merges)
                    nc.vector.copy_predicated(scores_g[:, n % 2], masks[:, level:level + 1, :].broadcast_to([P, 2, P]),
                                              psum[:, 4:6, level % 4 * P:(level % 4 + 1) * P]).then_inc(gla_scores_step, 1)
                    merges += 1

            def centre(h):
                dve.wait_ge(mean_done, h + 1)
                nc.vector.scalar_tensor_tensor(rq[:, h, :], psum[:, h % 2, :], -1.0 / P, rq[:, h, :], ALU.mult, ALU.add).then_inc(centred, 1)

            def merge_low(h):
                dve.wait_ge(merge_hi, h + 1)
                o = rq[:, h, :] if h < RET_H else rk[:, h - RET_H, :]
                nc.vector.tensor_tensor(h_lo[:, h, :], o, h_hi[:, h, :].bitcast(F32), ALU.subtract).then_inc(merge_lo, 1)

            gla_factors(*units()[0])
            for n, c, p in units():
                gla_merge(n, 0)
                if n + 1 < UNITS:
                    gla_factors(*units()[n + 1])
                else:
                    centre(0)
                    centre(1)
                gla_merge(n, 1)

            for h in range(2 * RET_H):
                o = rq[:, h, :] if h < RET_H else rk[:, h - RET_H, :]
                dve.wait_ge(merge_std, 2 * h + 2)
                nc.vector.scalar_tensor_tensor(gk[:, h % 2, :], psum[:, 2 + h % 2, :], P * EPS, gk[:, h % 2, :], ALU.add, ALU.mult).then_inc(merge_inv, 1)
                dve.wait_ge(merge_inv, 2 * h + 1)
                nc.vector.scalar_tensor_tensor(inv_2[:, h % 2, :], gk[:, h % 2, :], 1.5, inv_2[:, h % 2, :], ALU.subtract, ALU.mult).then_inc(merge_inv, 1)
                dve.wait_ge(merge_inv, 2 * h + 2)
                nc.vector.scalar_tensor_tensor(normed[:, h % 2, 0:T], o, merge_gains[:, h:h + 1], inv_2[:, h % 2, :],
                                               ALU.mult, ALU.mult).then_inc(merge_normed, 1)
                dve.wait_ge(merge_normed, h + 1)
                nc.vector.tensor_tensor(o, normed[:, h % 2, 0:T], rg[:, h, :] if h < RET_H else gg[:, h - RET_H, :], ALU.mult).then_inc(merged, 1)
                if h + 2 < RET_H:
                    centre(h + 2)
                if h:
                    merge_low(h - 1)
            merge_low(2 * RET_H - 1)
            for c in range(KD):
                turn, pos = slot_of(LAST, S_MIX2 + len(SLOTS_2) + c)
                dve.wait_ge(slot_used, turn * SLOTS + (SLOTS + pos + 1))
                nc.vector.scalar_tensor_tensor(x_lat[:, c, :], psum[:, 6 + c % 2, :], res[:, 1, c, 0:1], x_lat[:, c, :], ALU.mult, ALU.add).then_inc(x_updated.sem, 1)
                if c >= 2:
                    norm_add(LAST, 3, c - 1, T)
            norm_apply(LAST, 3, lambda c, g: mod_gain[:, 2, c, 0:1], [(x_lat, 0, T, h_hi, h_lo)], 2, lambda c, g: mod[:, 0, 6 * KD + c:6 * KD + c + 1])
            ffn(LAST, S_FFN2, NF, Y_FFN2, LAT, lambda c, g: res[:, 2, c, 0:1], lambda c: norm_add(LAST, 4, c, T))
            final_norm(4, lambda c: gains_2[:, ROW_FINAL + c:ROW_FINAL + c + 1])

        @block.tensor
        def _(pe):
            pe.wait_ge(x_rows_loaded, 32)
            for c in range(KD):
                for t in range(TT):
                    last = nc.tensor.transpose(psum[:, c, t * P:(t + 1) * P], x_rows[:, t, c * P:(c + 1) * P], ident[:])
                last.then_inc(x_turned, 1)
            pe.wait_ge(*x_updated(0, 0))
            pe.wait_ge(consts_loaded, CONSTS * 16)
            nc.tensor.transpose(psum[:, 7, 0:70], gain_rows[0:70, :], ident[0:70, 0:70])
            nc.tensor.transpose(psum[:, 7, P:2 * P], gain_rows_2[:], ident[:]).then_inc(gains_turned, 1)

            def norm_sums(layer, v, widths):
                pe.wait_ge(*sq_used(layer, (v + 1) * (KD - 1)))
                for g, (o, n) in enumerate(widths):
                    last = nc.tensor.matmul(psum[:, g, 0:n], ones[:], rstd[:, o:o + n], start=True, stop=True)
                last.then_inc(sum_done.sem, 1)

            def rows_ready(layer, v):
                return lambda k: pe.wait_ge(*h_lo_ready(layer, v * KD + k + 1))

            def dense(pos, k0, nk, rhs, outs, before=None):
                for k in range(nk):
                    if before is not None:
                        before(k)
                    for m, (w, r) in enumerate(((w_hi, 0), (w_hi, 1), (w_lo, 0))):
                        for g, dst in enumerate(outs):
                            last = nc.tensor.matmul(dst, w[:, pos, k * P:(k + 1) * P], rhs[g][r](k0 + k),
                                                    start=k == 0 and m == 0, stop=k == nk - 1 and m == 2)
                return last

            def ffn(layer, v, s, f, y, groups, rhs):
                for part, (f0, nf) in enumerate(PARTS):
                    turn, _ = slot_of(layer, s)
                    with pe.Fori(0, nf // 2) as it:
                        for i in range(2):
                            tile = it * 2 + (f + f0 + i)
                            if len(groups) > 1:
                                pe.wait_ge(*x_updated(layer, y - 1 + i))
                            pe.wait_ge(*gated_ready(layer, tile - 1))
                            for u in range(2):
                                pe.wait_ge(lo_ready, (turn + it) * SLOTS + (SLOTS + 2 * i + u + 1))
                                outs = [psum[:, 3 * i + u, 0:n] if g == 0 else psum[:, 3 * i + 2, u * n:u * n + n]
                                        for g, (_, _, n) in enumerate(groups)]
                                last = dense(2 * i + u, 0, KD, rhs, outs, rows_ready(layer, v) if part == i == u == 0 else None)
                                last.then_inc(slot_used, 1)
                    s += 2 * nf
                    turn, _ = slot_of(layer, s)
                    with pe.Fori(0, KD // SLOTS) as it:
                        def activations(k):
                            if k == 0 or k >= nf - 2:
                                pe.wait_ge(*a_lo_ready(layer, f + f0 + max(k, nf - 3) + 1))

                        for i in range(SLOTS):
                            pe.wait_ge(lo_ready, (turn + it) * SLOTS + (SLOTS + i + 1))
                            if len(groups) > 1 and i < 2:
                                pe.wait_ge(*gated_ready(layer, f + f0 + nf - 1 + i))
                            pe.wait_ge(*x_updated(layer, it * SLOTS + (y + i - 1)))
                            outs = [psum[:, 6 + i % 2, 0:n] if g == 0 else psum[:, 2 + 3 * (i % 2), 0:n]
                                    for g, (_, _, n) in enumerate(groups)]
                            last = dense(i, 0, nf, [tuple((lambda k, h=h, o=o, n=n: h[:, k, o:o + n]) for h in (a_hi, a_lo))
                                                    for o, _, n in groups], outs, activations if i == 0 else None)
                            last.then_inc(slot_used, 1)
                    s += KD
                    y += KD

            def mixer_projections(layer):
                turn0, _ = slot_of(layer, MIX_S0)
                events, ropes = 0, 0
                flat = squares[:].rearrange("p a n -> p (a n)")

                def weights(s):
                    pe.wait_ge(lo_ready, (turn0 + s // SLOTS) * SLOTS + (SLOTS + s % SLOTS + 1))

                def bank_of(n):
                    pe.wait_ge(*copied(layer, n - 1))
                    return psum[:, n % 2, :]

                def turn_bank():
                    nonlocal events
                    pe.wait_ge(*turn_read(layer, events - 1))
                    events += 1
                    return 2 + (events - 1) % 2

                def latent_sums(n):
                    pe.wait_ge(*latent_sq(layer, n + 1))
                    b = turn_bank()
                    chunks = ((0, 1), (2,))[n]
                    for c in chunks:
                        last = nc.tensor.matmul(psum[:, b, :], ones[:], flat[:, c * T:(c + 1) * T], start=c == chunks[0], stop=c == chunks[-1])
                    last.then_inc(latent_sum.sem, 1)

                def rotation(item, x, rows, m):
                    nonlocal ropes
                    pe.wait_ge(*copied(layer, item + 1))
                    b = turn_bank()
                    nc.tensor.matmul(psum[rows, b, :], rotate[rows, m, rows], x, start=True, stop=True).then_inc(rotated.sem, 1)
                    ropes += 1

                def rotate_tile(s):
                    kind = TILES[s][0]
                    rotation(s, rope_in[:, ropes % 2, :], slice(0, P), 0 if kind in ("kr", "dq", "dk") else 1)

                def compress(n):
                    v = n // AUX_V
                    pe.wait_ge(*aux_loaded[n % AUX_RING](layer, (n // AUX_RING + 1) * 16))
                    if n % AUX_V == 0:
                        pe.wait_ge(*taps_ready(layer, v + 1))
                        if v:
                            pe.wait_ge(*hid_copied(layer, 1))
                    for j in range(AUX_PAIRS):
                        pair = n % AUX_V * AUX_PAIRS + j
                        for g in range(2):
                            last = nc.tensor.matmul(psum[0:NC, 4 + g, 0:CMP_HID], taps[:, g, pair, :], aux[:, n % AUX_RING, j * CMP_HID:(j + 1) * CMP_HID],
                                                    start=pair == 0, stop=pair == PAIR_TAPS - 1)
                    last.then_inc(aux_used.sem, 1)

                def swap_tokens(v):
                    pe.wait_ge(*(roped(layer, 2) if v == 0 else copied(layer, 6)))
                    nc.tensor.matmul(psum[:, turn_bank(), :], swap[:], tok_cmp[:, v, :], start=True, stop=True).then_inc(swapped.sem, 1)

                def hidden_copied(v):
                    pe.wait_ge(*hid_copied(layer, v + 1))
                    if v:
                        pe.wait_ge(*hid_ready(layer, 1))

                def turn_hidden(v):
                    for half in range(2):
                        for g in range(2):
                            last = nc.tensor.transpose(psum[:, 6, (half * 2 + g) * 32:(half * 2 + g) * 32 + NC], hid_rows[:, g, half * P:(half + 1) * P],
                                                       ident[0:NC, 0:NC])
                    last.then_inc(hid_turned.sem, 1)

                pe.wait_ge(*params_loaded(layer, PARAMS * 16))
                pe.wait_ge(*x_updated(layer, MIX_Y0))
                for s in range(N_T):
                    if s == VALUES_AT:
                        hidden_copied(0)
                    weights(s)
                    dense(s % SLOTS, 0, KD, [lat], [bank_of(s)], rows_ready(layer, 1) if s == 0 else None).then_inc(slot_used, 1)
                    if s == 0:
                        nc.tensor.transpose(psum[:, 7, 0:2 * CMP_BLOCK], pos_rows[:], ident[0:2 * CMP_BLOCK, 0:2 * CMP_BLOCK]).then_inc(pos_turned.sem, 1)
                    if s in (2, 3):
                        latent_sums(s - 2)
                    if s >= 1 and TILES[s - 1][0] in ROPED:
                        rotate_tile(s - 1)
                    if s in (KEYS_AT - 1, VALUES_AT - 1):
                        swap_tokens(0 if s < KEYS_AT else 1)
                    if s == VALUES_AT:
                        turn_hidden(0)
                    for n in AUX_AT.get(s, ()):
                        compress(n)
                pe.wait_ge(*latent_lo_ready(layer, 3))
                halves3 = ((w_hi, latents_hi), (w_hi, latents_lo), (w_lo, latents_hi))
                for n in range(LATE_ITEMS):
                    s = N_T + n // 2 if n < MLA_H else ROW_S0 - 1
                    pos = s % SLOTS
                    if n == 0:
                        hidden_copied(1)
                    if n in (0, 2, MLA_H):
                        weights(s)
                    bank = bank_of(N_T + n)
                    if n < MLA_H:
                        for k in range(2):
                            for m, (w, x) in enumerate(halves3):
                                at = k * 2 * MLA_QK + n % 2 * MLA_QK
                                last = nc.tensor.matmul(bank[0:MLA_QK, :], w[:, pos, at:at + MLA_QK], x[:, k, :],
                                                        start=k == 0 and m == 0, stop=k == 1 and m == 2)
                    elif n < 2 * MLA_H:
                        at = (n - MLA_H) * P
                        for m, (w, x) in enumerate(halves3):
                            last = nc.tensor.matmul(bank, w[:, pos, at:at + P], x[:, 2, :], start=m == 0, stop=m == 2)
                    else:
                        for t in range(2):
                            tok = slice((2 * (n - 2 * MLA_H) + t) * P, (2 * (n - 2 * MLA_H) + t + 1) * P)
                            for m, (w, x) in enumerate(halves3):
                                last = nc.tensor.matmul(bank[:, t * 256:(t + 1) * 256], x[:, 2, tok],
                                                        w[:, pos, 0:512].rearrange("p (h n) -> p h n", h=MLA_H)[:, :, MLA_NOPE:],
                                                        start=m == 0, stop=m == 2)
                    last.then_inc(slot_used if n in SLOT_ENDS else item_done.sem, 1)
                    if n == 0:
                        turn_hidden(1)
                        pe.wait_ge(*copied(layer, N_T))
                        b = turn_bank()
                        for t in range(TT):
                            last = nc.tensor.transpose(psum[:, b, t * P:(t + 1) * P], rope_in[:, ropes % 2, t * P:(t + 1) * P], ident[:])
                        last.then_inc(gates_turned_1.sem, 1)
                    if 1 <= n <= MLA_H:
                        rotation(N_T + n - 1, q_mla[0:MLA_QK, n - 1, :], slice(0, MLA_QK), 0)
                pe.wait_ge(*hid_ready(layer, 2))
                for g in range(2):
                    for half in range(2):
                        nc.tensor.matmul(psum[DV * g:DV * (g + 1), 4, 0:NC], cmp_w2[:, 0, half, :], cmp_hid[:, 0, half, g, :],
                                         start=half == 0, stop=half == 1)
                for r in range(4):
                    for g in range(2):
                        for half in range(2):
                            last = nc.tensor.matmul(psum[32 * r:32 * r + NC, 5, g * DV:(g + 1) * DV], cmp_hid[:, 1, half, g, :],
                                                    cmp_w2[:, 1, half, :], start=half == 0, stop=half == 1)
                last.then_inc(cmp_kv_done.sem, 1)
                pe.wait_ge(*cmp_kv_ready(layer, 1))
                for q in range(N_R):
                    weights(ROW_S0 + q)
                    pos = (ROW_S0 + q) % SLOTS
                    for t in range(TT):
                        for k in range(ROW_K):
                            for m, (x, w) in enumerate(((h_hi, w_hi), (h_hi, w_lo), (h_lo, w_hi))):
                                last = nc.tensor.matmul(psum[:, 4 + t, :], x[:, q * ROW_K + k, t * P:(t + 1) * P], w[:, pos, k * 512:(k + 1) * 512],
                                                        start=q == 0 and k == 0 and m == 0, stop=q == N_R - 1 and k == ROW_K - 1 and m == 2)
                        if t == TT - 1:
                            last.then_inc(slot_used, 1)
                        elif q == N_R - 1:
                            last.then_inc(rows_done.sem, 1)

            def turn_o(layer, i):
                pe.wait_ge(*o_ready(layer, (i + 1) * NH))
                pe.wait_ge(*diff_ready(layer, i + 1))
                pe.wait_ge(*cmp_o_ready(layer, i + 1))
                for b in range(2):
                    for c in range(4):
                        last = nc.tensor.transpose(psum[:, 6 + b, c * P:(c + 1) * P], o_rows[:, i % 2, (4 * b + c) * P:(4 * b + c + 1) * P], ident[:])
                    last.then_inc(o_turned.sem, 1)

            def attention(layer):
                pe.wait_ge(*copied(layer, ITEMS))
                pe.wait_ge(*roped(layer, EVENTS - 5))
                pe.wait_ge(*turn_read(layer, EVENTS))
                pe.wait_ge(*cmp_kv_ready(layer, 1))
                pe.wait_ge(cond_ready, 2)
                for t in range(ATT + 2):
                    i, step = t // NH, t % NH
                    if t < ATT:
                        q, k, _ = key_values(*HEADS[step])
                        if t >= 2:
                            pe.wait_ge(*exp_ready(layer, t - 1))
                        n = (i + 1) * P
                        nc.tensor.matmul(psum[:, t % 2, 0:n], q(slice(i * P, (i + 1) * P)), k(n), start=True, stop=False)
                        nc.tensor.matmul(psum[:, t % 2, n - P:n], ident_b[:], causal_b[:], start=False, stop=True).then_inc(scores_done.sem, 1)
                        if step == AT_TURN and i > 0:
                            turn_o(layer, i - 1)
                        if step == AT_CMP:
                            if i:
                                pe.wait_ge(*o_lo_ready(layer, 2 * i))
                            for h in range(NSA_H):
                                g, c = h // 4, h % 4
                                rows = slice(DV * g, DV * (g + 1))
                                last = nc.tensor.matmul(psum[:, 6 + g, c * CMP_BLOCK:c * CMP_BLOCK + NC], q_nsa[rows, c, i * P:(i + 1) * P],
                                                        k_cmp[rows, :], start=True, stop=True)
                            last.then_inc(cmp_scores_done.sem, 1)
                        if step == AT_CMP + 4:
                            pe.wait_ge(*cmp_exp(layer, i + 1))
                            for g in range(2):
                                last = nc.tensor.transpose(psum[:, 7, g * P:(g + 1) * P],
                                                           cmp_p[:, 4 * g:4 * g + 4, :].rearrange("p h n -> p (h n)"), ident[:])
                            last.then_inc(cmp_turned.sem, 1)
                        if step == AT_CMP + 6:
                            pe.wait_ge(*cmp_pt_ready(layer, i + 1))
                            for g in range(NSA_G):
                                last = nc.tensor.matmul(psum[:, 6, g * 4 * DV:(g + 1) * 4 * DV], cmp_pt[:, g, :], v_cmp[:, g, :],
                                                        start=True, stop=True)
                            last.then_inc(cmp_o_done.sem, 1)
                    p = t - 1
                    if 0 <= p < ATT:
                        pe.wait_ge(*exp_ready(layer, p + 1))
                        if p >= 2:
                            pe.wait_ge(*last_turned(layer, p - 2))
                        for b in range(p // NH + 1):
                            last = nc.tensor.transpose(psum[:, 2 + p % 2, b * P:(b + 1) * P], probs[:, p % 2, b * P:(b + 1) * P], ident[:])
                        last.then_inc(probs_turned.sem, 1)
                    p = t - 2
                    if p >= 0:
                        _, _, v = key_values(*HEADS[p % NH])
                        pe.wait_ge(*last_turned(layer, p))
                        if p >= 2:
                            pe.wait_ge(*o_ready(layer, p - 1))
                        beside = psum[:, 4 + p % 2, DV:DV + 2 * P]
                        if p in ADA_AT:
                            for half in range(2):
                                turn, pos = slot_of(layer, MIX_S0 + PROJ_SLOTS + 2 * ADA_AT[p] + half)
                                pe.wait_ge(lo_ready, turn * SLOTS + (SLOTS + pos + 1))
                                for k in range(ADA_K):
                                    at = 4 * (half * ADA_K + k)
                                    for m, w in enumerate((w_hi, w_lo)):
                                        last = nc.tensor.matmul(beside[0:COND_M, :], cond_parts[:, at:at + COND_M], w[:, pos, k * 2 * P:(k + 1) * 2 * P],
                                                                start=half == 0 and k == 0 and m == 0, stop=half == 1 and k == ADA_K - 1 and m == 1)
                                last.then_inc(slot_used, 1)
                        if p - 2 in ADA_AT:
                            for b in range(2):
                                nc.tensor.matmul(beside[:, b * P:b * P + 2], mod_rows[:, b * P:(b + 1) * P], cond_sum[0:COND_M, :], start=True, stop=True)
                        for b in range(p // NH + 1):
                            last = nc.tensor.matmul(psum[:, 4 + p % 2, 0:DV], probs_t[:, p % 2, b * P:(b + 1) * P], v(b),
                                                    start=b == 0, stop=b == p // NH)
                        last.then_inc(o_done.sem, 1)
                turn_o(layer, TT - 1)

            def mixer_output(layer):
                pe.wait_ge(*o_lo_ready(layer, 2 * TT))
                for c in range(KD):
                    turn, pos = slot_of(layer, OUT_S0 + c)
                    pe.wait_ge(lo_ready, turn * SLOTS + (SLOTS + pos + 1))
                    if c >= 2:
                        pe.wait_ge(*x_updated(layer, MIX_Y0 + c - 1))
                    dense(pos, 0, KD, [lat], [psum[:, 6 + c % 2, :]]).then_inc(slot_used, 1)

            lat = halves(h_hi, h_lo)
            with pe.Fori(0, DEPTH) as layer:
                norm_sums(layer, 0, [(0, T)])
                ffn(layer, 0, FFN_S0[0], FFN_N0[0], FFN_Y0[0], LAT, [lat])
                norm_sums(layer, 1, [(0, T)])
                mixer_projections(layer)
                attention(layer)
                mixer_output(layer)
                norm_sums(layer, 2, [(0, T)])
                ffn(layer, 2, FFN_S0[1], FFN_N0[1], FFN_Y0[1], LAT, [lat])
            norm_sums(LAST, 0, [(0, T)])

            pe.wait_ge(ctx_loaded, 16)
            for c in range(KD):
                for t in range(TCT):
                    last = nc.tensor.transpose(psum[:, 2 + c // 2, (c % 2 * TCT + t) * P:(c % 2 * TCT + t + 1) * P], ctx_rows[:, t, c * P:(c + 1) * P], ident[:])
                if c % 2:
                    last.then_inc(ctx_turned, 1)
            context = halves(h_ctx_hi, h_ctx_lo)
            norm_sums(LAST, 1, [(0, T), (T, C)])
            ffn(LAST, 0, S_FFN1, 0, Y_FFN1, BOTH, [lat, context])
            norm_sums(LAST, 2, [(0, T), (T, C)])

            def rotation(r, n):
                pe.wait_ge(copied_2, n + 1)
                if r >= 2:
                    pe.wait_ge(rot_read_2, r - 1)
                nc.tensor.matmul(psum[:, 4 + r % 2, :], rotate[:, 1, :], squares[:, r % 2, 0:T], start=True, stop=True).then_inc(rotated_2, 1)

            def bank_free(n):
                before = [i for i in range(n) if OUTS_2[i][4] == OUTS_2[n][4]]
                if before:
                    pe.wait_ge(copied_2, before[-1] + 1)

            ropes = outs_done = 0
            rows_of = {False: (h_hi, h_lo), True: (h_ctx_hi, h_ctx_lo)}
            for s, (kind, j, k0, nk, cols) in enumerate(SLOTS_2):
                turn, pos = slot_of(LAST, S_MIX2 + s)
                pe.wait_ge(lo_ready, turn * SLOTS + (SLOTS + pos + 1))
                end = k0 + nk == KD
                final = next(i for i in range(s, len(SLOTS_2)) if SLOTS_2[i][2] + SLOTS_2[i][3] == KD)
                outs = [n for n, o in enumerate(OUTS_2) if o[0] == final]
                if k0 == 0:
                    for n in outs:
                        bank_free(n)
                if nk == KD:
                    last = dense(pos, 0, KD, [lat], [psum[:, OUTS_2[outs[0]][4], :]], rows_ready(LAST, 1) if s == 0 else None)
                elif kind == "gates":
                    for k in range(nk):
                        for m, (w, r) in enumerate(((w_hi, 0), (w_hi, 1), (w_lo, 0))):
                            for n, x, size in zip(outs, (lat, context), (T, C)):
                                last = nc.tensor.matmul(psum[:, OUTS_2[n][4], 0:size], w[:, pos, k * P:(k + 1) * P], x[r](k0 + k),
                                                        start=k0 + k == 0 and m == 0, stop=k0 + k == KD - 1 and m == 2)
                else:
                    for n in outs:
                        _, out_kind, _, t, b = OUTS_2[n]
                        xs = rows_of[out_kind.endswith("_ctx")]
                        for k in range(nk):
                            for m, (r, w) in enumerate(((0, w_hi), (0, w_lo), (1, w_hi))):
                                last = nc.tensor.matmul(psum[:, b, 0:cols], xs[r][:, k0 + k, t * P:(t + 1) * P], w[:, pos, k * cols:(k + 1) * cols],
                                                        start=k0 + k == 0 and m == 0, stop=k0 + k == KD - 1 and m == 2)
                        if end and n != outs[-1]:
                            last.then_inc(item_done_2, 1)
                last.then_inc(slot_used, 1)
                if outs_done and OUTS_2[outs_done - 1][1] in ROPED_2:
                    rotation(ropes, outs_done - 1)
                    ropes += 1
                outs_done = outs[-1] + 1 if end else 0

            pe.wait_ge(ctx_keys_ready, 1)
            for way in range(2):
                for h in range(RET_H):
                    cols = slice(h * P, (h + 1) * P)
                    for t in range(TCT):
                        last = nc.tensor.matmul(psum[:, way, cols], ctx_keys[:, way, t, cols], rv_ctx[:, t, cols], start=t == 0, stop=t == TCT - 1)
                last.then_inc(ret_state_done, 1)

            pe.wait_ge(gate_w_loaded, 64)
            for t in range(TT + TCT):
                tok = (t + TT) % (TT + TCT) if t < TCT else t - TCT
                if t >= 2:
                    pe.wait_ge(gate_read, t - 1)
                elif t == 0:
                    pe.wait_ge(copied_2, N_2)
                nc.tensor.matmul(psum[:, 6 + t % 2, :], gate_in[:, tok * P:(tok + 1) * P], gate_w[:], start=True, stop=True).then_inc(gate_done, 1)

            def ret_scores(h):
                for t in range(TT):
                    if h:
                        pe.wait_ge(ret_scores_ready, (h - 1) * TT + t + 1)
                    elif t < 2:
                        pe.wait_ge(ret_state_ready, t + 1)
                    nc.tensor.matmul(psum[:, t, :], rk[:, h, t * P:(t + 1) * P], rq[:, h, :], start=True, stop=True).then_inc(ret_scores_done, 1)

            pe.wait_ge(roped_2, 2 * RET_H)
            ret_scores(0)
            for h in range(RET_H):
                if h + 1 < RET_H:
                    ret_scores(h + 1)
                o = psum[:, 4 + h % 2, :]
                if h >= 2:
                    pe.wait_ge(ret_o_ready, h - 1)
                for t in range(TT):
                    pe.wait_ge(ret_scores_ready, h * TT + t + 1)
                    nc.tensor.matmul(o, rv[:, t, h * P:(h + 1) * P], scores_r[:, t, :], start=t == 0, stop=False)
                pe.wait_ge(q_dec_ready, h + 1)
                pe.wait_ge(ret_state_ready, 2)
                nc.tensor.matmul(o, ret_state[:, 0, h, :], q_dec[:, 0, :], start=False, stop=False)
                nc.tensor.matmul(o, ret_state[:, 1, h, :], q_dec[:, 1, :], start=False, stop=True).then_inc(ret_o_done, 1)

            pe.wait_ge(ret_o_ready, RET_H)
            for p in range(PAIRS):
                for t in range(TT):
                    last = nc.tensor.transpose(psum[:, p, t * P:(t + 1) * P], gk[:, p, t * P:(t + 1) * P], ident[:])
                last.then_inc(gk_turned, 1)
            for t in range(TT + TCT):
                for way in range(2):
                    for p in range(PAIRS):
                        d = (t * 2 + way) * PAIRS + p
                        last = nc.tensor.matmul(psum[:, 2, 2 * d:2 * d + 2], log_gates[:, t, (way * PAIRS + p) * P:(way * PAIRS + p + 1) * P], ones[:, 0:2],
                                                start=True, stop=True)
            last.then_inc(totals_done, 1)
            pe.wait_ge(tri_loaded, 16)

            def suffixes(t):
                if t >= 2:
                    pe.wait_ge(suffix_exp, t - 1)
                for way in range(2):
                    last = nc.tensor.matmul(psum[:, 4 + t % 2, way * 2 * P:(way + 1) * 2 * P], tri[:, way, :], log_gates[:, t, way * 2 * P:(way + 1) * 2 * P],
                                            start=True, stop=True)
                last.then_inc(suffix_done, 1)

            made = [0, 0]
            total = 0
            suffixes(0)
            for t in range(TT + TCT):
                if t + 1 < TT + TCT:
                    suffixes(t + 1)
                pe.wait_ge(gk_dec_ready, t + 1)
                for way in range(2):
                    if state_slot(t, way) is None:
                        continue
                    if made[way]:
                        pe.wait_ge(state_copied, made[way])
                    total += 1
                    made[way] = total
                    v = gv_ctx[:, t, :] if t < TCT else gv[:, t - TCT, :]
                    for p in range(PAIRS):
                        last = nc.tensor.matmul(psum[:, 6 + way, p * 2 * P:(p + 1) * 2 * P], gk_dec[:, t % 2, way, p * P:(p + 1) * P],
                                                v[:, p * 2 * P:(p + 1) * 2 * P], start=True, stop=True)
                    last.then_inc(state_done, 1)

            def gla_sums(n, c, p):
                if n:
                    pe.wait_ge(factor_exp, n)
                for b in range(4):
                    at = slice(b * 512, (b + 1) * 512)
                    if n == 0:
                        pe.wait_ge(sums_act_ready, TT + b + 1)
                        pe.wait_ge(sums_dve_ready, TT + b + 1)
                    for way, sums in enumerate((sums_f, sums_b)):
                        cols = slice((way * PAIRS + p) * P, (way * PAIRS + p + 1) * P)
                        for half, gates_half in enumerate((log_gates_hi, log_gates_lo)):
                            last = nc.tensor.matmul(psum[:, b, :], gates_half[:, c, cols], sums[:, at], start=way == half == 0, stop=way == half == 1)
                last.then_inc(sums_done, 1)

            def gla_scores(n, c, p, half):
                at = slice(c * P, (c + 1) * P)
                if half == 0:
                    pe.wait_ge(factors_ready, n + 1)
                if n or half:
                    pe.wait_ge(gla_scores_step, (2 * n + half) * 4)
                for i in range(4):
                    level = 4 * half + i
                    for r in range(2):
                        rows = slice(GLA_DK * r, GLA_DK * (r + 1))
                        k = factors[rows, n % 2, LEVELS + 1 + level, :] if level < LEVELS else gk[rows, p, at]
                        q = factors[rows, n % 2, level, :] if level < LEVELS else q_twice[rows, p, at]
                        last = nc.tensor.matmul(psum[:, 4 + r, i * P:(i + 1) * P], k, q, start=True, stop=True)
                last.then_inc(gla_scores_done, 1)

            def gla_output(n, c, p):
                pe.wait_ge(gla_scores_step, (n + 1) * (LEVELS + 1))
                if n:
                    pe.wait_ge(gla_o_ready, n)
                for r in range(2):
                    rows = slice(GLA_DK * r, GLA_DK * (r + 1))
                    o = psum[:, 6 + r, 0:P]
                    nc.tensor.matmul(o, gv[:, c, (2 * p + r) * P:(2 * p + r + 1) * P], scores_g[:, n % 2, r, :], start=True, stop=False)
                    nc.tensor.matmul(o, gla_state[rows, 0, p, TCT - 1 + c, :], factors[rows, n % 2, LEVELS, :], start=False, stop=False)
                    last = nc.tensor.matmul(o, gla_state[rows, 1, p, TCT + TT - 2 - c, :], factors[rows, n % 2, 2 * LEVELS + 1, :], start=False, stop=True)
                last.then_inc(gla_o_done, 1)

            def mean(h):
                nc.tensor.matmul(psum[:, h % 2, :], ones[:], rq[:, h, :], start=True, stop=True).then_inc(mean_done, 1)

            for ahead in range(2):
                gla_sums(*units()[ahead])
            for n, c, p in units():
                gla_scores(n, c, p, 0)
                if n == 1:
                    pe.wait_ge(state_step, STATES - 1)
                if n:
                    gla_output(*units()[n - 1])
                if n == UNITS - 1:
                    pe.wait_ge(factor_exp, UNITS)
                    mean(0)
                    mean(1)
                gla_scores(n, c, p, 1)
                if n + 2 < UNITS:
                    gla_sums(*units()[n + 2])
            gla_output(*units()[UNITS - 1])

            for h in range(2 * RET_H + 1):
                if 2 <= h < RET_H:
                    pe.wait_ge(centred, h - 1)
                    mean(h)
                g = h - 1
                if g >= 0:
                    pe.wait_ge(merge_sq, g + 1)
                    if g >= 2:
                        pe.wait_ge(merge_inv, 2 * g - 3)
                    nc.tensor.matmul(psum[:, 2 + g % 2, :], ones[:], squares[:, g % 2, 0:T], start=True, stop=True).then_inc(merge_sum, 1)
            for c in range(KD):
                turn, pos = slot_of(LAST, S_MIX2 + len(SLOTS_2) + c)
                pe.wait_ge(lo_ready, turn * SLOTS + (SLOTS + pos + 1))
                if c >= 2:
                    pe.wait_ge(*x_updated(LAST, Y_MIX2 + c - 1))
                dense(pos, 0, KD, [lat], [psum[:, 6 + c % 2, :]], (lambda k: pe.wait_ge(merge_lo, k + 1)) if c == 0 else None).then_inc(slot_used, 1)
            norm_sums(LAST, 3, [(0, T)])
            ffn(LAST, 2, S_FFN2, NF, Y_FFN2, LAT, [lat])
            norm_sums(LAST, 4, [(0, T)])
            for t in range(TT):
                if t >= 2:
                    pe.wait_ge(y_rows_ready, t - 1)
                for c in range(KD):
                    pe.wait_ge(*x_updated(LAST, Y_END + c + 1))
                    last = nc.tensor.transpose(psum[:, 2 + 2 * (t % 2) + c // 4, (c % 4) * P:(c % 4 + 1) * P],
                                               x_lat[:, c, t * P:(t + 1) * P], ident[:])
                    if c % 4 == 3:
                        last.then_inc(out_turned, 1)


def rope_table(dim):
    inv = np.float32(10000.0) ** (-np.arange(0, dim, 2, dtype=np.float32) / np.float32(dim))
    ang = (np.arange(T, dtype=np.float32)[:, None] * inv[None, :]).astype(np.float32)
    rows = np.arange(P) % (dim // 2)
    return np.cos(ang)[:, rows].T, np.sin(ang)[:, rows].T


def rotation_matrix(dim):
    r = np.zeros((P, P), np.float32)
    for i in range(P):
        if i % dim < dim // 2:
            r[i + dim // 2, i] = -1.0
        else:
            r[i - dim // 2, i] = 1.0
    return r


def constants_2():
    tok = np.arange(T)
    freqs = np.float32(10000.0) ** (-np.arange(32, dtype=np.float32) / np.float32(32))
    row, col = (tok // GRID_W).astype(np.float32), (tok % GRID_W).astype(np.float32)
    dims = np.arange(P)
    ang = np.where(dims[:, None] < P // 2, row[None, :], col[None, :]).astype(np.float32) * freqs[dims % 32][:, None]
    gap = np.arange(STRIP)[None, :] - MID - dims[:, None]
    mid = gap[:, MID:MID + P]
    ctx_tok = (np.arange(TCT)[None, :] * P + dims[:, None])
    j, i = dims[:, None], dims[None, :]
    q_f, q_b, k_f, k_b, masks = [], [], [], [], []
    for level in range(LEVELS):
        size = P >> level
        middle = i // size * size + size // 2
        second = i >= middle
        q_f.append(second & (j >= middle) & (j <= i))
        q_b.append(~second & (j >= i) & (j < middle))
        k_f.append(~second & (j > i) & (j < middle))
        k_b.append(second & (j >= middle) & (j < i))
        masks.append((j // size == i // size) & (j // (size // 2) != i // (size // 2)))
    masks.append(i == j)
    none = np.zeros((P, P), bool)
    f32 = np.float32
    return {
        "c_grid": np.stack([np.cos(ang), np.sin(ang)], 1).astype(f32),
        "c_key_pos": np.stack([C - 1 - ctx_tok, ctx_tok], 1).astype(f32),
        "c_distance": np.concatenate([np.abs(gap), mid >= 0, mid <= 0], 1).astype(f32),
        "c_row_pos": np.tile(np.stack([tok + 1, T - tok]).astype(f32), (P, 1, 1)),
        "c_masks": np.stack(masks, 1).astype(np.uint32),
        "c_tri": np.stack([j > i, j < i], 1).astype(f32),
        "c_sums_f": np.concatenate(q_f + [j <= i] + k_f + [none], 1).astype(f32),
        "c_sums_b": np.concatenate(q_b + [none] + k_b + [j >= i], 1).astype(f32),
    }


def constants():
    causal = np.where(np.arange(P)[None, :] <= np.arange(P)[:, None], 0.0, NEG).astype(np.float32)
    ends = np.arange(NC) * CMP_STRIDE + CMP_BLOCK - 1
    tokens = np.arange(T).reshape(TT, P).T
    lam0 = [0.8 - 0.6 * np.exp(-0.3 * i) for i in range(DEPTH)]
    return {
        "c_ident": np.eye(P, dtype=np.float32),
        "c_ones": np.ones((P, P), np.float32),
        "c_rope": np.stack([*rope_table(32), *rope_table(64)], 1).astype(np.float32),
        "c_rotate": np.stack([rotation_matrix(32), rotation_matrix(64)], 1),
        "c_causal": causal,
        "c_swap": np.roll(np.eye(P, dtype=np.float32), P // 2, 0),
        "c_cmp_mask": np.where(ends[None, None, :] <= tokens[:, :, None], 0.0, NEG).astype(np.float32),
        "c_cmp_any": (np.arange(P)[:, None] >= ends[0]).astype(np.float32),
        **constants_2(),
        "c_lam": np.tile(np.array([v for x in lam0 for v in (x, 1.0 - x)], np.float32), (P, 1)),
    }


INPUTS = """x ffn_norm_g ffn_w_gate ffn_w_up ffn_w_down mix_norm_g w_in mla_q_norm_g mla_w_uq mla_kv_norm_g mla_w_ukv
diff_lambda diff_norm_g nsa_cmp_pos nsa_cmp_w1 nsa_cmp_b1 nsa_cmp_w2 nsa_gate_b w_out final_norm_g c_2 ctx_2 c_ctx_2
ada_w_2 ada_b_2 norm1_w_2 ffn1_w1_2 ffn1_w3_2 ffn1_w2_2 norm2_w_2 w_in_2 ret_decay_f_2 ret_decay_b_2 ret_norm_w_2
gla_gate_w_f_2 gla_gate_b_f_2 gla_gate_w_b_2 gla_gate_b_b_2 gla_norm_w_2 w_out_2 norm3_w_2 ffn2_w1_2 ffn2_w3_2
ffn2_w2_2 final_norm_w_2""".split()


def kernel(**inputs):
    import concourse.bacc as bacc
    from concourse.bass_utils import run_bass_kernel_spmd

    nc = bacc.Bacc("TRN2", target_bir_lowering=False, num_devices=1)
    arrays = {name: np.ascontiguousarray(inputs[name]) for name in INPUTS}
    arrays.update(constants())
    aps = {name: nc.dram_tensor(name, v.shape, mybir.dt.from_np(v.dtype), kind="ExternalInput").ap()
           for name, v in arrays.items()}
    out = nc.dram_tensor("out", (1, T, D), F32, kind="ExternalOutput").ap()
    build(nc, aps, out)
    return run_bass_kernel_spmd(nc, [arrays], core_ids=[0]).results[0]["out"]
```
